# Optimizing a Trainium2 kernel written in Bass

```python
import jax
import jax.numpy as jnp
from jax import lax
import numpy as np
import math
import jax, jax.numpy as jnp

D_MODEL = 1024
BATCH = 1
SEQ = 1024
DEPTH = 1

MEM_LEN = 256
NORM_EPS = 1e-6

MLA_HEADS = 8
MLA_NOPE_DIM = 64
MLA_ROPE_DIM = 32
MLA_QK_DIM = MLA_NOPE_DIM + MLA_ROPE_DIM
MLA_V_DIM = 64
MLA_Q_RANK = 192
MLA_KV_RANK = 128
ROPE_BASE = 10000.0
Q_BLOCK = 128

HG_HEADS = 4
HG_KEY_DIM = 128
HG_VAL_DIM = 128
HG_CHUNK = 64

MLA_WIDTH = MLA_HEADS * MLA_V_DIM
HG_FWIDTH = HG_HEADS * HG_KEY_DIM
HG_WIDTH = HG_HEADS * HG_VAL_DIM
MIX_WIDTH = MLA_WIDTH + HG_WIDTH
IN_SIZES = (MLA_Q_RANK, MLA_KV_RANK, MLA_ROPE_DIM, HG_FWIDTH, HG_FWIDTH, HG_FWIDTH, HG_WIDTH, HG_WIDTH)
IN_WIDTH = sum(IN_SIZES)

X_HEADS = 4
X_HEAD_DIM = D_MODEL // X_HEADS

MOE_GROUPS = 8
MOE_PER_GROUP = 8
MOE_EXPERTS = MOE_GROUPS * MOE_PER_GROUP
MOE_TOP_K = 2
MOE_HIDDEN = 256
MOE_BLOCK = 128


def rms_norm(x, w):
    xf = x.astype(jnp.float32)
    y = xf * lax.rsqrt(jnp.mean(xf * xf, axis=-1, keepdims=True) + NORM_EPS)
    return (y * w.astype(jnp.float32)).astype(x.dtype)

def split_columns(p):
    out, start = [], 0
    for size in IN_SIZES:
        out.append(p[..., start:start + size])
        start += size
    return out

def rope_tables(positions):
    half = MLA_ROPE_DIM // 2
    inv_freq = 1.0 / (ROPE_BASE ** (jnp.arange(half, dtype=jnp.float32) / half))
    ang = positions.astype(jnp.float32)[..., None] * inv_freq
    return jnp.cos(ang)[:, :, None, :], jnp.sin(ang)[:, :, None, :]

def apply_rope(x, cos, sin):
    x1, x2 = jnp.split(x.astype(jnp.float32), 2, axis=-1)
    return jnp.concatenate([x1 * cos - x2 * sin, x2 * cos + x1 * sin], axis=-1).astype(x.dtype)

def blocked_attention(q, k, v, scale):
    B, S, H, Dq = q.shape
    nb = S // Q_BLOCK
    qb = q.reshape(B, nb, Q_BLOCK, H, Dq).transpose(1, 0, 2, 3, 4)

    def one_block(qblk):
        s = jnp.einsum('bqhd,bkhd->bhqk', qblk, k).astype(jnp.float32) * scale
        p = jax.nn.softmax(s, axis=-1).astype(v.dtype)
        return jnp.einsum('bhqk,bkhd->bqhd', p, v)

    o = lax.map(one_block, qb)
    return o.transpose(1, 0, 2, 3, 4).reshape(B, S, H, v.shape[-1])

def mla_mixer(c_q, c_kv, k_rope, cos, sin, q_a_norm, w_q_up, kv_a_norm, w_kv_up, q_norm, k_norm):
    B, S, _ = c_q.shape
    q = (rms_norm(c_q, q_a_norm) @ w_q_up).reshape(B, S, MLA_HEADS, MLA_QK_DIM)
    kv = (rms_norm(c_kv, kv_a_norm) @ w_kv_up).reshape(B, S, MLA_HEADS, MLA_NOPE_DIM + MLA_V_DIM)
    k_nope, v = kv[..., :MLA_NOPE_DIM], kv[..., MLA_NOPE_DIM:]
    k_r = jnp.broadcast_to(k_rope[:, :, None, :], (B, S, MLA_HEADS, MLA_ROPE_DIM))
    k = jnp.concatenate([k_nope, k_r], axis=-1)
    q = rms_norm(q, q_norm)
    k = rms_norm(k, k_norm)
    q = jnp.concatenate([q[..., :MLA_NOPE_DIM], apply_rope(q[..., MLA_NOPE_DIM:], cos, sin)], axis=-1)
    k = jnp.concatenate([k[..., :MLA_NOPE_DIM], apply_rope(k[..., MLA_NOPE_DIM:], cos, sin)], axis=-1)
    o = blocked_attention(q, k, v, MLA_QK_DIM ** -0.5)
    return o.reshape(B, S, MLA_WIDTH)

def gla_chunk_scan(q, k, g, v):
    B, S, H, DK = q.shape
    DV = v.shape[-1]
    n = S // HG_CHUNK

    def to_chunks(t):
        return t.astype(jnp.float32).reshape(B, n, HG_CHUNK, H, t.shape[-1]).transpose(1, 0, 3, 2, 4)

    qc, kc, gc, vc = to_chunks(q), to_chunks(k), to_chunks(g), to_chunks(v)
    mask = jnp.tril(jnp.ones((HG_CHUNK, HG_CHUNK), dtype=bool))

    def step(state, inp):
        qi, ki, gi, vi = inp
        b = jnp.cumsum(gi, axis=2)
        o_inter = jnp.einsum('bhtd,bhdv->bhtv', qi * jnp.exp(b), state)
        diff = b[:, :, :, None, :] - b[:, :, None, :, :]
        decay = jnp.exp(jnp.where(mask[:, :, None], diff, -jnp.inf))
        attn = jnp.einsum('bhtd,bhsd,bhtsd->bhts', qi, ki, decay)
        o_intra = jnp.einsum('bhts,bhsv->bhtv', attn, vi)
        b_last = b[:, :, -1:, :]
        new_state = jnp.exp(b_last[:, :, 0, :])[..., None] * state + jnp.einsum(
            'bhsd,bhsv->bhdv', ki * jnp.exp(b_last - b), vi)
        return new_state, o_inter + o_intra

    s0 = jnp.zeros((B, H, DK, DV), jnp.float32)
    _, o = lax.scan(step, s0, (qc, kc, gc, vc))
    return o.transpose(1, 0, 3, 2, 4).reshape(B, S, H, DV)

def hgrn2_mixer(hq, hf_fwd, hf_bwd, hi, hg, lb, o_norm):
    B, S, _ = hq.shape
    q = jax.nn.silu(hq).reshape(B, S, HG_HEADS, HG_KEY_DIM)
    i = hi.reshape(B, S, HG_HEADS, HG_VAL_DIM)

    def direction(f_pre, lb_dir, reverse):
        z = f_pre.astype(jnp.float32)
        log_f = jnp.logaddexp(jnp.log(lb_dir), jnp.log1p(-lb_dir) + jax.nn.log_sigmoid(z))
        log_f = log_f.reshape(B, S, HG_HEADS, HG_KEY_DIM)
        k = -jnp.expm1(log_f)
        args = (q, k, log_f, i)
        if reverse:
            args = tuple(jnp.flip(a, axis=1) for a in args)
        o = gla_chunk_scan(*args)
        return jnp.flip(o, axis=1) if reverse else o

    o = direction(hf_fwd, lb[0], False) + direction(hf_bwd, lb[1], True)
    o = rms_norm(o, o_norm).astype(hq.dtype) * jax.nn.silu(hg.reshape(B, S, HG_HEADS, HG_VAL_DIM))
    return o.reshape(B, S, HG_WIDTH)

def cross_attention(h, m, w_q, w_kv, q_norm, k_norm, w_o):
    B, S, D = h.shape
    M = m.shape[1]
    q = rms_norm((h @ w_q).reshape(B, S, X_HEADS, X_HEAD_DIM), q_norm)
    kv = (m @ w_kv).reshape(B, M, 2, X_HEADS, X_HEAD_DIM)
    k = rms_norm(kv[:, :, 0], k_norm)
    v = kv[:, :, 1]
    s = jnp.einsum('bqhd,bkhd->bhqk', q, k).astype(jnp.float32) * (X_HEAD_DIM ** -0.5)
    p = jax.nn.softmax(s, axis=-1).astype(v.dtype)
    o = jnp.einsum('bhqk,bkhd->bqhd', p, v).reshape(B, S, X_HEADS * X_HEAD_DIM)
    return o @ w_o

def dropless_experts(t, expert_id, weight, w_gate, w_up, w_down):
    T, D = t.shape
    A = T * MOE_TOP_K
    e_flat = expert_id.reshape(A)
    w_flat = weight.reshape(A)
    tok_flat = jnp.arange(A, dtype=jnp.int32) // MOE_TOP_K
    order = jnp.argsort(e_flat)
    e_sorted, tok_sorted, w_sorted = e_flat[order], tok_flat[order], w_flat[order]
    counts = jnp.bincount(e_flat, length=MOE_EXPERTS)
    padded = (counts + MOE_BLOCK - 1) // MOE_BLOCK * MOE_BLOCK
    start = jnp.cumsum(counts) - counts
    pend = jnp.cumsum(padded)
    pstart = pend - padded
    dest = pstart[e_sorted] + jnp.arange(A, dtype=jnp.int32) - start[e_sorted]
    n_blocks = -(-A // MOE_BLOCK) + MOE_EXPERTS
    rows = jnp.zeros((n_blocks * MOE_BLOCK, D), t.dtype).at[dest].set(t[tok_sorted])
    block_e = jnp.searchsorted(pend, jnp.arange(n_blocks, dtype=jnp.int32) * MOE_BLOCK, side='right')
    block_e = jnp.minimum(block_e, MOE_EXPERTS - 1)

    def expert_block(args):
        xb, e = args
        hb = jax.nn.silu(xb @ w_gate[e]) * (xb @ w_up[e])
        return hb @ w_down[e]

    out = lax.map(expert_block, (rows.reshape(n_blocks, MOE_BLOCK, D), block_e)).reshape(-1, D)
    contrib = out[dest] * w_sorted[:, None].astype(out.dtype)
    return jnp.zeros((T, D), out.dtype).at[tok_sorted].add(contrib)

def hier_moe(h, w_group, b_group, w_expert, b_expert, w_gate, w_up, w_down):
    B, S, D = h.shape
    t = h.reshape(B * S, D)
    g_logits = (t @ w_group).astype(jnp.float32) + b_group.astype(jnp.float32)
    g_prob = jax.nn.softmax(g_logits, axis=-1)
    g_sel = jnp.argmax(g_logits, axis=-1).astype(jnp.int32)
    g_weight = jnp.take_along_axis(g_prob, g_sel[:, None], axis=-1)
    e_logits = ((t @ w_expert).astype(jnp.float32) + b_expert.astype(jnp.float32)).reshape(
        -1, MOE_GROUPS, MOE_PER_GROUP)
    e_logits = jnp.take_along_axis(e_logits, g_sel[:, None, None], axis=1)[:, 0]
    top_logit, top_local = lax.top_k(e_logits, MOE_TOP_K)
    top_w = jax.nn.softmax(top_logit, axis=-1) * g_weight
    expert_id = g_sel[:, None] * MOE_PER_GROUP + top_local.astype(jnp.int32)
    y = dropless_experts(t, expert_id, top_w, w_gate, w_up, w_down)
    return y.reshape(B, S, D)

def first_inputs(seed: int = 0) -> dict:
    key = jax.random.key(seed)
    keys = jax.random.split(key, 40)
    counter = [0]

    def nk():
        k = keys[counter[0]]
        counter[0] += 1
        return k

    def nrm(shape, fan_in):
        return jax.random.normal(nk(), shape, jnp.float32) * (fan_in ** -0.5)

    def gain(shape):
        return 1.0 + 0.02 * jax.random.normal(nk(), shape, jnp.float32)

    L = DEPTH
    x = jax.random.normal(nk(), (BATCH, SEQ, D_MODEL), jnp.float32)
    mem = jax.random.normal(nk(), (BATCH, MEM_LEN, D_MODEL), jnp.float32)
    positions = jnp.arange(SEQ, dtype=jnp.int32)[None, :] + jax.random.randint(
        nk(), (BATCH, 1), 0, SEQ, dtype=jnp.int32)
    return {
        'x': x,
        'mem': mem,
        'positions': positions,
        'norm_mix': gain((L, D_MODEL)),
        'w_in': nrm((L, D_MODEL, IN_WIDTH), D_MODEL),
        'mla_q_a_norm': gain((L, MLA_Q_RANK)),
        'mla_w_q_up': nrm((L, MLA_Q_RANK, MLA_HEADS * MLA_QK_DIM), MLA_Q_RANK),
        'mla_kv_a_norm': gain((L, MLA_KV_RANK)),
        'mla_w_kv_up': nrm((L, MLA_KV_RANK, MLA_HEADS * (MLA_NOPE_DIM + MLA_V_DIM)), MLA_KV_RANK),
        'mla_q_norm': gain((L, MLA_QK_DIM)),
        'mla_k_norm': gain((L, MLA_QK_DIM)),
        'hg_lb_logits': 0.1 * jax.random.normal(nk(), (L + 1, 2, HG_FWIDTH), jnp.float32),
        'hg_o_norm': gain((L, HG_VAL_DIM)),
        'w_out': nrm((L, MIX_WIDTH, D_MODEL), MIX_WIDTH),
        'norm_cross': gain((L, D_MODEL)),
        'norm_mem': gain((L, D_MODEL)),
        'x_w_q': nrm((L, D_MODEL, X_HEADS * X_HEAD_DIM), D_MODEL),
        'x_w_kv': nrm((L, D_MODEL, 2 * X_HEADS * X_HEAD_DIM), D_MODEL),
        'x_q_norm': gain((L, X_HEAD_DIM)),
        'x_k_norm': gain((L, X_HEAD_DIM)),
        'x_w_o': nrm((L, X_HEADS * X_HEAD_DIM, D_MODEL), X_HEADS * X_HEAD_DIM),
        'norm_ffn': gain((L, D_MODEL)),
        'moe_w_group': nrm((L, D_MODEL, MOE_GROUPS), D_MODEL),
        'moe_b_group': 0.01 * jax.random.normal(nk(), (L, MOE_GROUPS), jnp.float32),
        'moe_w_expert': nrm((L, D_MODEL, MOE_EXPERTS), D_MODEL),
        'moe_b_expert': 0.01 * jax.random.normal(nk(), (L, MOE_EXPERTS), jnp.float32),
        'moe_w_gate': nrm((L, MOE_EXPERTS, D_MODEL, MOE_HIDDEN), D_MODEL),
        'moe_w_up': nrm((L, MOE_EXPERTS, D_MODEL, MOE_HIDDEN), D_MODEL),
        'moe_w_down': nrm((L, MOE_EXPERTS, MOE_HIDDEN, D_MODEL), MOE_HIDDEN),
    }

def first_block(x, mem, positions, norm_mix, w_in, mla_q_a_norm, mla_w_q_up, mla_kv_a_norm, mla_w_kv_up,
              mla_q_norm, mla_k_norm, hg_lb_logits, hg_o_norm, w_out, norm_cross, norm_mem, x_w_q, x_w_kv,
              x_q_norm, x_k_norm, x_w_o, norm_ffn, moe_w_group, moe_b_group, moe_w_expert, moe_b_expert,
              moe_w_gate, moe_w_up, moe_w_down):
    cos, sin = rope_tables(positions)
    lb_table = jnp.cumsum(jax.nn.softmax(hg_lb_logits.astype(jnp.float32), axis=0), axis=0)
    for l in range(DEPTH):
        h = rms_norm(x, norm_mix[l])
        c_q, c_kv, k_rope, hq, hf_fwd, hf_bwd, hi, hg = split_columns(h @ w_in[l])
        a = mla_mixer(c_q, c_kv, k_rope, cos, sin, mla_q_a_norm[l], mla_w_q_up[l], mla_kv_a_norm[l],
                      mla_w_kv_up[l], mla_q_norm[l], mla_k_norm[l])
        r = hgrn2_mixer(hq, hf_fwd, hf_bwd, hi, hg, lb_table[l], hg_o_norm[l])
        x = x + jnp.concatenate([a, r], axis=-1) @ w_out[l]
        x = x + cross_attention(rms_norm(x, norm_cross[l]), rms_norm(mem, norm_mem[l]), x_w_q[l], x_w_kv[l],
                                x_q_norm[l], x_k_norm[l], x_w_o[l])
        x = x + hier_moe(rms_norm(x, norm_ffn[l]), moe_w_group[l], moe_b_group[l], moe_w_expert[l],
                         moe_b_expert[l], moe_w_gate[l], moe_w_up[l], moe_w_down[l])
    return x


_first_inputs = first_inputs


def first_inputs(seed=0):
    import zlib

    import numpy as np

    out = dict(_first_inputs(seed))
    spreads = {}
    factors = {'norm_mix': 2.963,
     'mla_q_a_norm': 8.0,
     'mla_kv_a_norm': 8.0,
     'mla_q_norm': 8.0,
     'mla_k_norm': 8.0,
     'hg_lb_logits': 5.734,
     'hg_o_norm': 3.587,
     'norm_cross': 8.0,
     'norm_mem': 8.0,
     'x_q_norm': 8.0,
     'x_k_norm': 8.0,
     'moe_b_group': 5.14,
     'moe_b_expert': 5.75}
    for name, (base, spread) in spreads.items():
        noise = np.random.default_rng([zlib.crc32(name.encode()), seed]).standard_normal(out[name].shape)
        drawn = base * np.exp(spread * noise) if base else spread * noise
        out[name] = jnp.asarray(drawn.astype(out[name].dtype))
    for name, factor in factors.items():
        out[name] = (out[name] * factor).astype(out[name].dtype)
    return out


SSM_GROUP = 16
SSM_WIDTH = D_MODEL // 2
SSM_GROUPS = SSM_WIDTH // SSM_GROUP
SSM_STATE = 64
CONV_WIDTH = D_MODEL
CONV_K = 3
D_FF = 4 * D_MODEL
DT_MIN = 1e-3
DT_MAX = 1e-1
SPLIT_SIZES = (SSM_WIDTH, CONV_WIDTH, CONV_WIDTH, CONV_WIDTH, D_MODEL, D_MODEL)
IN_COLS = sum(SPLIT_SIZES)
SPLIT_POINTS = tuple(int(v) for v in np.cumsum(SPLIT_SIZES)[:-1])


def rmsnorm(x, g):
    xf = x.astype(jnp.float32)
    var = jnp.mean(xf * xf, axis=-1, keepdims=True)
    return (xf * lax.rsqrt(var + NORM_EPS) * g.astype(jnp.float32)).astype(x.dtype)

def _ssm_combine(e1, e2):
    a1r, a1i, b1r, b1i = e1
    a2r, a2i, b2r, b2i = e2
    ar = a1r * a2r - a1i * a2i
    ai = a1r * a2i + a1i * a2r
    br = a2r * b1r - a2i * b1i + b2r
    bi = a2r * b1i + a2i * b1r + b2i
    return (ar, ai, br, bi)

def s5_branch(u, lam_re, lam_im, log_dt, b_re, b_im, c_re, c_im, d_skip):
    f32 = jnp.float32
    bsz, seq, _ = u.shape
    uf = u.astype(f32).reshape(bsz, seq, SSM_GROUPS, SSM_GROUP)
    lr = lam_re.astype(f32)
    li = lam_im.astype(f32)
    dt = jnp.exp(log_dt.astype(f32))[:, None]
    mag = jnp.exp(lr * dt)
    ab_re = mag * jnp.cos(li * dt)
    ab_im = mag * jnp.sin(li * dt)
    er = ab_re - 1.0
    ei = ab_im
    den = lr * lr + li * li
    q_re = (er * lr + ei * li) / den
    q_im = (ei * lr - er * li) / den
    br = b_re.astype(f32)
    bi = b_im.astype(f32)
    bb_re = q_re[..., None] * br - q_im[..., None] * bi
    bb_im = q_re[..., None] * bi + q_im[..., None] * br
    bu_re = jnp.einsum('gnc,bsgc->bsgn', bb_re, uf)
    bu_im = jnp.einsum('gnc,bsgc->bsgn', bb_im, uf)
    a_re = jnp.broadcast_to(ab_re[None, None], (1, seq, SSM_GROUPS, SSM_STATE))
    a_im = jnp.broadcast_to(ab_im[None, None], (1, seq, SSM_GROUPS, SSM_STATE))
    _, _, s_re, s_im = lax.associative_scan(_ssm_combine, (a_re, a_im, bu_re, bu_im), axis=1)
    y = (jnp.einsum('gcn,bsgn->bsgc', c_re.astype(f32), s_re)
         - jnp.einsum('gcn,bsgn->bsgc', c_im.astype(f32), s_im))
    y = y + d_skip.astype(f32).reshape(SSM_GROUPS, SSM_GROUP) * uf
    return y.reshape(bsz, seq, SSM_WIDTH)

def causal_short_conv(v, w, b):
    seq = v.shape[1]
    vp = jnp.pad(v, ((0, 0), (CONV_K - 1, 0), (0, 0)))
    out = b
    for k in range(CONV_K):
        out = out + w[k] * vp[:, k:k + seq]
    return out

def mixer_block(xn, w_in, b_in, lam_re, lam_im, log_dt, b_re, b_im, c_re, c_im, d_skip,
                w_glu_a, w_glu_b, conv_w, conv_b, w_conv_out, w_out):
    proj = jnp.einsum('bsd,de->bse', xn, w_in) + b_in
    u_ssm, c_bgate, c_cgate, c_val, g_ssm, g_conv = jnp.split(proj, SPLIT_POINTS, axis=-1)
    y_ssm = s5_branch(u_ssm, lam_re, lam_im, log_dt, b_re, b_im, c_re, c_im, d_skip).astype(xn.dtype)
    z = jax.nn.gelu(y_ssm)
    y_a = jnp.einsum('bse,ed->bsd', z, w_glu_a) * jax.nn.sigmoid(jnp.einsum('bse,ed->bsd', z, w_glu_b))
    y_b = jnp.einsum('bse,ed->bsd', c_bgate * causal_short_conv(c_cgate * c_val, conv_w, conv_b), w_conv_out)
    merged = jax.nn.sigmoid(g_ssm) * y_a + jax.nn.sigmoid(g_conv) * y_b
    return jnp.einsum('bsd,de->bse', merged, w_out)

def squared_relu_mlp(xn, w_ff1, w_ff2):
    h = jax.nn.relu(jnp.einsum('bsd,df->bsf', xn, w_ff1))
    return jnp.einsum('bsf,fd->bsd', h * h, w_ff2)

def second_inputs(seed: int = 0) -> dict:
    key = jax.random.key(seed)
    ks = jax.random.split(key, 24)
    L, D, G, N, C = DEPTH, D_MODEL, SSM_GROUPS, SSM_STATE, SSM_GROUP
    nrm = jax.random.normal
    x = nrm(ks[0], (BATCH, SEQ, D), jnp.float32)
    norm_mix_g = 1.0 + 0.02 * nrm(ks[1], (L, D), jnp.float32)
    w_in = nrm(ks[2], (L, D, IN_COLS), jnp.float32) * D ** -0.5
    b_in = 0.02 * nrm(ks[3], (L, IN_COLS), jnp.float32)
    n_idx = jnp.arange(N, dtype=jnp.float32)
    lam_re = -0.5 + 0.01 * nrm(ks[4], (L, G, N), jnp.float32)
    lam_im = math.pi * n_idx[None, None, :] + 0.01 * nrm(ks[5], (L, G, N), jnp.float32)
    log_dt = jax.random.uniform(ks[6], (L, G), jnp.float32, math.log(DT_MIN), math.log(DT_MAX))
    ssm_b_re = nrm(ks[7], (L, G, N, C), jnp.float32) * (2.0 * C) ** -0.5
    ssm_b_im = nrm(ks[8], (L, G, N, C), jnp.float32) * (2.0 * C) ** -0.5
    ssm_c_re = nrm(ks[9], (L, G, C, N), jnp.float32) * (2.0 * N) ** -0.5
    ssm_c_im = nrm(ks[10], (L, G, C, N), jnp.float32) * (2.0 * N) ** -0.5
    ssm_d = 1.0 + 0.1 * nrm(ks[11], (L, SSM_WIDTH), jnp.float32)
    w_glu_a = nrm(ks[12], (L, SSM_WIDTH, D), jnp.float32) * SSM_WIDTH ** -0.5
    w_glu_b = nrm(ks[13], (L, SSM_WIDTH, D), jnp.float32) * SSM_WIDTH ** -0.5
    conv_w = nrm(ks[14], (L, CONV_K, CONV_WIDTH), jnp.float32) * CONV_K ** -0.5
    conv_b = 0.02 * nrm(ks[15], (L, CONV_WIDTH), jnp.float32)
    w_conv_out = nrm(ks[16], (L, CONV_WIDTH, D), jnp.float32) * CONV_WIDTH ** -0.5
    w_out = nrm(ks[17], (L, D, D), jnp.float32) * D ** -0.5
    norm_mlp_g = 1.0 + 0.02 * nrm(ks[18], (L, D), jnp.float32)
    w_ff1 = nrm(ks[19], (L, D, D_FF), jnp.float32) * D ** -0.5
    w_ff2 = nrm(ks[20], (L, D_FF, D), jnp.float32) * D_FF ** -0.5
    norm_final_g = 1.0 + 0.02 * nrm(ks[21], (D,), jnp.float32)
    return {"x": x, "norm_mix_g": norm_mix_g, "w_in": w_in, "b_in": b_in,
            "lam_re": lam_re, "lam_im": lam_im, "log_dt": log_dt,
            "ssm_b_re": ssm_b_re, "ssm_b_im": ssm_b_im, "ssm_c_re": ssm_c_re, "ssm_c_im": ssm_c_im,
            "ssm_d": ssm_d, "w_glu_a": w_glu_a, "w_glu_b": w_glu_b,
            "conv_w": conv_w, "conv_b": conv_b, "w_conv_out": w_conv_out, "w_out": w_out,
            "norm_mlp_g": norm_mlp_g, "w_ff1": w_ff1, "w_ff2": w_ff2, "norm_final_g": norm_final_g}

def second_block(x, norm_mix_g, w_in, b_in, lam_re, lam_im, log_dt, ssm_b_re, ssm_b_im, ssm_c_re, ssm_c_im,
              ssm_d, w_glu_a, w_glu_b, conv_w, conv_b, w_conv_out, w_out, norm_mlp_g, w_ff1, w_ff2,
              norm_final_g):
    h = x
    for l in range(DEPTH):
        xn = rmsnorm(h, norm_mix_g[l])
        h = h + mixer_block(xn, w_in[l], b_in[l], lam_re[l], lam_im[l], log_dt[l],
                            ssm_b_re[l], ssm_b_im[l], ssm_c_re[l], ssm_c_im[l], ssm_d[l],
                            w_glu_a[l], w_glu_b[l], conv_w[l], conv_b[l], w_conv_out[l], w_out[l])
        xn = rmsnorm(h, norm_mlp_g[l])
        h = h + squared_relu_mlp(xn, w_ff1[l], w_ff2[l])
    return rmsnorm(h, norm_final_g)


def setup_inputs(seed=0):
    out = dict(first_inputs(seed))
    for name, value in second_inputs(seed + 1).items():
        if name != "x":
            out[name + "_2"] = value
    return out


def reference(
    x, mem, positions, norm_mix, w_in, mla_q_a_norm, mla_w_q_up, mla_kv_a_norm, mla_w_kv_up,
    mla_q_norm, mla_k_norm, hg_lb_logits, hg_o_norm, w_out, norm_cross, norm_mem, x_w_q, x_w_kv,
    x_q_norm, x_k_norm, x_w_o, norm_ffn, moe_w_group, moe_b_group, moe_w_expert, moe_b_expert,
    moe_w_gate, moe_w_up, moe_w_down, norm_mix_g_2, w_in_2, b_in_2, lam_re_2, lam_im_2,
    log_dt_2, ssm_b_re_2, ssm_b_im_2, ssm_c_re_2, ssm_c_im_2, ssm_d_2, w_glu_a_2, w_glu_b_2,
    conv_w_2, conv_b_2, w_conv_out_2, w_out_2, norm_mlp_g_2, w_ff1_2, w_ff2_2, norm_final_g_2,
):
    x = first_block(
        x, mem, positions, norm_mix, w_in, mla_q_a_norm, mla_w_q_up, mla_kv_a_norm, mla_w_kv_up,
        mla_q_norm, mla_k_norm, hg_lb_logits, hg_o_norm, w_out, norm_cross, norm_mem, x_w_q,
        x_w_kv, x_q_norm, x_k_norm, x_w_o, norm_ffn, moe_w_group, moe_b_group, moe_w_expert,
        moe_b_expert, moe_w_gate, moe_w_up, moe_w_down,
    )
    return second_block(
        x, norm_mix_g_2, w_in_2, b_in_2, lam_re_2, lam_im_2, log_dt_2, ssm_b_re_2, ssm_b_im_2,
        ssm_c_re_2, ssm_c_im_2, ssm_d_2, w_glu_a_2, w_glu_b_2, conv_w_2, conv_b_2, w_conv_out_2,
        w_out_2, norm_mlp_g_2, w_ff1_2, w_ff2_2, norm_final_g_2,
    )


_drawn_inputs = setup_inputs


def setup_inputs(seed=0):
    import zlib

    import numpy as np

    out = dict(_drawn_inputs(seed))
    spreads = {}
    factors = {'norm_ffn': 8.0,
     'moe_w_group': 3.831,
     'moe_b_group': 8.0,
     'moe_w_expert': 4.103,
     'moe_b_expert': 8.0,
     'moe_w_gate': 3.809,
     'moe_w_up': 3.583,
     'moe_w_down': 3.585,
     'norm_mix_g_2': 59.373,
     'b_in_2': 59.419,
     'lam_re_2': 64.0,
     'lam_im_2': 64.0,
     'log_dt_2': 64.0,
     'ssm_b_re_2': 64.0,
     'ssm_b_im_2': 64.0,
     'ssm_c_re_2': 64.0,
     'ssm_c_im_2': 64.0,
     'ssm_d_2': 200.0,
     'w_glu_a_2': 3.276,
     'w_glu_b_2': 23.905,
     'conv_b_2': 200.0,
     'norm_mlp_g_2': 200.0,
     'norm_final_g_2': 22.885}
    for name, (base, spread) in spreads.items():
        noise = np.random.default_rng([zlib.crc32(name.encode()), seed]).standard_normal(out[name].shape)
        drawn = base * np.exp(spread * noise) if base else spread * noise
        out[name] = jnp.asarray(drawn.astype(out[name].dtype))
    for name, factor in factors.items():
        out[name] = (out[name] * factor).astype(out[name].dtype)
    return out
```

```python
import math
from contextlib import ExitStack

import numpy as np

import concourse.bass as bass
from concourse import mybir

P = 128
F32 = mybir.dt.float32
I32 = mybir.dt.int32
ALU = mybir.AluOpType
ACT = mybir.ActivationFunctionType
AX = mybir.AxisListType.X

T = 1024
NT = T // P
D = 1024
KD = D // P
EPS = 1e-6
CH = 512

MH, NOPE, ROPE, VD = 8, 64, 32, 64
QK = NOPE + ROPE
QR, KVR = 192, 128
HALF = ROPE // 2
ROPE_BASE = 10000.0
HH, HK = 4, 128
LEVELS = 7
MEM = 256
XH, XD = 4, 256
G, PG, E, EH = 8, 8, 64, 256
OVB = 15
NBLK = E + OVB
SG, SC, SN = 32, 16, 64
SJ = 8
SM = T // SJ
PAIRS = SG // 2
DFF = 4096
TWO_PI = 2 * math.pi
PI_A = 6.28125
PI_B = math.floor((TWO_PI - PI_A) * 2 ** 20) / 2 ** 20
PI_C = TWO_PI - PI_A - PI_B
ROUND = 1.5 * 2 ** 23


class Chain:

    def __init__(self, eng, sem, tally):
        self.eng, self.sem, self.tally = eng, sem, tally

    def __call__(self, ins):
        self.tally[0] += 1
        ins.then_inc(self.sem, 1)
        self.eng.wait_ge(self.sem, self.tally[0])


class Core:

    def __init__(self, nc, ctx):
        self.nc, self.ctx, self.n, self.live = nc, ctx, 0, []
        self.own = {}
        for e in ("vector", "scalar", "gpsimd", "tensor"):
            self.own[e] = (ctx.enter_context(nc.semaphore(f"{e}_step")), [0])

    def chain(self, name, eng):
        sem, tally = self.own[name]
        return Chain(eng, sem, tally)

    def sem(self, name):
        self.n += 1
        self.live.append(self.nc.alloc_semaphore(f"{name}_{self.n}"))
        return self.live[-1]

    def recycle(self, most=60):
        if len(self.live) > most:
            with self.nc.Block() as block:
                @block.gpsimd
                def _(pool):
                    self.nc.clear_and_free_semaphores(self.live)
            self.live = []


def sbuf(ctx, nc, name, shape, dt=F32):
    return ctx.enter_context(nc.sbuf_tensor(name, shape, dt))


def psum(ctx, nc, name, banks):
    return ctx.enter_context(nc.psum_tensor(name, [P, banks, CH], F32))



def make_constants(c):
    nc = c.nc
    s = lambda n, shape, dt=F32: sbuf(c.ctx, nc, n, shape, dt)
    c.ident = s("ident", [P, P])
    c.ones = s("ones", [P, P])
    c.before = s("before", [P, P])
    c.row = s("row", [P, P])
    c.col = s("col", [P, 1])
    c.eps = s("eps", [P, 1])
    with nc.Block() as block:
        @block.gpsimd
        def _(pool):
            do = c.chain("gpsimd", pool)
            do(nc.gpsimd.memset(c.ident[:], 0.0))
            do(nc.gpsimd.memset(c.ones[:], 1.0))
            do(nc.gpsimd.memset(c.eps[:], EPS))
            do(nc.gpsimd.affine_select(out=c.ident[:], in_=c.ident[:], compare_op=ALU.not_equal, fill=1.0,
                                       base=0, pattern=[[-1, P]], channel_multiplier=1))
            do(nc.gpsimd.affine_select(out=c.before[:], in_=c.ones[:], compare_op=ALU.is_gt, fill=0.0,
                                       base=0, pattern=[[1, P]], channel_multiplier=-1))
            do(nc.gpsimd.iota(c.row[:], [[1, P]], base=0, channel_multiplier=0,
                              allow_small_or_imprecise_dtypes=True))
            do(nc.gpsimd.iota(c.col[:], [[0, 1]], base=0, channel_multiplier=1,
                              allow_small_or_imprecise_dtypes=True))


def load(c, pairs):
    nc = c.nc
    c.recycle()
    done = c.sem("loaded")
    with nc.Block() as block:
        @block.sync
        def _(sp):
            for dst, src in pairs:
                with nc.allow_non_contiguous_dma("small parameters"):
                    sp.dma_start(dst, src).then_inc(done, 16)
            sp.wait_ge(done, 16 * len(pairs))



def norm_transpose(c, name, src, dst, gain, tiles, keep=None):
    nc = c.nc
    c.recycle()
    with ExitStack() as ctx:
        junk = sbuf(ctx, nc, f"{name}_junk", [P, D])
        ssq = sbuf(ctx, nc, f"{name}_ssq", [P, tiles])
        rstd = sbuf(ctx, nc, f"{name}_rstd", [P, tiles])
        normed = sbuf(ctx, nc, f"{name}_normed", [P, 2, D])
        ps = psum(ctx, nc, f"{name}_ps", 4)
        squared, scale_ready, row_ready, turned, evacuated = [
            c.sem(f"{name}_{x}") for x in ("squared", "scale_ready", "row_ready", "turned", "evacuated")]
        kept = [c.sem(f"{name}_kept{b}") for b in range(2)]
        with nc.Block() as block:
            @block.scalar
            def _(act):
                do = c.chain("scalar", act)
                for m in range(tiles):
                    do(nc.scalar.activation(junk[:], src[:, m], ACT.Square, accum_out=ssq[:, m:m + 1]))
                do(nc.scalar.activation(rstd[:], ssq[:], ACT.Sqrt, bias=c.eps[:, 0:1], scale=1.0 / D))
                nc.scalar.activation(junk[:, 0:1], ssq[:, 0:1], ACT.Copy).then_inc(squared, 1)
                act.wait_ge(scale_ready, 1)
                for m in range(tiles):
                    if m >= 2:
                        act.wait_ge(turned, m - 1)
                        if keep is not None:
                            act.wait_ge(kept[m % 2], 16 * (m // 2))
                    nc.scalar.activation(normed[:, m % 2], src[:, m], ACT.Copy,
                                         scale=rstd[:, m:m + 1]).then_inc(row_ready, 1)

            @block.vector
            def _(dve):
                dve.wait_ge(squared, 1)
                nc.vector.reciprocal(rstd[:], rstd[:]).then_inc(scale_ready, 1)
                for m in range(tiles):
                    dve.wait_ge(turned, m + 1)
                    b = 2 * (m % 2)
                    nc.vector.tensor_tensor(
                        dst[:, :, m * P:(m + 1) * P],
                        ps[:, b:b + 2, :].rearrange("p b (k t) -> p (b k) t", t=P),
                        gain[:].unsqueeze(2).to_broadcast([P, KD, P]), ALU.mult).then_inc(evacuated, 1)

            @block.tensor
            def _(pe):
                for m in range(tiles):
                    pe.wait_ge(row_ready, m + 1)
                    if m >= 2:
                        pe.wait_ge(evacuated, m - 1)
                    for k in range(KD):
                        ins = nc.tensor.transpose(ps[:, 2 * (m % 2) + k // 4, (k % 4) * P:(k % 4 + 1) * P],
                                                  normed[:, m % 2, k * P:(k + 1) * P], c.ident[:])
                    ins.then_inc(turned, 1)

            if keep is not None:
                @block.sync
                def _(sp):
                    for m in range(tiles):
                        sp.wait_ge(row_ready, m + 1)
                        sp.dma_start(keep[m * P:(m + 1) * P, :], normed[:, m % 2]).then_inc(kept[m % 2], 16)
                    for b in range(2):
                        sp.wait_ge(kept[b], 16 * tiles // 2)


def project(c, name, wbuf, weights, stationary, moving, evacuate, engine, banks=8, nk=KD):
    nc = c.nc
    c.recycle()
    n = len(weights)
    with ExitStack() as ctx:
        ps = psum(ctx, nc, f"{name}_ps", 8)
        arrived = [c.sem(f"{name}_w{b}_arrived") for b in range(2)]
        products, emptied = c.sem(f"{name}_products"), c.sem(f"{name}_emptied")
        with nc.Block() as block:
            @block.sync
            def _(sp):
                for i, w in enumerate(weights):
                    if i >= 2:
                        sp.wait_ge(products, banks * (i - 1))
                    sp.dma_start(wbuf[:w.shape[0], i % 2, :w.shape[1], :w.shape[2]], w).then_inc(arrived[i % 2], 16)

            @block.tensor
            def _(pe):
                for i in range(n):
                    pe.wait_ge(arrived[i % 2], 16 * (i // 2 + 1))
                    w = wbuf[:, i % 2]
                    for b in range(banks):
                        if i:
                            pe.wait_ge(emptied, banks * (i - 1) + b + 1)
                        for k in range(nk):
                            mv = moving(i, b, k, w)
                            ins = nc.tensor.matmul(ps[:, b, :mv.shape[-1]], stationary(i, b, k, w), mv,
                                                   start=(k == 0), stop=(k == nk - 1))
                        ins.then_inc(products, 1)

            def empty(eng):
                for i in range(n):
                    for b in range(banks):
                        eng.wait_ge(products, banks * i + b + 1)
                        evacuate(i, b, ps[:, b]).then_inc(emptied, 1)

            if engine == "scalar":
                @block.scalar
                def _(act):
                    empty(act)
            else:
                @block.vector
                def _(dve):
                    empty(dve)


def turn(c, name, items, evacuate):
    nc = c.nc
    c.recycle()
    with ExitStack() as ctx:
        ps = psum(ctx, nc, f"{name}_ps", 8)
        turned = c.sem(f"{name}_turned")
        out = [c.sem(f"{name}_out{e}") for e in range(2)]

        def run(eng, copy, parity):
            for n in range(parity, len(items), 2):
                eng.wait_ge(turned, n + 1)
                evacuate(n, ps[:, n % 8], copy).then_inc(out[parity], 1)

        with nc.Block() as block:
            @block.tensor
            def _(pe):
                for n, parts in enumerate(items):
                    if n >= 8:
                        pe.wait_ge(out[n % 2], n // 2 - 3)
                    for q, a in enumerate(parts):
                        rows, cols = a.shape[0], a.shape[-1]
                        ins = nc.tensor.transpose(ps[:cols, n % 8, q * P:q * P + rows], a, c.ident[:rows, :rows])
                    ins.then_inc(turned, 1)

            @block.scalar
            def _(act):
                run(act, lambda o, i: nc.scalar.activation(o, i, ACT.Copy), 0)

            @block.vector
            def _(dve):
                run(dve, lambda o, i: nc.vector.tensor_copy(o, i), 1)


def attention(c, name, heads, keys, qT, kT, v, out, scale, width):
    nc = c.nc
    c.recycle()
    nk = keys // P
    n = heads * NT
    sb_ = min(keys, CH)
    nsb = keys // sb_
    with ExitStack() as ctx:
        ps_s = [psum(ctx, nc, f"{name}_scores{b}", nsb) for b in range(2)]
        ps_t = psum(ctx, nc, f"{name}_probsT", nsb)
        ps_o = psum(ctx, nc, f"{name}_out", 2)
        probs = sbuf(ctx, nc, f"{name}_probs", [P, 2, keys])
        probsT = sbuf(ctx, nc, f"{name}_probsT_sb", [P, 2, nk, P])
        top = sbuf(ctx, nc, f"{name}_top", [P, n])
        bias = sbuf(ctx, nc, f"{name}_bias", [P, n])
        total = sbuf(ctx, nc, f"{name}_total", [P, n])
        inv = sbuf(ctx, nc, f"{name}_inv", [P, n])
        scored, bias_ready, probs_ready, turned, copied, mixed, stored = [
            c.sem(f"{name}_{x}") for x in
            ("scored", "bias_ready", "probs_ready", "turned", "copied", "mixed", "stored")]
        with nc.Block() as block:
            @block.tensor
            def _(pe):
                def scores(i):
                    h, m = divmod(i, NT)
                    if i >= 2:
                        pe.wait_ge(probs_ready, i - 1)
                    pieces = list(zip(qT(h, m), kT(h)))
                    for s in range(nsb):
                        for k, (q, kk) in enumerate(pieces):
                            ins = nc.tensor.matmul(ps_s[i % 2][:, s, :sb_], q, kk[:, s * sb_:(s + 1) * sb_],
                                                   start=(k == 0), stop=(k == len(pieces) - 1))
                    ins.then_inc(scored, 1)

                def turn_probs(i):
                    pe.wait_ge(probs_ready, i + 1)
                    if i >= 1:
                        pe.wait_ge(copied, i)
                    for j in range(nk):
                        ins = nc.tensor.transpose(ps_t[:, j // 4, (j % 4) * P:(j % 4 + 1) * P],
                                                  probs[:, i % 2, j * P:(j + 1) * P], c.ident[:])
                    ins.then_inc(turned, 1)

                def mix(i):
                    h, m = divmod(i, NT)
                    pe.wait_ge(copied, i + 1)
                    if i >= 2:
                        pe.wait_ge(stored, i - 1)
                    for j in range(nk):
                        ins = nc.tensor.matmul(ps_o[:, i % 2, :width], probsT[:, i % 2, j, :], v(h, j),
                                               start=(j == 0), stop=(j == nk - 1))
                    ins.then_inc(mixed, 1)

                for i in range(n + 2):
                    if i < n:
                        scores(i)
                    if 1 <= i <= n:
                        turn_probs(i - 1)
                    if i >= 2:
                        mix(i - 2)

            @block.vector
            def _(dve):
                do = c.chain("vector", dve)

                def row_max(i):
                    dve.wait_ge(scored, i + 1)
                    do(nc.vector.tensor_reduce(top[:, i:i + 1], ps_s[i % 2][:, :, :sb_], mybir.AxisListType.XY, ALU.max))
                    nc.vector.tensor_scalar(bias[:, i:i + 1], top[:, i:i + 1], -scale, None,
                                            ALU.mult).then_inc(bias_ready, 1)

                def finish(i):
                    dve.wait_ge(probs_ready, i + 1)
                    do(nc.vector.reciprocal(inv[:, i:i + 1], total[:, i:i + 1]))
                    dve.wait_ge(mixed, i + 1)
                    h, m = divmod(i, NT)
                    nc.vector.tensor_scalar(out(h, m), ps_o[:, i % 2, :width], inv[:, i:i + 1], None,
                                            ALU.mult).then_inc(stored, 1)

                for i in range(n + 2):
                    if i < n:
                        row_max(i)
                    if i >= 2:
                        finish(i - 2)

            @block.scalar
            def _(act):
                def exps(i):
                    act.wait_ge(bias_ready, i + 1)
                    if i >= 2:
                        act.wait_ge(turned, i - 1)
                    nc.scalar.activation(probs[:, i % 2].rearrange("p (s k) -> p s k", k=sb_),
                                         ps_s[i % 2][:, :, :sb_], ACT.Exp, bias=bias[:, i:i + 1],
                                         scale=scale, accum_out=total[:, i:i + 1]).then_inc(probs_ready, 1)

                def copy_out(i):
                    act.wait_ge(turned, i + 1)
                    if i >= 2:
                        act.wait_ge(mixed, i - 1)
                    nc.scalar.activation(probsT[:, i % 2].rearrange("p j q -> p (j q)"),
                                         ps_t[:].rearrange("p s k -> p (s k)")[:, :nk * P],
                                         ACT.Copy).then_inc(copied, 1)

                for i in range(n + 1):
                    if i < n:
                        exps(i)
                    if i >= 1:
                        copy_out(i - 1)


def group_norm(c, name, x, sq, ssq, width, gain):
    nc = c.nc
    c.recycle()
    g = x.shape[1]
    meaned, rooted = c.sem(f"{name}_meaned"), c.sem(f"{name}_rooted")
    with nc.Block() as block:
        @block.vector
        def _(dve):
            do = c.chain("vector", dve)
            do(nc.vector.tensor_tensor(sq, x, x, ALU.mult))
            nc.vector.tensor_reduce(ssq, sq, AX, ALU.add).then_inc(meaned, 1)
            dve.wait_ge(rooted, 1)
            do(nc.vector.reciprocal(ssq, ssq))
            do(nc.vector.tensor_tensor(x, x, ssq.unsqueeze(2).to_broadcast([P, g, width]), ALU.mult))
            if gain is not None:
                do(nc.vector.tensor_tensor(x, x, gain.to_broadcast([P, g, width]), ALU.mult))

        @block.scalar
        def _(act):
            act.wait_ge(meaned, 1)
            nc.scalar.activation(ssq, ssq, ACT.Sqrt, bias=c.eps[:, 0:1], scale=1.0 / width).then_inc(rooted, 1)


def reduce_angle(nc, do, ang, tmp):
    do(nc.vector.tensor_scalar(tmp, ang, 1.0 / TWO_PI, ROUND, ALU.mult, ALU.add))
    do(nc.vector.tensor_scalar(tmp, tmp, -ROUND, None, ALU.add))
    for part in (PI_A, PI_B, PI_C):
        do(nc.vector.scalar_tensor_tensor(ang, tmp, -part, ang, ALU.mult, ALU.add))
    do(nc.vector.tensor_scalar(ang, ang, math.pi, -math.pi, ALU.min, ALU.max))



def level_masks(c, ctx):
    nc = c.nc
    fwd = sbuf(ctx, nc, "mask_fwd", [P, LEVELS, P])
    bwd = sbuf(ctx, nc, "mask_bwd", [P, LEVELS, P])
    with ExitStack() as tmp:
        base = sbuf(tmp, nc, "mask_base", [P, LEVELS, P])
        half = sbuf(tmp, nc, "mask_half", [P, LEVELS, P])
        baseT = sbuf(tmp, nc, "mask_baseT", [P, LEVELS, P])
        halfT = sbuf(tmp, nc, "mask_halfT", [P, LEVELS, P])
        same = sbuf(tmp, nc, "mask_same", [P, LEVELS, P])
        with nc.Block() as block:
            @block.gpsimd
            def _(pool):
                do = c.chain("gpsimd", pool)
                for l in range(LEVELS):
                    w = 2 << l
                    do(nc.gpsimd.iota(base[:, l], [[w, P // w], [0, w]], base=0, channel_multiplier=0,
                                      allow_small_or_imprecise_dtypes=True))
                    do(nc.gpsimd.iota(half[:, l], [[0, P // w], [1, 2], [0, w // 2]], base=0,
                                      channel_multiplier=0, allow_small_or_imprecise_dtypes=True))
        items = [[src[:, l]] for src in (base, half) for l in range(LEVELS)]

        def out(n, bank, copy):
            return copy((baseT if n < LEVELS else halfT)[:, n % LEVELS], bank[:, :P])

        turn(c, "masks", items, out)
        with nc.Block() as block:
            @block.vector
            def _(dve):
                do = c.chain("vector", dve)
                do(nc.vector.tensor_tensor(same[:], base[:], baseT[:], ALU.is_equal))
                do(nc.vector.tensor_tensor(fwd[:], half[:], halfT[:], ALU.is_gt))
                do(nc.vector.tensor_tensor(bwd[:], half[:], halfT[:], ALU.is_lt))
                do(nc.vector.tensor_tensor(fwd[:], fwd[:], same[:], ALU.mult))
                do(nc.vector.tensor_tensor(bwd[:], bwd[:], same[:], ALU.mult))
    return fwd, bwd


def hgrn_gates(c, logf, key, lb, lb1, reset, bcum):
    nc = c.nc
    c.recycle()
    decays = c.sem("hgrn_decays")
    logs = c.sem("hgrn_logs")
    with nc.Block() as block:
        @block.vector
        def _(dve):
            do = c.chain("vector", dve)
            for d in range(2):
                for h in range(HH):
                    do(nc.vector.tensor_scalar(logf[:, d, h], logf[:, d, h], lb1[:, d, h:h + 1], lb[:, d, h:h + 1],
                                               ALU.mult, ALU.add))
                    nc.vector.tensor_scalar(logf[:, d, h], logf[:, d, h], 2.0 ** -64, None,
                                            ALU.max).then_inc(decays, 1)
                    do(nc.vector.tensor_scalar(key[:, d, h], key[:, d, h], lb1[:, d, h:h + 1], None, ALU.mult))
            for d in range(2):
                dve.wait_ge(logs, HH * (d + 1))
                src = logf[:, d].rearrange("p h t -> p (h t)")
                dst = bcum[:, d].rearrange("p h t -> p (h t)")
                if d:
                    src, dst = src[:, ::-1], dst[:, ::-1]
                do(nc.vector.tensor_tensor_scan(dst, reset[:].rearrange("p h t -> p (h t)"), src, 0.0,
                                                ALU.mult, ALU.add))

        @block.scalar
        def _(act):
            for d in range(2):
                for h in range(HH):
                    act.wait_ge(decays, HH * d + h + 1)
                    nc.scalar.activation(logf[:, d, h], logf[:, d, h], ACT.Ln).then_inc(logs, 1)


def hgrn_pairs(c, h, q, key, bcum, masks, pairT):
    nc = c.nc
    c.recycle()
    items = [(d, l) for l in range(LEVELS) for d in range(2)]
    with ExitStack() as ctx:
        gap = sbuf(ctx, nc, f"hgrn{h}_gap", [P, 2, T])
        side = sbuf(ctx, nc, f"hgrn{h}_side", [P, 2, T])
        both = sbuf(ctx, nc, f"hgrn{h}_both", [P, T])
        ps = psum(ctx, nc, f"hgrn{h}_ps", 6)
        both_ready, gap_ready, grown, side_ready, product, placed = [
            c.sem(f"hgrn{h}_{x}") for x in ("both_ready", "gap_ready", "grown", "side_ready", "product", "placed")]

        def halves(ap, l):
            w = 2 << l
            v = ap.rearrange("p (n w) -> p n w", w=w)
            return v[:, :, 0:w // 2], v[:, :, w // 2:w]

        with nc.Block() as block:
            @block.vector
            def _(dve):
                do = c.chain("vector", dve)
                nc.vector.tensor_tensor(both[:], key[:, 0, h], key[:, 1, h], ALU.add).then_inc(both_ready, 1)

                def gaps(n):
                    d, l = items[n]
                    left, right = halves(bcum[:, d, h], l)
                    gl, gr = halves(gap[:, n % 2], l)
                    mid = (right[:, :, 0:1] if d else left[:, :, (1 << l) - 1:1 << l]).to_broadcast(
                        [P, T // (2 << l), 1 << l])
                    if n >= 2:
                        dve.wait_ge(side_ready, 2 * (n - 1))
                    for qs, o, b in ((not d, gr, right), (d, gl, left)):
                        first, second = (b, mid) if qs else (mid, b)
                        nc.vector.tensor_tensor(o, first, second, ALU.subtract).then_inc(gap_ready, 1)

                def sides(n):
                    d, l = items[n]
                    dve.wait_ge(grown, n + 1)
                    if n >= 2:
                        dve.wait_ge(product, n)
                    ql, qr = halves(q[:, h], l)
                    kl, kr = halves(key[:, d, h], l)
                    gl, gr = halves(gap[:, n % 2], l)
                    sl, sr = halves(side[:, n % 2], l)
                    nc.vector.tensor_tensor(sl, gl, ql if d else kl, ALU.mult).then_inc(side_ready, 1)
                    nc.vector.tensor_tensor(sr, gr, kr if d else qr, ALU.mult).then_inc(side_ready, 1)

                def place(n):
                    d, l = items[n]
                    dve.wait_ge(product, n + 2)
                    dve.wait_ge(placed, n + 1)
                    b = 2 * (n % 2)
                    nc.vector.copy_predicated(
                        pairT[:], masks[d][:, l].bitcast(I32).unsqueeze(1).to_broadcast([P, NT, P]),
                        ps[:, b:b + 2, :].rearrange("p b (c t) -> p (b c) t", t=P)).then_inc(placed, 1)

                dve.wait_ge(product, 1)
                nc.vector.tensor_tensor(pairT[:], ps[:, 4:6, :].rearrange("p b (c t) -> p (b c) t", t=P),
                                        c.ident[:].unsqueeze(1).to_broadcast([P, NT, P]),
                                        ALU.mult).then_inc(placed, 1)
                for n in range(len(items) + 2):
                    if n < len(items):
                        gaps(n)
                    if 1 <= n <= len(items):
                        sides(n - 1)
                    if n >= 2:
                        place(n - 2)

            @block.scalar
            def _(act):
                for n in range(len(items)):
                    act.wait_ge(gap_ready, 2 * (n + 1))
                    nc.scalar.activation(gap[:, n % 2], gap[:, n % 2], ACT.Exp).then_inc(grown, 1)

            @block.tensor
            def _(pe):
                pe.wait_ge(both_ready, 1)
                for t in range(NT):
                    ins = nc.tensor.matmul(ps[:, 4 + t // 4, (t % 4) * P:(t % 4 + 1) * P],
                                           both[:, t * P:(t + 1) * P], q[:, h, t * P:(t + 1) * P],
                                           start=True, stop=True)
                ins.then_inc(product, 1)
                for n in range(len(items)):
                    pe.wait_ge(side_ready, 2 * (n + 1))
                    if n >= 2:
                        pe.wait_ge(placed, n)
                    for t in range(NT):
                        x = side[:, n % 2, t * P:(t + 1) * P]
                        ins = nc.tensor.matmul(ps[:, 2 * (n % 2) + t // 4, (t % 4) * P:(t % 4 + 1) * P], x, x,
                                               start=True, stop=True)
                    ins.then_inc(product, 1)


def hgrn_states(c, h, q, key, bcum, values, pairT, out):
    nc = c.nc
    c.recycle()
    hv = slice(h * HK, (h + 1) * HK)
    with ExitStack() as ctx:
        s = lambda n, shape: sbuf(ctx, nc, f"hst{h}_{n}", shape)
        qd, kd, kdT = s("qd", [P, 2, T]), s("kd", [P, 2, T]), s("kdT", [P, 2, NT, P])
        state, last = s("state", [P, 2, NT, P]), s("last", [P, 2, NT])
        ps = psum(ctx, nc, f"hst{h}_ps", 8)
        kgap, kgrown, kside, turned, copied, update, stated, summed = [
            c.sem(f"hst{h}_{x}") for x in
            ("kgap", "kgrown", "kside", "turned", "copied", "update", "stated", "summed")]
        wide = lambda b: ps[:, b:b + 2, :].rearrange("p b (c t) -> p (b c) t", t=P)
        with nc.Block() as block:
            @block.vector
            def _(dve):
                do = c.chain("vector", dve)
                for d in range(2):
                    b3 = bcum[:, d, h].rearrange("p (c t) -> p c t", t=P)
                    end = b3[:, :, 0:1] if d else b3[:, :, P - 1:P]
                    nc.vector.tensor_tensor(kd[:, d].rearrange("p (c t) -> p c t", t=P),
                                            end.to_broadcast([P, NT, P]), b3, ALU.subtract).then_inc(kgap, 1)
                for d in range(2):
                    dve.wait_ge(kgrown, 3 * (d + 1))
                    nc.vector.tensor_tensor(kd[:, d], kd[:, d], key[:, d, h], ALU.mult).then_inc(kside, 1)
                    do(nc.vector.tensor_tensor(qd[:, d], qd[:, d], q[:, h], ALU.mult))
                for d in range(2):
                    order = list(range(NT))[::-1] if d else list(range(NT))
                    do(nc.vector.memset(state[:, d, order[0]], 0.0))
                    dve.wait_ge(update, d + 1)
                    for prev, nxt in zip(order, order[1:]):
                        do(nc.vector.scalar_tensor_tensor(
                            state[:, d, nxt], state[:, d, prev], last[:, d, prev:prev + 1],
                            wide(4 + 2 * d)[:, prev], ALU.mult, ALU.add))
                nc.vector.tensor_copy(last[:, 0, 0:1], last[:, 0, 1:2]).then_inc(stated, 1)
                dve.wait_ge(summed, 1)
                do(nc.vector.tensor_copy(out[:, :, hv], wide(0)))

            @block.scalar
            def _(act):
                for d in range(2):
                    b3 = bcum[:, d, h].rearrange("p (c t) -> p c t", t=P)
                    end = b3[:, :, 0:1] if d else b3[:, :, P - 1:P]
                    nc.scalar.activation(qd[:, d], bcum[:, d, h], ACT.Exp).then_inc(kgrown, 1)
                    nc.scalar.activation(last[:, d].unsqueeze(2), end, ACT.Exp).then_inc(kgrown, 1)
                    act.wait_ge(kgap, d + 1)
                    nc.scalar.activation(kd[:, d], kd[:, d], ACT.Exp).then_inc(kgrown, 1)
                for d in range(2):
                    act.wait_ge(turned, d + 1)
                    nc.scalar.activation(kdT[:, d], wide(2 * d), ACT.Copy).then_inc(copied, 1)

            @block.tensor
            def _(pe):
                for d in range(2):
                    pe.wait_ge(kside, d + 1)
                    for t in range(NT):
                        ins = nc.tensor.transpose(wide(2 * d)[:, t], kd[:, d, t * P:(t + 1) * P], c.ident[:])
                    ins.then_inc(turned, 1)
                for d in range(2):
                    pe.wait_ge(copied, d + 1)
                    for t in range(NT):
                        ins = nc.tensor.matmul(wide(4 + 2 * d)[:, t], kdT[:, d, t], values[:, t, hv],
                                               start=True, stop=True)
                    ins.then_inc(update, 1)
                pe.wait_ge(stated, 1)
                for t in range(NT):
                    nc.tensor.matmul(wide(0)[:, t], pairT[:, t], values[:, t, hv], start=True, stop=False)
                    for d in range(2):
                        ins = nc.tensor.matmul(wide(0)[:, t], qd[:, d, t * P:(t + 1) * P], state[:, d, t],
                                               start=False, stop=(d == 1))
                ins.then_inc(summed, 1)


def mix_first(c, a, x, dbg=None):
    nc = c.nc
    with ExitStack() as ctx:
        s = lambda n, shape, dt=F32: sbuf(ctx, nc, n, shape, dt)
        hT = s("mix_hT", [P, KD, T])
        mla_in = s("mla_in", [P, NT, QR + KVR + ROPE])
        w_in = a["w_in"][0].rearrange("(k p) n -> p k n", p=P)
        with ExitStack() as hg:
            s = lambda n, shape, dt=F32: sbuf(hg, nc, n, shape, dt)
            q = s("hg_q", [P, HH, T])
            logf = x[:].rearrange("p (d h) t -> p d h t", d=2)
            key = s("hg_key", [P, 2, HH, T])
            values = s("hg_values", [P, NT, HH * HK])
            with ExitStack() as w_:
                gain = sbuf(w_, nc, "mix_gain", [P, KD])
                load(c, [(gain[:], a["norm_mix"][0].rearrange("(k p) -> p k", p=P))])
                norm_transpose(c, "mix", x, hT, gain, NT)
            with ExitStack() as w_:
                wbuf = sbuf(w_, nc, "mix_w", [P, 2, KD, CH])
                o = QR + KVR + ROPE
                cols = [slice(0, o)] + [slice(o + i * CH, o + (i + 1) * CH) for i in range(4)]

                def is_rows(i):
                    return i in (0, 4)

                def stationary(i, b, k, w):
                    if is_rows(i):
                        return hT[:, k, b * P:(b + 1) * P]
                    return w[:, k, (b // 2) * P:(b // 2 + 1) * P]

                def moving(i, b, k, w):
                    if is_rows(i):
                        return w[:, k, :cols[i].stop - cols[i].start]
                    return hT[:, k, (b % 2) * CH:(b % 2 + 1) * CH]

                def evacuate(i, b, ps):
                    ch, t = b // 2, slice((b % 2) * CH, (b % 2 + 1) * CH)
                    if i == 0:
                        return nc.scalar.activation(mla_in[:, b], ps[:, :o], ACT.Copy)
                    if i == 4:
                        return nc.scalar.activation(values[:, b], ps, ACT.Copy)
                    if i == 1:
                        return nc.scalar.activation(q[:, ch, t], ps, ACT.Silu)
                    nc.scalar.activation(logf[:, i - 2, ch, t], ps, ACT.Sigmoid)
                    return nc.scalar.activation(key[:, i - 2, ch, t], ps, ACT.Sigmoid, scale=-1.0)

                project(c, "mix_in", wbuf, [w_in[:, :, q_] for q_ in cols], stationary, moving, evacuate, "scalar")
            gate = s("hg_gate", [P, NT, HH * HK])
            with ExitStack() as w_:
                wbuf = sbuf(w_, nc, "mix_wg", [P, 1, KD, CH])
                project(c, "mix_gate", wbuf, [w_in[:, :, o + 4 * CH:o + 5 * CH]],
                        lambda i, b, k, w: hT[:, k, b * P:(b + 1) * P], lambda i, b, k, w: w[:, k],
                        lambda i, b, ps: nc.scalar.activation(gate[:, b], ps, ACT.Silu), "scalar")
            lbl, lb, lb1 = s("lb_logits", [P, 2, 2, HH]), s("lb", [P, 2, HH]), s("lb1", [P, 2, HH])
            onorm = s("hg_onorm", [P, 1, HK])
            load(c, [(lbl[:, r, d], a["hg_lb_logits"][r, d].rearrange("(h p) -> p h", p=P))
                     for r in range(2) for d in range(2)]
                 + [(onorm[:, 0], a["hg_o_norm"][0].unsqueeze(0).to_broadcast([P, HK]))])
            reset = hT[:, 0:HH]
            with nc.Block() as block:
                @block.vector
                def _(dve):
                    do = c.chain("vector", dve)
                    do(nc.vector.tensor_tensor(lb[:], lbl[:, 0], lbl[:, 1], ALU.subtract))
                    do(nc.vector.memset(reset, 1.0))
                    do(nc.vector.memset(reset.rearrange("p h (c t) -> p (h c) t", t=P)[:, :, 0:1], 0.0))
            with nc.Block() as block:
                @block.scalar
                def _(act):
                    do = c.chain("scalar", act)
                    do(nc.scalar.activation(lb1[:], lb[:], ACT.Sigmoid, scale=-1.0))
                    do(nc.scalar.activation(lb[:], lb[:], ACT.Sigmoid))
            hgrn_gates(c, logf, key, lb, lb1, reset, logf)
            masks = level_masks(c, hg)
            pairT = s("hg_pairT", [P, NT, P])
            mixed = hT[:, 4:8].rearrange("p k t -> p (k t)").rearrange("p (m v) -> p m v", v=HH * HK)
            for h in range(HH):
                hgrn_pairs(c, h, q, key, logf, masks, pairT)
                hgrn_states(c, h, q, key, logf, values, pairT, mixed)
            ssq = s("hg_ssq", [P, NT * HH])
            heads = lambda t: t.rearrange("p m (h v) -> p (m h) v", v=HK)
            group_norm(c, "hg_norm", heads(mixed), heads(values[:]), ssq[:], HK, onorm[:])
            with nc.Block() as block:
                @block.vector
                def _(dve):
                    do = c.chain("vector", dve)
                    do(nc.vector.tensor_tensor(values[:], mixed, gate[:], ALU.mult))
            items = [[values[:, m, h * P:(h + 1) * P] for h in range(HH)] for m in range(NT)]
            turn(c, "hg_turn", items, lambda n, ps, copy: copy(
                hT[:, HH:, n * P:(n + 1) * P], ps.rearrange("p (h t) -> p h t", t=P)))
        mla(c, a, mla_in, hT, x[:].rearrange("p m d -> p (m d)")[:, :NT * MH * QK].rearrange(
            "p (m h d) -> p m h d", m=NT, h=MH))
        load(c, [(x[:], a["x"][0].rearrange("(m p) d -> p m d", p=P))])
        out_project(c, "mix_out", hT, a["w_out"][0], x)


def out_project(c, name, srcT, w, x, nk=KD):
    nc = c.nc
    w = w.rearrange("(k p) n -> p k n", p=P)
    with ExitStack() as ctx:
        wbuf = sbuf(ctx, nc, f"{name}_w", [P, 2, nk, CH])
        project(c, name, wbuf, [w[:, :, i * CH:(i + 1) * CH] for i in range(D // CH)],
                lambda i, b, k, w: srcT[:, k, b * P:(b + 1) * P], lambda i, b, k, w: w[:, k],
                lambda i, b, ps: nc.vector.tensor_tensor(x[:, b, i * CH:(i + 1) * CH], ps,
                                                         x[:, b, i * CH:(i + 1) * CH], ALU.add),
                "vector", nk=nk)


def rope_tables(c, ctx, a):
    nc = c.nc
    s = lambda n, shape, dt=F32: sbuf(ctx, nc, n, shape, dt)
    cos, sin = s("rope_cos", [P, NT, HALF]), s("rope_sin", [P, NT, HALF])
    with ExitStack() as tmp:
        s = lambda n, shape, dt=F32: sbuf(tmp, nc, n, shape, dt)
        wide = a["positions"].dtype != I32
        posi = s("rope_posi", [P, NT, 2 if wide else 1], I32)
        pos, ang, t = s("rope_pos", [P, NT]), s("rope_ang", [P, NT, HALF]), s("rope_tmp", [P, NT, HALF])
        src = a["positions"][0]
        if wide:
            src = src.bitcast(I32)
        load(c, [(posi[:], src.rearrange("(m p two) -> p m two", p=P, two=2 if wide else 1))])
        with nc.Block() as block:
            @block.vector
            def _(dve):
                do = c.chain("vector", dve)
                do(nc.vector.tensor_copy(pos[:], posi[:, :, 0]))
                for j in range(HALF):
                    freq = float(np.float32(1.0) / np.float32(ROPE_BASE ** (j / HALF)))
                    do(nc.vector.tensor_scalar(ang[:, :, j], pos[:], freq, None, ALU.mult))
                reduce_angle(nc, do, ang[:], t[:])
                do(nc.vector.tensor_scalar(t[:], ang[:], -1.0, None, ALU.mult))
                do(nc.vector.tensor_tensor(t[:], t[:], ang[:], ALU.min))
                do(nc.vector.tensor_scalar(t[:], t[:], math.pi / 2, None, ALU.add))
        with nc.Block() as block:
            @block.scalar
            def _(act):
                nc.scalar.activation(sin[:], ang[:], ACT.Sin)
                nc.scalar.activation(cos[:], t[:], ACT.Sin)
    return cos, sin


def mla(c, a, mla_in, mixT, scratch):
    nc = c.nc
    with ExitStack() as ctx:
        s = lambda n, shape, dt=F32: sbuf(ctx, nc, n, shape, dt)
        qT, kT = s("mla_qT", [QK, MH, T]), s("mla_kT", [QK, MH, T])
        v = s("mla_v", [P, NT, MH, VD])
        with ExitStack() as ctx2:
            s = lambda n, shape, dt=F32: sbuf(ctx2, nc, n, shape, dt)
            q = scratch
            cos, sin = rope_tables(c, ctx2, a)
            qn, kn = s("mla_qn", [P, 1, QK]), s("mla_kn", [P, 1, QK])
            ssq = s("mla_ssq", [P, NT * MH])
            with ExitStack() as ctx3:
                s = lambda n, shape, dt=F32: sbuf(ctx3, nc, n, shape, dt)
                qga, qgb, kvg = s("mla_qga", [P, 1]), s("mla_qgb", [QR - P, 1]), s("mla_kvg", [P, 1])
                wqa, wqb = s("mla_wqa", [P, MH * QK]), s("mla_wqb", [QR - P, MH * QK])
                wkv = s("mla_wkv", [P, MH * (NOPE + VD)])
                cqT, cqT2, ckvT = s("mla_cqT", [P, T]), s("mla_cqT2", [QR - P, T]), s("mla_ckvT", [P, T])
                k = s("mla_k", [P, NT, MH, QK])
                load(c, [(qga[:], a["mla_q_a_norm"][0, 0:P].unsqueeze(1)),
                         (qgb[:], a["mla_q_a_norm"][0, P:QR].unsqueeze(1)),
                         (kvg[:], a["mla_kv_a_norm"][0].unsqueeze(1)),
                         (wqa[:], a["mla_w_q_up"][0, 0:P, :]), (wqb[:], a["mla_w_q_up"][0, P:QR, :]),
                         (wkv[:], a["mla_w_kv_up"][0]),
                         (qn[:, 0], a["mla_q_norm"][0].unsqueeze(0).to_broadcast([P, QK])),
                         (kn[:, 0], a["mla_k_norm"][0].unsqueeze(0).to_broadcast([P, QK]))])
                flat = lambda t: t.rearrange("p m h d -> p m (h d)")
                junk = flat(q[:])
                group_norm(c, "mla_cq", mla_in[:, :, 0:QR], junk[:, :, 0:QR], ssq[:, 0:NT], QR, None)
                group_norm(c, "mla_ckv", mla_in[:, :, QR:QR + KVR], junk[:, :, 0:KVR], ssq[:, 0:NT], KVR, None)
                items = [[mla_in[:, m, 0:P], mla_in[:, m, P:QR], mla_in[:, m, QR:QR + KVR]] for m in range(NT)]

                def out(n, ps, copy):
                    t = slice(n * P, (n + 1) * P)
                    if n % 2:
                        nc.vector.tensor_scalar(cqT[:, t], ps[:, 0:P], qga[:, 0:1], None, ALU.mult)
                        nc.vector.tensor_scalar(cqT2[:, t], ps[:QR - P, P:2 * P], qgb[:, 0:1], None, ALU.mult)
                        return nc.vector.tensor_scalar(ckvT[:, t], ps[:, 2 * P:3 * P], kvg[:, 0:1], None, ALU.mult)
                    nc.scalar.activation(cqT[:, t], ps[:, 0:P], ACT.Copy, scale=qga[:, 0:1])
                    nc.scalar.activation(cqT2[:, t], ps[:QR - P, P:2 * P], ACT.Copy, scale=qgb[:, 0:1])
                    return nc.scalar.activation(ckvT[:, t], ps[:, 2 * P:3 * P], ACT.Copy, scale=kvg[:, 0:1])

                turn(c, "mla_turn", items, out)
                up = ExitStack()
                ps = psum(up, nc, "mla_up_ps", 8)
                made = c.sem("mla_up_made")
                q_taken, kv_taken = c.sem("mla_q_taken"), c.sem("mla_kv_taken")
                hq = MH // 2 * QK
                with nc.Block() as block:
                    @block.tensor
                    def _(pe):
                        for m in range(NT):
                            t, b0 = slice(m * P, (m + 1) * P), 4 * (m % 2)
                            if m >= 2:
                                pe.wait_ge(q_taken, m - 1)
                                pe.wait_ge(kv_taken, m - 1)
                            for b in range(2):
                                nc.tensor.matmul(ps[:, b0 + b, :hq], cqT[:, t], wqa[:, b * hq:(b + 1) * hq],
                                                 start=True, stop=False)
                                nc.tensor.matmul(ps[:, b0 + b, :hq], cqT2[:, t], wqb[:, b * hq:(b + 1) * hq],
                                                 start=False, stop=True)
                            for b in range(2):
                                ins = nc.tensor.matmul(ps[:, b0 + 2 + b], ckvT[:, t], wkv[:, b * CH:(b + 1) * CH],
                                                       start=True, stop=True)
                            ins.then_inc(made, 1)

                    @block.scalar
                    def _(act):
                        for m in range(NT):
                            act.wait_ge(made, m + 1)
                            b0 = 4 * (m % 2)
                            nc.scalar.activation(
                                q[:, m].rearrange("p (b h) d -> p b (h d)", b=2), ps[:, b0:b0 + 2, :hq],
                                ACT.Copy).then_inc(q_taken, 1)

                    @block.vector
                    def _(dve):
                        for m in range(NT):
                            dve.wait_ge(made, m + 1)
                            b0 = 4 * (m % 2)
                            kv = ps[:, b0 + 2:b0 + 4, :].rearrange("p b (h d) -> p (b h) d", d=NOPE + VD)
                            nc.vector.tensor_copy(k[:, m, :, 0:NOPE], kv[:, :, 0:NOPE])
                            nc.vector.tensor_copy(
                                k[:, m, :, NOPE:],
                                mla_in[:, m, QR + KVR:].unsqueeze(1).to_broadcast([P, MH, ROPE]))
                            nc.vector.tensor_copy(v[:, m], kv[:, :, NOPE:]).then_inc(kv_taken, 1)
                up.close()
                for name, y, gain, dst in (("mla_qn", q, qn, qT), ("mla_kn", k, kn, kT)):
                    grp = y[:].rearrange("p m h d -> p (m h) d")
                    sqt = mixT[:, 0:4].rearrange("p k t -> p (k t)")[:, :NT * MH // 2 * QK].rearrange(
                        "p (g d) -> p g d", d=QK)
                    for hf in range(2):
                        gs = slice(hf * NT * MH // 2, (hf + 1) * NT * MH // 2)
                        group_norm(c, f"{name}{hf}", grp[:, gs], sqt, ssq[:, gs], QK, gain[:])
                    rope(c, name, y, cos, sin, sqt)
                    items = [[y[:, m, 4 * hh + i] for i in range(4)] for m in range(NT) for hh in range(2)]

                    def out(n, ps, copy, dst=dst):
                        m, hh = divmod(n, 2)
                        return copy(dst[:, 4 * hh:4 * hh + 4, m * P:(m + 1) * P],
                                    ps[:QK].rearrange("p (h t) -> p h t", t=P))

                    turn(c, f"{name}_turn", items, out)
        with ExitStack() as ctx2:
            o = sbuf(ctx2, nc, "mla_o", [P, NT, MH, VD])
            attention(c, "mla_attn", MH, T,
                      lambda h, m: [qT[:, h, m * P:(m + 1) * P]], lambda h: [kT[:, h]],
                      lambda h, j: v[:, j, h], lambda h, m: o[:, m, h], QK ** -0.5, VD)
            of = o[:].rearrange("p m h d -> p m (h d)")
            items = [[of[:, m, k * P:(k + 1) * P] for k in range(4)] for m in range(NT)]
            turn(c, "mla_oturn", items, lambda n, ps, copy: copy(
                mixT[:, 0:4, n * P:(n + 1) * P], ps.rearrange("p (h t) -> p h t", t=P)))


def rope(c, name, y, cos, sin, tmp):
    nc = c.nc
    with nc.Block() as block:
        @block.vector
        def _(dve):
            do = c.chain("vector", dve)
            for m in range(NT):
                y1, y2 = y[:, m, :, NOPE:NOPE + HALF], y[:, m, :, NOPE + HALF:]
                cs, sn = [t[:, m].unsqueeze(1).to_broadcast([P, MH, HALF]) for t in (cos, sin)]
                parts = [tmp[:, i * MH:(i + 1) * MH, 0:HALF] for i in range(4)]
                do_all = [(parts[0], y1, cs), (parts[1], y2, sn), (parts[2], y2, cs), (parts[3], y1, sn)]
                for o, l, r in do_all[:3]:
                    nc.vector.tensor_tensor(o, l, r, ALU.mult)
                do(nc.vector.tensor_tensor(*do_all[3], ALU.mult))
                nc.vector.tensor_tensor(y1, parts[0], parts[1], ALU.subtract)
                do(nc.vector.tensor_tensor(y2, parts[2], parts[3], ALU.add))



def cross_first(c, a, x):
    nc = c.nc
    kv_cols = 2 * XH * XD
    with ExitStack() as ctx:
        s = lambda n, shape, dt=F32: sbuf(ctx, nc, n, shape, dt)
        gain, mgain = s("x_gain", [P, KD]), s("x_mgain", [P, KD])
        qn, kn = s("x_qn", [P, 1, XD]), s("x_kn", [P, 1, XD])
        kT = s("x_kT", [P, XH * 2, MEM])
        kv = s("x_kv", [P, MEM // P, kv_cols])
        ssq = s("x_ssq", [P, NT * XH])
        hT = s("x_hT", [P, KD, T])
        q = s("x_q", [P, NT, XH * XD])
        mem = q[:, 0:MEM // P]
        per_k = lambda n: a[n][0].rearrange("(k p) -> p k", p=P)
        load(c, [(mem, a["mem"][0].rearrange("(m p) d -> p m d", p=P)),
                 (gain[:], per_k("norm_cross")), (mgain[:], per_k("norm_mem")),
                 (qn[:, 0], a["x_q_norm"][0].unsqueeze(0).to_broadcast([P, XD])),
                 (kn[:, 0], a["x_k_norm"][0].unsqueeze(0).to_broadcast([P, XD]))])
        memT = hT[:, :, 0:MEM]
        norm_transpose(c, "x_mem", mem, memT, mgain, MEM // P)
        cols = lambda w, i: w[0].rearrange("(k p) n -> p k n", p=P)[:, :, i * CH:(i + 1) * CH]
        with ExitStack() as w_:
            wbuf = sbuf(w_, nc, "x_w", [P, 2, KD, CH])
            project(c, "x_kv_up", wbuf, [cols(a["x_w_kv"], i) for i in range(kv_cols // CH)],
                    lambda i, b, k, w: memT[:, k, b * P:(b + 1) * P], lambda i, b, k, w: w[:, k],
                    lambda i, b, ps: nc.scalar.activation(kv[:, b, i * CH:(i + 1) * CH], ps, ACT.Copy),
                    "scalar", banks=MEM // P)
            for m in range(MEM // P):
                grp = kv[:, m, 0:XH * XD].rearrange("p (h d) -> p h d", d=XD)
                group_norm(c, f"x_k{m}", grp, q[:, 0].rearrange("p (h d) -> p h d", d=XD), ssq[:, 0:XH], XD, kn[:])
            items = [[kv[:, m, (4 * g + j) * P:(4 * g + j + 1) * P] for j in range(4)]
                     for m in range(MEM // P) for g in range(2)]
            turn(c, "x_kturn", items, lambda n, ps, copy: copy(
                kT[:, 4 * (n % 2):4 * (n % 2) + 4, (n // 2) * P:(n // 2 + 1) * P],
                ps.rearrange("p (j t) -> p j t", t=P)))
            norm_transpose(c, "x_x", x, hT, gain, NT)
            project(c, "x_q_up", wbuf, [cols(a["x_w_q"], i) for i in range(D // CH)],
                    lambda i, b, k, w: hT[:, k, b * P:(b + 1) * P], lambda i, b, k, w: w[:, k],
                    lambda i, b, ps: nc.scalar.activation(q[:, b, i * CH:(i + 1) * CH], ps, ACT.Copy), "scalar")
        heads = q[:].rearrange("p m (h d) -> p (m h) d", d=XD)
        group_norm(c, "x_qn", heads, hT[:].rearrange("p k t -> p (k t)").rearrange("p (g d) -> p g d", d=XD),
                   ssq[:], XD, qn[:])

        def turn_rows(name, src):
            items = [[src[:, m, (4 * g + j) * P:(4 * g + j + 1) * P] for j in range(4)]
                     for m in range(NT) for g in range(2)]
            turn(c, name, items, lambda n, ps, copy: copy(
                hT[:, 4 * (n % 2):4 * (n % 2) + 4, (n // 2) * P:(n // 2 + 1) * P],
                ps.rearrange("p (j t) -> p j t", t=P)))

        turn_rows("x_qturn", q)
        attention(c, "x_attn", XH, MEM,
                  lambda h, m: [hT[:, 2 * h + j, m * P:(m + 1) * P] for j in range(2)],
                  lambda h: [kT[:, 2 * h + j] for j in range(2)],
                  lambda h, j: kv[:, j, XH * XD + h * XD:XH * XD + (h + 1) * XD],
                  lambda h, m: q[:, m, h * XD:(h + 1) * XD], XD ** -0.5, XD)
        turn_rows("x_oturn", q)
        out_project(c, "x_out", hT, a["x_w_o"][0], x)



def pick_first(nc, do, v, mx, ids, eq, oh):
    wide = mx.unsqueeze(2).to_broadcast([P, NT, 8])
    do(nc.vector.tensor_tensor(eq, v, wide, ALU.is_equal))
    do(nc.vector.scalar_tensor_tensor(eq, eq, -8.0, ids, ALU.mult, ALU.add))
    do(nc.vector.tensor_reduce(mx, eq, AX, ALU.min))
    do(nc.vector.tensor_tensor(oh, eq, wide, ALU.is_equal))


def route(c, a, hT, w1, w2, slot_tok, slot_row, ov_expert, ov_count):
    nc = c.nc
    c.recycle()
    NE = G + E
    with ExitStack() as ctx:
        s = lambda n, shape, dt=F32: sbuf(ctx, nc, n, shape, dt)
        wr, bias = s("rt_w", [P, KD, NE]), s("rt_bias", [P, 1, NE])
        lg = s("rt_logits", [P, NT, NE])
        load(c, [(wr[:, :, 0:G], a["moe_w_group"][0].rearrange("(k p) n -> p k n", p=P)),
                 (wr[:, :, G:], a["moe_w_expert"][0].rearrange("(k p) n -> p k n", p=P)),
                 (bias[:, 0, 0:G], a["moe_b_group"][0].unsqueeze(0).to_broadcast([P, G])),
                 (bias[:, 0, G:], a["moe_b_expert"][0].unsqueeze(0).to_broadcast([P, E]))])
        ps = psum(ctx, nc, "rt_ps", 8)
        with nc.Block() as block:
            @block.tensor
            def _(pe):
                for m in range(NT):
                    for k in range(KD):
                        nc.tensor.matmul(ps[:, m, :NE], hT[:, k, m * P:(m + 1) * P], wr[:, k],
                                         start=(k == 0), stop=(k == KD - 1))
        ids8, tok = s("rt_ids8", [P, NT, 8]), s("rt_tok", [P, NT])
        e128, ids15 = s("rt_e128", [P, 1, E]), s("rt_ids15", [P, OVB])
        idsb = s("rt_idsb", [P, NBLK])
        gm, eq, gh = s("rt_gm", [P, NT]), s("rt_eq", [P, NT, 8]), s("rt_gh", [P, NT, 8])
        ex, gs = s("rt_ex", [P, NT, 8]), s("rt_gs", [P, NT])
        prod = s("rt_prod", [P, NT, G, PG])
        sel, m1, m2 = s("rt_sel", [P, NT, 8]), s("rt_m1", [P, NT]), s("rt_m2", [P, NT])
        oh = [s(f"rt_oh{k}", [P, NT, 8]) for k in range(2)]
        pick = [s(f"rt_pick{k}", [P, NT, G, PG]) for k in range(2)]
        both = s("rt_both", [P, NT, E])
        with nc.Block() as block:
            @block.gpsimd
            def _(pool):
                it = lambda t, pat, base, mul: nc.gpsimd.iota(t, pat, base=base, channel_multiplier=mul,
                                                              allow_small_or_imprecise_dtypes=True)
                it(ids8[:], [[0, NT], [1, 8]], 0, 0)
                it(tok[:], [[P, NT]], 0, 1)
                it(e128[:, 0], [[P, E]], 0, 0)
                it(ids15[:], [[1, OVB]], 0, 0)
                it(idsb[:], [[1, NBLK]], 0, 0)

            @block.vector
            def _(dve):
                do = c.chain("vector", dve)
                do(nc.vector.tensor_tensor(lg[:], ps[:, :, :NE], bias[:].to_broadcast([P, NT, NE]), ALU.add))
                do(nc.vector.tensor_reduce(gm[:], lg[:, :, 0:G], AX, ALU.max))
                do(nc.vector.tensor_tensor(ex[:], lg[:, :, 0:G], gm[:].unsqueeze(2).to_broadcast([P, NT, G]),
                                           ALU.subtract))
        with nc.Block() as block:
            @block.scalar
            def _(act):
                nc.scalar.activation(ex[:], ex[:], ACT.Exp)

            @block.vector
            def _(dve):
                do = c.chain("vector", dve)
                pick_first(nc, do, lg[:, :, 0:G], gm[:], ids8[:], eq[:], gh[:])
                do(nc.vector.tensor_tensor(prod[:], lg[:, :, G:].rearrange("p m (g l) -> p m g l", l=PG),
                                           gh[:].unsqueeze(3).to_broadcast([P, NT, G, PG]), ALU.mult))
                do(nc.vector.tensor_reduce(sel[:], prod[:].rearrange("p m g l -> p m l g"), AX, ALU.add))
                do(nc.vector.tensor_reduce(m1[:], sel[:], AX, ALU.max))
                do(nc.vector.tensor_copy(gm[:], m1[:]))
                pick_first(nc, do, sel[:], gm[:], ids8[:], eq[:], oh[0][:])
                do(nc.vector.scalar_tensor_tensor(sel[:], oh[0][:], -1e30, sel[:], ALU.mult, ALU.add))
                do(nc.vector.tensor_reduce(m2[:], sel[:], AX, ALU.max))
                do(nc.vector.tensor_copy(gm[:], m2[:]))
                pick_first(nc, do, sel[:], gm[:], ids8[:], eq[:], oh[1][:])
                do(nc.vector.tensor_tensor(m2[:], m2[:], m1[:], ALU.subtract))
                for k in range(2):
                    do(nc.vector.tensor_tensor(pick[k][:], gh[:].unsqueeze(3).to_broadcast([P, NT, G, PG]),
                                               oh[k][:].unsqueeze(2).to_broadcast([P, NT, G, PG]), ALU.mult))
                flat = [pick[k][:].rearrange("p m g l -> p m (g l)") for k in range(2)]
                do(nc.vector.tensor_tensor(both[:], flat[0], flat[1], ALU.add))
        with nc.Block() as block:
            @block.scalar
            def _(act):
                nc.scalar.activation(m2[:], m2[:], ACT.Exp)

            @block.tensor
            def _(pe):
                for m in range(NT):
                    for i in range(m + 1):
                        nc.tensor.matmul(ps[:, 0, m * E:(m + 1) * E], (c.before if i == m else c.ones)[:],
                                         both[:, i], start=(i == 0), stop=(i == m))
                for i in range(NT):
                    nc.tensor.matmul(ps[:, 1, :E], c.ones[:], both[:, i], start=(i == 0), stop=(i == NT - 1))
        nb, oend, high = s("rt_nb", [P, 1, E]), s("rt_oend", [P, 1, E]), s("rt_high", [P, 1, E])
        rank, low, dst = s("rt_rank", [P, NT, E]), s("rt_low", [P, NT, E]), s("rt_dst", [P, NT, E])
        dest, blk, pos, val = [s(f"rt_{n}", [P, 2, NT]) for n in ("dest", "blk", "pos", "val")]
        atpos = s("rt_atpos", [P, 2, NT, P])
        atblk = s("rt_atblk", [P, 2, NT, NBLK])
        over = s("rt_over", [P, OVB, E])
        oe = s("rt_oe", [P, OVB])
        with nc.Block() as block:
            @block.vector
            def _(dve):
                do = c.chain("vector", dve)
                v = nc.vector
                do(v.tensor_reduce(gs[:], ex[:], AX, ALU.add))
                do(v.tensor_scalar(m1[:], m2[:], 1.0, None, ALU.add))
                do(v.tensor_tensor(gs[:], gs[:], m1[:], ALU.mult))
                do(v.reciprocal(w1, gs[:]))
                do(v.tensor_tensor(w2, w1, m2[:], ALU.mult))
                do(v.tensor_scalar(nb[:, 0], ps[:, 1, :E], -float(P), 0.0, ALU.add, ALU.max))
                do(v.tensor_scalar(nb[:], nb[:], 1.0 / P, (P - 0.5) / P - 0.5, ALU.mult, ALU.add))
                do(v.tensor_scalar(nb[:], nb[:], ROUND, None, ALU.add))
                do(v.tensor_scalar(nb[:], nb[:], -ROUND, None, ALU.add))
                do(v.tensor_tensor_scan(oend[:, 0], c.ones[:, :E], nb[:, 0], 0.0, ALU.mult, ALU.add))
                do(v.tensor_tensor(high[:], oend[:], nb[:], ALU.subtract))
                do(v.tensor_scalar(high[:], high[:], float(P), float(E * P - P), ALU.mult, ALU.add))
                do(v.tensor_copy(rank[:].rearrange("p m e -> p (m e)"), ps[:, 0]))
                do(v.tensor_scalar(low[:], rank[:], float(P), None, ALU.is_lt))
                do(v.tensor_tensor(e128[:], e128[:], high[:], ALU.subtract))
                do(v.tensor_tensor(low[:], low[:], e128[:].to_broadcast([P, NT, E]), ALU.mult))
                do(v.tensor_tensor(dst[:], rank[:], high[:].to_broadcast([P, NT, E]), ALU.add))
                do(v.tensor_tensor(dst[:], dst[:], low[:], ALU.add))
                for k in range(2):
                    do(v.tensor_tensor(rank[:], dst[:], pick[k][:].rearrange("p m g l -> p m (g l)"), ALU.mult))
                    do(v.tensor_reduce(dest[:, k], rank[:], AX, ALU.add))
                    do(v.tensor_scalar(val[:, k], tok[:], 2.0, float(k + 1), ALU.mult, ALU.add))
                do(v.tensor_scalar(blk[:], dest[:], 1.0 / P, 0.5 / P - 0.5, ALU.mult, ALU.add))
                do(v.tensor_scalar(blk[:], blk[:], ROUND, None, ALU.add))
                do(v.tensor_scalar(blk[:], blk[:], -ROUND, None, ALU.add))
                do(v.scalar_tensor_tensor(pos[:], blk[:], -float(P), dest[:], ALU.mult, ALU.add))
                for k in range(2):
                    for m in range(NT):
                        v.tensor_scalar(atpos[:, k, m], c.row[:], pos[:, k, m:m + 1], None, ALU.is_equal)
                        v.tensor_scalar(atblk[:, k, m], idsb[:], blk[:, k, m:m + 1], val[:, k, m:m + 1],
                                        ALU.is_equal, ALU.mult)
                do(v.tensor_tensor(over[:], oend[:].to_broadcast([P, OVB, E]),
                                   ids15[:].unsqueeze(2).to_broadcast([P, OVB, E]), ALU.is_le))
                do(v.tensor_reduce(oe[:], over[:], AX, ALU.add))
                do(v.tensor_scalar(ov_expert, oe[0:1, :], float(E - 1), None, ALU.min))
                do(v.tensor_copy(ov_count, oend[0:1, 0, E - 1:E]))
        with nc.Block() as block:
            @block.tensor
            def _(pe):
                n = [(k, m) for k in range(2) for m in range(NT)]
                for i, (k, m) in enumerate(n):
                    nc.tensor.matmul(ps[:, 2, :NBLK], atpos[:, k, m], atblk[:, k, m], start=(i == 0),
                                     stop=(i == len(n) - 1))
        free, rowv, tokv = s("rt_free", [P, NBLK]), s("rt_rowv", [P, NBLK]), s("rt_tokv", [P, NBLK])
        with nc.Block() as block:
            @block.vector
            def _(dve):
                do = c.chain("vector", dve)
                v = nc.vector
                do(v.tensor_scalar(free[:], ps[:, 2, :NBLK], 0.0, 4.0 * T, ALU.is_equal, ALU.mult))
                do(v.tensor_scalar(rowv[:], ps[:, 2, :NBLK], -1.0, None, ALU.add))
                do(v.tensor_scalar(tokv[:], rowv[:], 0.5, -0.25, ALU.mult, ALU.add))
                do(v.tensor_scalar(tokv[:], tokv[:], ROUND, None, ALU.add))
                do(v.tensor_scalar(tokv[:], tokv[:], -ROUND, None, ALU.add))
                do(v.tensor_tensor(tokv[:], tokv[:], free[:], ALU.add))
                do(v.tensor_tensor(rowv[:], rowv[:], free[:], ALU.add))
                do(v.tensor_copy(slot_tok, tokv[:]))
                do(v.tensor_copy(slot_row, rowv[:]))


def wait_for(eng, sem, value):
    if not (isinstance(value, int) and value <= 0):
        eng.wait_ge(sem, value)


class ExpertSteps:

    def __init__(self, c, ctx, name, a, xn, y, gain, slot_tok, slot_row, depth):
        self.nc, self.c, self.a, self.xn, self.y, self.gain, self.depth = c.nc, c, a, xn, y, gain, depth
        self.slot_tok, self.slot_row = slot_tok, slot_row
        s = lambda n, shape, dt=F32: sbuf(ctx, c.nc, f"{name}_{n}", shape, dt)
        d = depth
        self.wgu, self.wd = s("wgu", [P, d, KD, 2 * EH]), s("wd", [P, d, EH // P, D])
        self.rows, self.rowsT = s("rows", [P, d, D]), s("rowsT", [P, d, KD, P])
        self.itok, self.irow = s("itok", [P, d], I32), s("irow", [P, d], I32)
        self.gated, self.hid, self.hidT = s("gated", [P, d, EH]), s("hid", [P, d, EH]), s("hidT", [P, d, 2, P])
        self.res = s("res", [P, d, D])
        self.ps_t, self.ps_h = psum(ctx, c.nc, f"{name}_pt", 2), psum(ctx, c.nc, f"{name}_ph", 2)
        self.ps_u, self.ps_y = psum(ctx, c.nc, f"{name}_pu", 1), psum(ctx, c.nc, f"{name}_py", 2)
        m = c.sem
        self.gathered = [m(f"{name}_gathered{b}") for b in range(d)]
        self.gu_in = [m(f"{name}_gate_up_in{b}") for b in range(d)]
        self.d_in = [m(f"{name}_down_in{b}") for b in range(d)]
        self.scattered = [m(f"{name}_scattered{b}") for b in range(d)]
        self.placed, self.gathers, self.scatters = [m(f"{name}_{x}") for x in ("placed", "gathers", "scatters")]
        self.indexed, self.rows_turned, self.rowsT_ready, self.up_done, self.gated_ready = [
            m(f"{name}_{x}") for x in ("indexed", "rows_turned", "rowsT_ready", "up_done", "gated_ready")]
        self.hid_ready, self.hid_turned, self.hidT_ready, self.down_done, self.res_ready = [
            m(f"{name}_{x}") for x in ("hid_ready", "hid_turned", "hidT_ready", "down_done", "res_ready")]

    def load_weights(self, sp, n, b, expert):
        a, d = self.a, self.depth
        wait_for(sp, self.up_done, n - d + 1)
        for i, w in enumerate(("moe_w_gate", "moe_w_up")):
            src = a[w][0, bass.ds(expert, 1)].rearrange("o (k p) n -> p (o k) n", p=P)
            sp.dma_start(self.wgu[:, b, :, i * EH:(i + 1) * EH], src).then_inc(self.gu_in[b], 16)
        wait_for(sp, self.down_done, n - d + 1)
        src = a["moe_w_down"][0, bass.ds(expert, 1)].rearrange("o (k p) n -> p (o k) n", p=P)
        sp.dma_start(self.wd[:, b], src).then_inc(self.d_in[b], 16)

    def gather(self, pool, n, b, column):
        nc, d = self.nc, self.depth
        source = self.slot_tok[:, bass.ds(column if isinstance(column, int) else pool.snap(column), 1)]
        wait_for(pool, self.rows_turned, n - d + 1)
        nc.gpsimd.tensor_copy(self.itok[:, b:b + 1], source).then_inc(self.indexed, 1)
        bound = pool.to_reg(T - 1)
        pool.wait_ge(self.indexed, n + 1)
        pool.sem_inc(self.gathers, 1)
        nc.gpsimd.indirect_dma_start(
            out=self.rows[:, b], out_offset=None, in_=self.xn[:],
            in_offset=bass.IndirectOffsetOnAxis(ap=self.itok[:, b:b + 1], axis=0),
            bounds_check=bound, oob_is_err=False).then_inc(self.gathered[b], 16)

    def scatter(self, pool, n, b, column, use):
        source = self.slot_row[:, bass.ds(column if isinstance(column, int) else pool.snap(column), 1)]
        wait_for(pool, self.scattered[b], 16 * use)
        self.nc.gpsimd.tensor_copy(self.irow[:, b:b + 1], source).then_inc(self.placed, 1)
        bound = pool.to_reg(2 * T - 1)
        pool.wait_ge(self.placed, n + 1)
        pool.wait_ge(self.res_ready, n + 1)
        pool.sem_inc(self.scatters, 1)
        self.nc.gpsimd.indirect_dma_start(
            out=self.y[:], out_offset=bass.IndirectOffsetOnAxis(ap=self.irow[:, b:b + 1], axis=0),
            in_=self.res[:, b], in_offset=None,
            bounds_check=bound, oob_is_err=False).then_inc(self.scattered[b], 16)

    def turn_rows(self, pe, n, b, use):
        pe.wait_ge(self.gathered[b], 16 * use + 16)
        wait_for(pe, self.rowsT_ready, n)
        for k in range(KD):
            ins = self.nc.tensor.transpose(self.ps_t[:, k // 4, (k % 4) * P:(k % 4 + 1) * P],
                                           self.rows[:, b, k * P:(k + 1) * P], self.c.ident[:])
        ins.then_inc(self.rows_turned, 1)

    def up(self, pe, n, b, use):
        pe.wait_ge(self.rowsT_ready, n + 1)
        pe.wait_ge(self.gu_in[b], 32 * use + 32)
        wait_for(pe, self.hid_ready, n - self.depth + 1)
        for k in range(KD):
            ins = self.nc.tensor.matmul(self.ps_h[:, b], self.rowsT[:, b, k], self.wgu[:, b, k],
                                        start=(k == 0), stop=(k == KD - 1))
        ins.then_inc(self.up_done, 1)

    def turn_hidden(self, pe, n, b):
        pe.wait_ge(self.hid_ready, n + 1)
        wait_for(pe, self.hidT_ready, n)
        for k in range(EH // P):
            ins = self.nc.tensor.transpose(self.ps_u[:, 0, k * P:(k + 1) * P],
                                           self.hid[:, b, k * P:(k + 1) * P], self.c.ident[:])
        ins.then_inc(self.hid_turned, 1)

    def down(self, pe, n, b, use):
        pe.wait_ge(self.hidT_ready, n + 1)
        pe.wait_ge(self.d_in[b], 16 * use + 16)
        wait_for(pe, self.res_ready, n)
        for h in range(D // CH):
            for k in range(EH // P):
                ins = self.nc.tensor.matmul(self.ps_y[:, h], self.hidT[:, b, k], self.wd[:, b, k, h * CH:(h + 1) * CH],
                                            start=(k == 0), stop=(k == EH // P - 1))
        ins.then_inc(self.down_done, 1)

    def take_rowsT(self, dve, n, b):
        dve.wait_ge(self.rows_turned, n + 1)
        wait_for(dve, self.up_done, n - self.depth + 1)
        self.nc.vector.tensor_tensor(
            self.rowsT[:, b], self.ps_t[:].rearrange("p b (k t) -> p (b k) t", t=P),
            self.gain[:].unsqueeze(2).to_broadcast([P, KD, P]), ALU.mult).then_inc(self.rowsT_ready, 1)

    def take_hidden(self, dve, n, b):
        dve.wait_ge(self.gated_ready, n + 1)
        wait_for(dve, self.hid_turned, n - self.depth + 1)
        self.nc.vector.tensor_tensor(self.hid[:, b], self.ps_h[:, b, EH:], self.gated[:, b],
                                     ALU.mult).then_inc(self.hid_ready, 1)

    def take_hiddenT(self, dve, n, b):
        dve.wait_ge(self.hid_turned, n + 1)
        wait_for(dve, self.down_done, n - self.depth + 1)
        self.nc.vector.tensor_copy(self.hidT[:, b].rearrange("p k t -> p (k t)"),
                                   self.ps_u[:, 0, :EH]).then_inc(self.hidT_ready, 1)

    def gate(self, act, n, b):
        act.wait_ge(self.up_done, n + 1)
        wait_for(act, self.hid_ready, n - self.depth + 1)
        self.nc.scalar.activation(self.gated[:, b], self.ps_h[:, b, :EH], ACT.Silu).then_inc(self.gated_ready, 1)

    def take_result(self, act, n, b, use):
        act.wait_ge(self.down_done, n + 1)
        wait_for(act, self.scattered[b], 16 * use)
        self.nc.scalar.activation(self.res[:, b].rearrange("p (h n) -> p h n", n=CH), self.ps_y[:],
                                  ACT.Copy).then_inc(self.res_ready, 1)


def over_blocks(eng, body, first, last):
    for n in (first, first + 1):
        body(n, n % 2, n // 2)
    with eng.Fori(first // 2 + 1, last // 2 - 1) as i:
        for b in range(2):
            body(i * 2 + b, b, i)
    for n in (last - 2, last - 1):
        body(n, n % 2, n // 2)


def moe_first(c, a, x):
    nc = c.nc
    xn = nc.dram_tensor("ffn_rows", [T, D], F32).ap()
    y = nc.dram_tensor("expert_results", [2 * T, D], F32).ap()
    with ExitStack() as ctx:
        s = lambda n, shape, dt=F32: sbuf(ctx, nc, n, shape, dt)
        gain = s("ffn_gain", [P, KD])
        w1, w2 = s("moe_w1", [P, NT]), s("moe_w2", [P, NT])
        slot_tok, slot_row = s("slot_tok", [P, NBLK], I32), s("slot_row", [P, NBLK], I32)
        ov_expert, ov_count = s("ov_expert", [1, OVB], I32), s("ov_count", [1, 1], I32)
        with ExitStack() as tmp:
            hT = sbuf(tmp, nc, "ffn_hT", [P, KD, T])
            load(c, [(gain[:], a["norm_ffn"][0].rearrange("(k p) -> p k", p=P))])
            norm_transpose(c, "ffn", x, hT, gain, NT, keep=xn)
            route(c, a, hT, w1[:], w2[:], slot_tok[:], slot_row[:], ov_expert[:], ov_count[:])
        c.recycle(0)
        with ExitStack() as run:
            st = ExpertSteps(c, run, "moe", a, xn, y, gain, slot_tok, slot_row, 2)
            clear_rows(c, st.rows)
            last = E - 1
            with nc.Block() as block:
                @block.sync
                def _(sp):
                    over_blocks(sp, lambda n, b, use: st.load_weights(sp, n, b, n), 0, E)

                @block.gpsimd
                def _(pool):
                    for n in range(2):
                        st.gather(pool, n, n, n)

                    def body(n, b, use):
                        if not (isinstance(n, int) and n > last - 2):
                            st.gather(pool, n + 2, b, n + 2)
                        st.scatter(pool, n, b, n, use)

                    over_blocks(pool, body, 0, E)
                    for b in range(2):
                        pool.wait_ge(st.scattered[b], 16 * E // 2)

                @block.tensor
                def _(pe):
                    st.turn_rows(pe, 0, 0, 0)
                    st.up(pe, 0, 0, 0)
                    st.turn_rows(pe, 1, 1, 0)

                    def body(n, b, use):
                        ends = isinstance(n, int)
                        if not (ends and n > last - 2):
                            st.turn_rows(pe, n + 2, b, use + 1)
                        if not (ends and n > last - 1):
                            st.up(pe, n + 1, 1 - b, use + b)
                        st.turn_hidden(pe, n, b)
                        st.down(pe, n, b, use)

                    over_blocks(pe, body, 0, E)

                @block.vector
                def _(dve):
                    st.take_rowsT(dve, 0, 0)
                    st.take_rowsT(dve, 1, 1)
                    st.take_hidden(dve, 0, 0)

                    def body(n, b, use):
                        ends = isinstance(n, int)
                        if not (ends and n > last - 2):
                            st.take_rowsT(dve, n + 2, b)
                        if not (ends and n > last - 1):
                            st.take_hidden(dve, n + 1, 1 - b)
                        st.take_hiddenT(dve, n, b)

                    over_blocks(dve, body, 0, E)

                @block.scalar
                def _(act):
                    st.gate(act, 0, 0)

                    def body(n, b, use):
                        if not (isinstance(n, int) and n > last - 1):
                            st.gate(act, n + 1, 1 - b)
                        st.take_result(act, n, b, use)

                    over_blocks(act, body, 0, E)
        c.recycle(0)
        with ExitStack() as run:
            st = ExpertSteps(c, run, "over", a, xn, y, gain, slot_tok, slot_row, 1)
            clear_rows(c, st.rows)
            blocks_out = c.sem("over_blocks_out")

            def each(eng, body):
                count = eng.value_load(ov_count[0:1, 0:1], min_val=0, max_val=OVB)
                with eng.Fori(0, OVB) as j:
                    with eng.If(j < count):
                        body(j)

            with nc.Block() as block:
                @block.sync
                def _(sp):
                    def body(j):
                        e = sp.value_load(ov_expert[0:1, bass.ds(j, 1)], min_val=0, max_val=E - 1)
                        st.load_weights(sp, j, 0, e)
                    each(sp, body)

                @block.gpsimd
                def _(pool):
                    def body(j):
                        st.gather(pool, j, 0, j + E)
                        st.scatter(pool, j, 0, j + E, j)
                        pool.wait_ge(st.scattered[0], 16 * j + 16)
                        pool.sem_inc(blocks_out, 1)
                    each(pool, body)

                @block.tensor
                def _(pe):
                    def body(j):
                        st.turn_rows(pe, j, 0, j)
                        st.up(pe, j, 0, j)
                        st.turn_hidden(pe, j, 0)
                        st.down(pe, j, 0, j)
                    each(pe, body)

                @block.vector
                def _(dve):
                    def body(j):
                        st.take_rowsT(dve, j, 0)
                        st.take_hidden(dve, j, 0)
                        st.take_hiddenT(dve, j, 0)
                    each(dve, body)

                @block.scalar
                def _(act):
                    def body(j):
                        st.gate(act, j, 0)
                        st.take_result(act, j, 0, j)
                    each(act, body)
        c.recycle(0)
        with ExitStack() as run:
            got = sbuf(run, nc, "moe_got", [P, 2, 2, D])
            arrived = [c.sem(f"moe_got{b}") for b in range(2)]
            added = c.sem("moe_added")
            src = y.rearrange("(m p k) d -> p m k d", p=P, k=2)
            with nc.Block() as block:
                @block.sync
                def _(sp):
                    for m in range(NT):
                        if m >= 2:
                            sp.wait_ge(added, 2 * (m - 1))
                        sp.dma_start(got[:, m % 2], src[:, m]).then_inc(arrived[m % 2], 16)

                @block.vector
                def _(dve):
                    for m in range(NT):
                        dve.wait_ge(arrived[m % 2], 16 * (m // 2 + 1))
                        for k, w in enumerate((w1, w2)):
                            nc.vector.scalar_tensor_tensor(x[:, m], got[:, m % 2, k], w[:, m:m + 1], x[:, m],
                                                           ALU.mult, ALU.add).then_inc(added, 1)
                            dve.wait_ge(added, 2 * m + k + 1)


def clear_rows(c, rows):
    nc = c.nc
    with nc.Block() as block:
        @block.vector
        def _(dve):
            nc.vector.memset(rows[:], 0.0)



def s5_parameters(c, a, tmp, kept, scratch):
    nc = c.nc
    c.recycle()
    t = lambda n, shape, dt=F32: sbuf(tmp, nc, f"s5_{n}", shape, dt)
    Q = PAIRS
    cre, cim, rho, cos8, sin8, bnr, bni = kept
    lr, li, dt = t("lr", [P, Q]), t("li", [P, Q]), t("dt", [P, Q])
    br, bi = t("br", [P, Q, SC]), t("bi", [P, Q, SC])
    craw = scratch[:, 4096 - 2 * 4 * P:4096].rearrange("p (i t n) -> p i t n", i=2, t=4)
    loads = []
    for two in range(2):
        h = slice(two * SN, (two + 1) * SN)
        loads += [(lr[h], a["lam_re_2"][0, two::2].rearrange("q n -> n q")),
                  (li[h], a["lam_im_2"][0, two::2].rearrange("q n -> n q")),
                  (dt[h], a["log_dt_2"][0, two::2].unsqueeze(0).to_broadcast([SN, Q])),
                  (br[h], a["ssm_b_re_2"][0, two::2].rearrange("q n c -> n q c")),
                  (bi[h], a["ssm_b_im_2"][0, two::2].rearrange("q n c -> n q c"))]
        for i, n in enumerate(("ssm_c_re_2", "ssm_c_im_2")):
            loads.append((craw[:, i, :, h], a[n][0].rearrange("g c n -> (g c) n").rearrange(
                "(t p) n -> p t n", p=P)))
    load(c, loads)
    cn = t("cn", [P, 2, Q, SC])
    items = [[craw[:, i, j] for j in range(4)] for i in range(2)]

    def split(n, ps, copy):
        v = ps.rearrange("p (q two c) -> p q two c", two=2, c=SC)
        copy(cn[0:SN, n], v[0:SN, :, 0])
        return copy(cn[SN:P, n], v[SN:P, :, 1])

    turn(c, "s5_cturn", items, split)
    ang, size, root, tq = t("ang", [P, Q]), t("size", [P, Q]), t("root", [P, Q]), t("tq", [P, Q])
    sn, cs = t("sin", [P, Q]), t("cos", [P, Q])
    with nc.Block() as block:
        @block.scalar
        def _(act):
            nc.scalar.activation(dt[:], dt[:], ACT.Exp)
    with nc.Block() as block:
        @block.vector
        def _(dve):
            do = c.chain("vector", dve)
            do(nc.vector.tensor_tensor(size[:], lr[:], dt[:], ALU.mult))
            do(nc.vector.tensor_tensor(ang[:], li[:], dt[:], ALU.mult))
            reduce_angle(nc, do, ang[:], tq[:])
            do(nc.vector.tensor_scalar(tq[:], ang[:], -1.0, None, ALU.mult))
            do(nc.vector.tensor_tensor(tq[:], tq[:], ang[:], ALU.min))
            do(nc.vector.tensor_scalar(tq[:], tq[:], math.pi / 2, None, ALU.add))
    with nc.Block() as block:
        @block.scalar
        def _(act):
            nc.scalar.activation(rho[:], size[:], ACT.Exp, scale=float(SJ))
            nc.scalar.activation(root[:], size[:], ACT.Exp)
            nc.scalar.activation(sn[:], ang[:], ACT.Sin)
            nc.scalar.activation(cs[:], tq[:], ACT.Sin)
    pr, pi = t("pr", [P, SJ + 1, Q]), t("pi", [P, SJ + 1, Q])
    er, den, qr, qi = [t(n, [P, Q]) for n in ("er", "den", "qr", "qi")]
    bbr, bbi = t("bbr", [P, Q, SC]), t("bbi", [P, Q, SC])
    tmp4 = scratch[:, 0:Q * (SJ + 1) * SC]
    with nc.Block() as block:
        @block.vector
        def _(dve):
            do = c.chain("vector", dve)
            tt = lambda o, l, r, op: do(nc.vector.tensor_tensor(o, l, r, op))

            def product(o_re, o_im, l, r, t, im_sign=1):
                tt(o_re, l[0], r[0], ALU.mult)
                tt(t, l[1], r[1], ALU.mult)
                tt(o_re, o_re, t, ALU.subtract)
                tt(o_im, l[0], r[1], ALU.mult)
                tt(t, l[1], r[0], ALU.mult)
                tt(o_im, o_im, t, ALU.add)
                if im_sign < 0:
                    do(nc.vector.tensor_scalar(o_im, o_im, -1.0, None, ALU.mult))

            do(nc.vector.memset(pr[:, 0], 1.0))
            do(nc.vector.memset(pi[:, 0], 0.0))
            tt(pr[:, 1], root[:], cs[:], ALU.mult)
            tt(pi[:, 1], root[:], sn[:], ALU.mult)
            done = 1
            while done < SJ:
                lhs = (pr[:, 1:done + 1], pi[:, 1:done + 1])
                rhs = tuple(p[:, done:done + 1].to_broadcast([P, done, Q]) for p in (pr, pi))
                t3 = tmp4[:, :done * Q].rearrange("p (j q) -> p j q", q=Q)
                product(pr[:, done + 1:2 * done + 1], pi[:, done + 1:2 * done + 1], lhs, rhs, t3)
                done *= 2
            cur = (cs[:], sn[:])
            for n, o in enumerate(((qr[:], qi[:]), (er[:], den[:]), (cos8[:], sin8[:]))):
                product(o[0], o[1], cur, cur, tq[:])
                cur = o
            tt(den[:], lr[:], lr[:], ALU.mult)
            tt(tq[:], li[:], li[:], ALU.mult)
            tt(den[:], den[:], tq[:], ALU.add)
            do(nc.vector.reciprocal(den[:], den[:]))
            do(nc.vector.tensor_scalar(er[:], pr[:, 1], -1.0, None, ALU.add))
            tt(qr[:], er[:], lr[:], ALU.mult)
            tt(tq[:], pi[:, 1], li[:], ALU.mult)
            tt(qr[:], qr[:], tq[:], ALU.add)
            tt(qr[:], qr[:], den[:], ALU.mult)
            tt(qi[:], pi[:, 1], lr[:], ALU.mult)
            tt(tq[:], er[:], li[:], ALU.mult)
            tt(qi[:], qi[:], tq[:], ALU.subtract)
            tt(qi[:], qi[:], den[:], ALU.mult)
            wide = lambda v: v.unsqueeze(2).to_broadcast([P, Q, SC])
            product(bbr[:], bbi[:], (wide(qr[:]), wide(qi[:])), (br[:], bi[:]),
                    tmp4[:, :Q * SC].rearrange("p (q c) -> p q c", c=SC))
            for j in range(SJ):
                power = tuple(wide(p[:, SJ - 1 - j]) for p in (pr, pi))
                product(bnr[:, :, j], bni[:, :, j], power, (bbr[:], bbi[:]),
                        tmp4[:, :Q * SC].rearrange("p (q c) -> p q c", c=SC))
            for j in range(SJ + 1):
                power = tuple(wide(p[:, j]) for p in (pr, pi))
                product(cre[:, :, j], cim[:, :, j], power, (cn[:, 0], cn[:, 1]),
                        tmp4[:, :Q * SC].rearrange("p (q c) -> p q c", c=SC), im_sign=-1)
    return bbr, bbi


def s5(c, a, u, y):
    nc = c.nc
    Q = PAIRS
    with ExitStack() as keep:
        k = lambda n, shape, dt=F32: sbuf(keep, nc, f"s5_{n}", shape, dt)
        cre, cim = k("cre", [P, Q, SJ + 1, SC]), k("cim", [P, Q, SJ + 1, SC])
        rho, cos8, sin8 = k("rho", [P, Q]), k("cos8", [P, Q]), k("sin8", [P, Q])
        bnr, bni = k("bnr", [P, Q, SJ, SC]), k("bni", [P, Q, SJ, SC])
        wre, wim = [b[:].rearrange("p q j c -> p q (j c)") for b in (bnr, bni)]
        with ExitStack() as mid:
            bTr, bTi = [sbuf(mid, nc, f"s5_bT{n}", [P, Q, P]) for n in "ri"]
            toe = sbuf(mid, nc, "s5_toe", [P, SG, SJ * SC])
            dskip = sbuf(mid, nc, "s5_dskip", [P, SG, SC])
            tmp = ExitStack()
            bbr, bbi = s5_parameters(c, a, tmp, (cre, cim, rho, cos8, sin8, bnr, bni),
                                     toe[:].rearrange("p g n -> p (g n)"))
            items = [[src[:, 4 * i + j].rearrange("p j c -> p (j c)") for j in range(4)]
                     for src in (bnr, bni) for i in range(4)]
            turn(c, "s5_bturn", items, lambda n, ps, copy: copy(
                (bTr, bTi)[n // 4][:, 4 * (n % 4):4 * (n % 4) + 4], ps.rearrange("p (q s) -> p q s", s=P)))
            resp = y[0:SC].rearrange("p j g c -> p (j g c)").rearrange("p (g n) -> p g n", g=SG)
            with ExitStack() as pctx:
                ps = psum(pctx, nc, "s5_resp_ps", 8)
                with nc.Block() as block:
                    @block.tensor
                    def _(pe):
                        for g in range(SG):
                            q, h = g // 2, slice((g % 2) * SN, (g % 2 + 1) * SN)
                            o = ps[0:SC, 4 * (g % 2) + q // 4, (q % 4) * P:(q % 4 + 1) * P]
                            rows = lambda t: t[h, q, 0:SJ].rearrange("p j c -> p (j c)")
                            nc.tensor.matmul(o, bbr[h, q], rows(cre), start=True, stop=False)
                            nc.tensor.matmul(o, bbi[h, q], rows(cim), start=False, stop=True)

                    @block.vector
                    def _(dve):
                        nc.vector.memset(toe[:], 0.0)
                with nc.Block() as block:
                    @block.vector
                    def _(dve):
                        for b in range(8):
                            first = 8 * (b % 4) + b // 4
                            nc.vector.tensor_copy(resp[:, first:first + 7:2],
                                                  ps[0:SC, b].rearrange("p (g n) -> p g n", g=4))
            load(c, [(toe[j * SC:(j + 1) * SC, :, j * SC:], resp[:, :, 0:(SJ - j) * SC]) for j in range(SJ)]
                 + [(dskip[:], a["ssm_d_2"][0].rearrange("(g c) -> g c", c=SC).unsqueeze(0).to_broadcast(
                     [P, SG, SC]))])
            tmp.close()
            uT = y.rearrange("p j g c -> p (j g c)").rearrange("p (g m) -> p g m", g=SG)
            items = [[u[:, 4 * i + j].rearrange("p j c -> p (j c)") for j in range(4)] for i in range(SG // 4)]
            turn(c, "s5_uturn", items, lambda n, ps, copy: copy(
                uT[:, 4 * n:4 * n + 4], ps.rearrange("p (g m) -> p g m", m=SM)))
            with ExitStack() as pctx:
                ps = psum(pctx, nc, "s5_w_ps", 8)
                with nc.Block() as block:
                    @block.tensor
                    def _(pe):
                        for g in range(SG):
                            q, h = g // 2, slice((g % 2) * SN, (g % 2 + 1) * SN)
                            for i, bT in enumerate((bTr, bTi)):
                                nc.tensor.matmul(ps[h, 4 * i + q // 4, (q % 4) * SM:(q % 4 + 1) * SM],
                                                 bT[:, q, h], uT[:, g], start=True, stop=True)
                with nc.Block() as block:
                    @block.vector
                    def _(dve):
                        nc.vector.tensor_copy(wre.rearrange("p (b q) m -> p b (q m)", b=4), ps[:, 0:4])
                        nc.vector.tensor_tensor(
                            u, u, dskip[:].unsqueeze(2).to_broadcast([P, SG, SJ, SC]), ALU.mult)

                    @block.scalar
                    def _(act):
                        nc.scalar.activation(wim.rearrange("p (b q) m -> p b (q m)", b=4), ps[:, 4:8], ACT.Copy)
                with nc.Block() as block:
                    @block.tensor
                    def _(pe):
                        for g in range(SG):
                            nc.tensor.matmul(ps[:, g // 4, (g % 4) * P:(g % 4 + 1) * P], uT[:, g], toe[:, g],
                                             start=True, stop=True)
                with nc.Block() as block:
                    @block.vector
                    def _(dve):
                        flat = u.rearrange("p (b g) j c -> p b (g j c)", b=8)
                        nc.vector.tensor_tensor(flat, ps[:], flat, ALU.add)
        s = lambda n, shape: sbuf(keep, nc, f"s5_{n}", shape)
        ct, st = s("ct", [P, Q, SM]), s("st", [P, Q, SM])
        both = y.rearrange("p j g c -> p (j g c)").rearrange("p (i q m) -> p i q m", i=2, q=Q)
        tr, ti = both[:, 0], both[:, 1]
        sre, sim = s("sre", [P, Q, SM + 1]), s("sim", [P, Q, SM + 1])
        with nc.Block() as block:
            @block.vector
            def _(dve):
                do = c.chain("vector", dve)
                tt = lambda o, l, r, op: do(nc.vector.tensor_tensor(o, l, r, op))
                do(nc.vector.memset(ct[:, :, 0:1], 1.0))
                do(nc.vector.memset(st[:, :, 0:1], 0.0))
                n = 1
                while n < SM:
                    cw, sw = [v[:].unsqueeze(2).to_broadcast([P, Q, n]) for v in (cos8, sin8)]
                    tt(tr[:, :, :n], ct[:, :, :n], cw, ALU.mult)
                    tt(ti[:, :, :n], st[:, :, :n], sw, ALU.mult)
                    tt(ct[:, :, n:2 * n], tr[:, :, :n], ti[:, :, :n], ALU.subtract)
                    tt(tr[:, :, :n], ct[:, :, :n], sw, ALU.mult)
                    tt(ti[:, :, :n], st[:, :, :n], cw, ALU.mult)
                    tt(st[:, :, n:2 * n], tr[:, :, :n], ti[:, :, :n], ALU.add)
                    tt(tr[:, :, 0], cos8[:], cos8[:], ALU.mult)
                    tt(ti[:, :, 0], sin8[:], sin8[:], ALU.mult)
                    tt(sin8[:], cos8[:], sin8[:], ALU.mult)
                    do(nc.vector.tensor_scalar(sin8[:], sin8[:], 2.0, None, ALU.mult))
                    tt(cos8[:], tr[:, :, 0], ti[:, :, 0], ALU.subtract)
                    n *= 2
                tt(tr, wre, ct[:], ALU.mult)
                tt(ti, wim, st[:], ALU.mult)
                tt(tr, tr, ti, ALU.add)
                tt(ti, wim, ct[:], ALU.mult)
                tt(wre, wre, st[:], ALU.mult)
                tt(ti, ti, wre, ALU.subtract)
                do(nc.vector.memset(sre[:, :, 0:SM], 1.0))
                tt(wim, sre[:, :, 0:SM], rho[:].unsqueeze(2).to_broadcast([P, Q, SM]), ALU.mult)
                do(nc.vector.memset(wim[:, :, 0:1], 0.0))
                flat = lambda t: t.rearrange("p q m -> p (q m)")
                do(nc.vector.tensor_tensor_scan(flat(wre), flat(wim), flat(tr), 0.0, ALU.mult, ALU.add))
                do(nc.vector.tensor_tensor_scan(flat(tr), flat(wim), flat(ti), 0.0, ALU.mult, ALU.add))
                do(nc.vector.memset(sre[:, :, 0:1], 0.0))
                do(nc.vector.memset(sim[:, :, 0:1], 0.0))
                tt(ti, wre, ct[:], ALU.mult)
                tt(wim, tr, st[:], ALU.mult)
                tt(sre[:, :, 1:], ti, wim, ALU.subtract)
                tt(ti, wre, st[:], ALU.mult)
                tt(wim, tr, ct[:], ALU.mult)
                tt(sim[:, :, 1:], ti, wim, ALU.add)
        with ExitStack() as pctx:
            ps = psum(pctx, nc, "s5_y_ps", 8)
            with nc.Block() as block:
                @block.tensor
                def _(pe):
                    for g in range(SG):
                        q, h = g // 2, slice((g % 2) * SN, (g % 2 + 1) * SN)
                        o = ps[:, 4 * (g % 2) + q // 4, (q % 4) * P:(q % 4 + 1) * P]
                        rows = lambda t: t[h, q, 1:SJ + 1].rearrange("p j c -> p (j c)")
                        nc.tensor.matmul(o, sre[h, q, 0:SM], rows(cre), start=True, stop=False)
                        nc.tensor.matmul(o, sim[h, q, 0:SM], rows(cim), start=False, stop=True)
            with nc.Block() as block:
                @block.vector
                def _(dve):
                    for b in range(8):
                        first = 8 * (b % 4) + b // 4
                        gs = slice(first, first + 7, 2)
                        nc.vector.tensor_tensor(
                            y[:, :, gs].rearrange("p j g c -> p g j c"),
                            ps[:, b].rearrange("p (g j c) -> p g j c", g=4, j=SJ), u[:, gs], ALU.add)


def channels_project(c, name, w, srcT, evacuate, engine, nk=KD, wbuf=None):
    nc = c.nc
    with ExitStack() as ctx:
        wbuf = sbuf(ctx, nc, f"{name}_w", [P, 2, nk, CH])
        n = w.shape[-1] // CH
        w = w.rearrange("(k p) n -> p k n", p=P)
        project(c, name, wbuf, [w[:, :, i * CH:(i + 1) * CH] for i in range(n)],
                lambda i, b, k, w: w[:, k, (b // 2) * P:(b // 2 + 1) * P],
                lambda i, b, k, w: srcT[:, k, (b % 2) * CH:(b % 2 + 1) * CH],
                lambda i, b, ps: evacuate(4 * i + b // 2, slice((b % 2) * CH, (b % 2 + 1) * CH), ps),
                engine, nk=nk)


def mix_second(c, a, x):
    nc = c.nc
    SW = SG * SC
    w_in = a["w_in_2"][0]
    part = lambda i: w_in[:, SW + i * D:SW + (i + 1) * D]
    with ExitStack() as ctx:
        s = lambda n, shape, dt=F32: sbuf(ctx, nc, n, shape, dt)
        t1, t2 = s("m2_t1", [P, KD, T]), s("m2_t2", [P, KD, T])
        u = s("m2_u", [P, SG, SJ, SC])
        with ExitStack() as early:
            s = lambda n, shape, dt=F32: sbuf(early, nc, n, shape, dt)
            gain, bias = s("m2_gain", [P, KD]), s("m2_bias", [P, 5, KD])
            cw, cb = s("m2_cw", [P, 3, KD]), s("m2_cb", [P, KD])
            ubias = s("m2_ubias", [P, SG, SC])
            hT = s("m2_hT", [P, KD, T])
            load(c, [(gain[:], a["norm_mix_g_2"][0].rearrange("(k p) -> p k", p=P)),
                     (cb[:], a["conv_b_2"][0].rearrange("(k p) -> p k", p=P)),
                     (ubias[:].rearrange("p g c -> p (g c)"), a["b_in_2"][0, 0:SW].unsqueeze(0).to_broadcast([P, SW]))]
                 + [(bias[:, i], a["b_in_2"][0, SW + i * D:SW + (i + 1) * D].rearrange("(k p) -> p k", p=P))
                    for i in range(5)]
                 + [(cw[:, i], a["conv_w_2"][0, i].rearrange("(k p) -> p k", p=P)) for i in range(3)])
            norm_transpose(c, "m2_norm", x, hT, gain, NT)
            v = nc.vector
            add_in = lambda i, dst: lambda ch, t, ps: v.tensor_scalar(
                dst[:, ch, t], ps, bias[:, i, ch:ch + 1], None, ALU.add)
            times_in = lambda i, dst: lambda ch, t, ps: v.scalar_tensor_tensor(
                dst[:, ch, t], ps, bias[:, i, ch:ch + 1], dst[:, ch, t], ALU.add, ALU.mult)
            gate_in = lambda i, dst: lambda ch, t, ps: nc.scalar.activation(
                dst[:, ch, t], ps, ACT.Sigmoid, bias=bias[:, i, ch:ch + 1])
            channels_project(c, "m2_c", part(1), hT, add_in(1, t1), "vector")
            channels_project(c, "m2_v", part(2), hT, times_in(2, t1), "vector")
            with nc.Block() as block:
                @block.vector
                def _(dve):
                    do = c.chain("vector", dve)
                    for k in range(KD):
                        do(v.tensor_scalar(t2[:, k], t1[:, k], cw[:, 2, k:k + 1], cb[:, k:k + 1], ALU.mult, ALU.add))
                        for lag in (1, 2):
                            do(v.scalar_tensor_tensor(t2[:, k, lag:], t1[:, k, :T - lag], cw[:, 2 - lag, k:k + 1],
                                                      t2[:, k, lag:], ALU.mult, ALU.add))
            channels_project(c, "m2_b", part(0), hT, times_in(0, t2), "vector")
            channels_project(c, "m2_gc", part(4), hT, gate_in(4, t1), "scalar")
            channels_project(c, "m2_co", a["w_conv_out_2"][0], t2, lambda ch, t, ps: v.tensor_tensor(
                t1[:, ch, t], ps, t1[:, ch, t], ALU.mult), "vector")
            channels_project(c, "m2_gs", part(3), hT, gate_in(3, t2), "scalar")
            with ExitStack() as w_:
                wbuf = sbuf(w_, nc, "m2_wu", [P, 1, KD, SW])
                project(c, "m2_u", wbuf, [w_in[:, 0:SW].rearrange("(k p) n -> p k n", p=P)],
                        lambda i, b, k, w: hT[:, k, b::SJ], lambda i, b, k, w: w[:, k],
                        lambda i, b, ps: v.tensor_tensor(u[:, :, b], ps.rearrange("p (g c) -> p g c", c=SC),
                                                         ubias[:], ALU.add), "vector")
        with ExitStack() as late:
            zT = sbuf(late, nc, "m2_zT", [P, SW // P, T])
            y = zT[:].rearrange("p k t -> p (k t)").rearrange("p (j g c) -> p j g c", j=SJ, c=SC)
            s5(c, a, u[:], y)
            z = u[:].rearrange("p g j c -> p (g j c)")
            with nc.Block() as block:
                @block.scalar
                def _(act):
                    nc.scalar.activation(z, y.rearrange("p j g c -> p (j g c)"), ACT.Gelu_apprx_tanh)
            z = z.rearrange("p (j n) -> p j n", j=SJ)
            items = [[z[:, j, k * P:(k + 1) * P] for k in range(4)] for j in range(SJ)]
            turn(c, "m2_zturn", items, lambda n, ps, copy: copy(
                zT[:, :, n::SJ], ps.rearrange("p (k m) -> p k m", m=P)))
            glu = sbuf(late, nc, "m2_glu", [P, KD, T])
            channels_project(c, "m2_gb", a["w_glu_b_2"][0], zT, lambda ch, t, ps: nc.scalar.activation(
                glu[:, ch, t], ps, ACT.Sigmoid), "scalar", nk=SW // P)
            channels_project(c, "m2_ga", a["w_glu_a_2"][0], zT, lambda ch, t, ps: nc.vector.tensor_tensor(
                glu[:, ch, t], ps, glu[:, ch, t], ALU.mult), "vector", nk=SW // P)
            with nc.Block() as block:
                @block.vector
                def _(dve):
                    do = c.chain("vector", dve)
                    do(nc.vector.tensor_tensor(glu[:], glu[:], t2[:], ALU.mult))
                    do(nc.vector.tensor_tensor(t1[:], t1[:], glu[:], ALU.add))
        out_project(c, "m2_out", t1, a["w_out_2"][0], x)


def mlp_second(c, a, x):
    nc = c.nc
    with ExitStack() as ctx:
        s = lambda n, shape, dt=F32: sbuf(ctx, nc, n, shape, dt)
        gain, hT, hid = s("mlp_gain", [P, KD]), s("mlp_hT", [P, KD, T]), s("mlp_hid", [P, KD, T])
        load(c, [(gain[:], a["norm_mlp_g_2"][0].rearrange("(k p) -> p k", p=P))])
        norm_transpose(c, "mlp_norm", x, hT, gain, NT)
        do = c.chain("scalar", nc.scalar)

        def relu_squared(ch, t, ps):
            do(nc.scalar.activation(hid[:, ch, t], ps, ACT.Relu))
            return nc.scalar.activation(hid[:, ch, t], hid[:, ch, t], ACT.Square)

        for f in range(DFF // D):
            channels_project(c, f"mlp_up{f}", a["w_ff1_2"][0, :, f * D:(f + 1) * D], hT, relu_squared, "scalar")
            out_project(c, f"mlp_down{f}", hid, a["w_ff2_2"][0, f * D:(f + 1) * D, :], x)


def final_norm(c, a, x):
    nc = c.nc
    with ExitStack() as ctx:
        s = lambda n, shape, dt=F32: sbuf(ctx, nc, n, shape, dt)
        gain, sq, ssq = s("fin_gain", [P, 1, D]), s("fin_sq", [P, NT, D]), s("fin_ssq", [P, NT])
        load(c, [(gain[:, 0], a["norm_final_g_2"].unsqueeze(0).to_broadcast([P, D]))])
        group_norm(c, "fin", x[:], sq[:], ssq[:], D, gain[:])


INS = ['x', 'mem', 'positions', 'norm_mix', 'w_in', 'mla_q_a_norm', 'mla_w_q_up', 'mla_kv_a_norm', 'mla_w_kv_up',
       'mla_q_norm', 'mla_k_norm', 'hg_lb_logits', 'hg_o_norm', 'w_out', 'norm_cross', 'norm_mem', 'x_w_q',
       'x_w_kv', 'x_q_norm', 'x_k_norm', 'x_w_o', 'norm_ffn', 'moe_w_group', 'moe_b_group', 'moe_w_expert',
       'moe_b_expert', 'moe_w_gate', 'moe_w_up', 'moe_w_down', 'norm_mix_g_2', 'w_in_2', 'b_in_2', 'lam_re_2',
       'lam_im_2', 'log_dt_2', 'ssm_b_re_2', 'ssm_b_im_2', 'ssm_c_re_2', 'ssm_c_im_2', 'ssm_d_2', 'w_glu_a_2',
       'w_glu_b_2', 'conv_w_2', 'conv_b_2', 'w_conv_out_2', 'w_out_2', 'norm_mlp_g_2', 'w_ff1_2', 'w_ff2_2',
       'norm_final_g_2']


def program(nc, a, out, stages=("mix", "cross", "moe", "mix2", "mlp", "final")):
    with ExitStack() as ctx:
        c = Core(nc, ctx)
        done = ctx.enter_context(nc.semaphore("result_stored"))
        x = sbuf(ctx, nc, "x", [P, NT, D])
        make_constants(c)
        load(c, [(x[:], a["x"][0].rearrange("(m p) d -> p m d", p=P))])
        for st in stages:
            STAGES[st](c, a, x)
        with nc.Block() as block:
            @block.sync
            def _(sp):
                sp.dma_start(out[0].rearrange("(m p) d -> p m d", p=P), x[:]).then_inc(done, 16)
                sp.wait_ge(done, 16)


STAGES = {"mix": mix_first, "cross": cross_first, "moe": moe_first, "mix2": mix_second,
          "mlp": mlp_second, "final": final_norm}


def kernel(**inputs):
    import numpy as _np
    import concourse.bacc as _bacc
    from concourse import mybir as _mybir
    from concourse.bass_utils import run_bass_kernel_spmd as _run

    nc = _bacc.Bacc("TRN2", target_bir_lowering=False, num_devices=1)
    arrays, a = {}, {}
    for name in INS:
        v = _np.ascontiguousarray(inputs[name])
        arrays[f"in_{name}_dram"] = v
        a[name] = nc.dram_tensor(f"in_{name}_dram", v.shape, _mybir.dt.from_np(v.dtype), kind="ExternalInput").ap()
    out = nc.dram_tensor("out_0_dram", (1, T, D), F32, kind="ExternalOutput").ap()
    program(nc, a, out)
    r = _run(nc, [arrays], core_ids=[0])
    return r.results[0]["out_0_dram"]
```

```python
import math
from contextlib import ExitStack

import numpy as np

import concourse.bass as bass
from concourse import mybir

P = 128
F32 = mybir.dt.float32
F32R = mybir.dt.float32r
I32 = mybir.dt.int32
ALU = mybir.AluOpType
ACT = mybir.ActivationFunctionType
AX = mybir.AxisListType.X

T = 1024
NT = T // P
D = 1024
KD = D // P
EPS = 1e-6
CH = 512

MH, NOPE, ROPE, VD = 8, 64, 32, 64
QK = NOPE + ROPE
QR, KVR = 192, 128
HALF = ROPE // 2
ROPE_BASE = 10000.0
HH, HK = 4, 128
PAIR_BUFS = 3
LEVELS = 7
MEM = 256
XH, XD = 4, 256
G, PG, E, EH = 8, 8, 64, 256
CAP = 64
PAIRED = E * CAP // P
OVB = 31
NBLK = PAIRED + OVB
SG, SC, SN = 32, 16, 64
SJ = 8
SM = T // SJ
PAIRS = SG // 2
DFF = 4096
TWO_PI = 2 * math.pi
PI_A = 6.28125
PI_B = math.floor((TWO_PI - PI_A) * 2 ** 20) / 2 ** 20
PI_C = TWO_PI - PI_A - PI_B
ROUND = 1.5 * 2 ** 23


class Chain:

    def __init__(self, eng, sem, tally):
        self.eng, self.sem, self.tally = eng, sem, tally

    def __call__(self, ins):
        self.tally[0] += 1
        ins.then_inc(self.sem, 1)
        self.eng.wait_ge(self.sem, self.tally[0])


class Core:

    def __init__(self, nc, ctx):
        self.nc, self.ctx, self.n, self.live = nc, ctx, 0, []
        self.own = {}
        for e in ("vector", "scalar", "gpsimd", "tensor"):
            self.own[e] = (ctx.enter_context(nc.semaphore(f"{e}_step")), [0])
        self.arrived = [ctx.enter_context(nc.semaphore(f"weights{b}_arrived")) for b in range(2)]
        self.arrivals = [0, 0]

    def chain(self, name, eng):
        sem, tally = self.own[name]
        return Chain(eng, sem, tally)

    def sem(self, name):
        self.n += 1
        self.live.append(self.nc.alloc_semaphore(f"{name}_{self.n}"))
        return self.live[-1]

    def hold_sem(self, name):
        return self.ctx.enter_context(self.nc.semaphore(name))

    def recycle(self, most=60):
        if len(self.live) > most:
            with self.nc.Block() as block:
                @block.gpsimd
                def _(pool):
                    self.nc.clear_and_free_semaphores(self.live)
            self.live = []


def sbuf(ctx, nc, name, shape, dt=F32):
    return ctx.enter_context(nc.sbuf_tensor(name, shape, dt))


def twins(ctx, nc, name, other, shape):
    tensor = sbuf(ctx, nc, name, shape)
    return tensor, nc.alloc_sbuf_tensor_at(other, shape, F32, offset=nc.sbuf_base - 4 * math.prod(shape[1:]))


def psum(ctx, nc, name, banks):
    return ctx.enter_context(nc.psum_tensor(name, [P, banks, CH], F32))



def make_constants(c):
    nc = c.nc
    s = lambda n, shape, dt=F32: sbuf(c.ctx, nc, n, shape, dt)
    c.ident = s("ident", [P, P])
    c.ones = s("ones", [P, P])
    c.before = s("before", [P, P])
    c.row = s("row", [P, P])
    c.col = s("col", [P, 1])
    c.eps = s("eps", [P, 1])
    with nc.Block() as block:
        @block.gpsimd
        def _(pool):
            do = c.chain("gpsimd", pool)
            do(nc.gpsimd.memset(c.ident[:], 0.0))
            do(nc.gpsimd.memset(c.ones[:], 1.0))
            do(nc.gpsimd.memset(c.eps[:], EPS))
            do(nc.gpsimd.affine_select(out=c.ident[:], in_=c.ident[:], compare_op=ALU.not_equal, fill=1.0,
                                       base=0, pattern=[[-1, P]], channel_multiplier=1))
            do(nc.gpsimd.affine_select(out=c.before[:], in_=c.ones[:], compare_op=ALU.is_gt, fill=0.0,
                                       base=0, pattern=[[1, P]], channel_multiplier=-1))
            do(nc.gpsimd.iota(c.row[:], [[1, P]], base=0, channel_multiplier=0,
                              allow_small_or_imprecise_dtypes=True))
            do(nc.gpsimd.iota(c.col[:], [[0, 1]], base=0, channel_multiplier=1,
                              allow_small_or_imprecise_dtypes=True))


def load(c, pairs):
    nc = c.nc
    c.recycle()
    done = c.sem("loaded")
    with nc.Block() as block:
        @block.sync
        def _(sp):
            for dst, src in pairs:
                with nc.allow_non_contiguous_dma("small parameters"):
                    sp.dma_start(dst, src).then_inc(done, 16)
            sp.wait_ge(done, 16 * len(pairs))



def norm_transpose(c, name, src, dst, gain, tiles, keep=None):
    nc = c.nc
    c.recycle()
    with ExitStack() as ctx:
        junk = sbuf(ctx, nc, f"{name}_junk", [P, D])
        ssq = sbuf(ctx, nc, f"{name}_ssq", [P, tiles])
        rstd = sbuf(ctx, nc, f"{name}_rstd", [P, tiles])
        normed = sbuf(ctx, nc, f"{name}_normed", [P, 2, D])
        ps = psum(ctx, nc, f"{name}_ps", 4)
        squared, scale_ready, row_ready, turned, evacuated = [
            c.sem(f"{name}_{x}") for x in ("squared", "scale_ready", "row_ready", "turned", "evacuated")]
        kept = [c.sem(f"{name}_kept{b}") for b in range(2)]
        with nc.Block() as block:
            @block.scalar
            def _(act):
                do = c.chain("scalar", act)
                for m in range(tiles):
                    do(nc.scalar.activation(junk[:], src[:, m], ACT.Square, accum_out=ssq[:, m:m + 1]))
                do(nc.scalar.activation(rstd[:], ssq[:], ACT.Sqrt, bias=c.eps[:, 0:1], scale=1.0 / D))
                nc.scalar.activation(junk[:, 0:1], ssq[:, 0:1], ACT.Copy).then_inc(squared, 1)
                act.wait_ge(scale_ready, 1)
                for m in range(tiles):
                    if m >= 2:
                        act.wait_ge(turned, m - 1)
                        if keep is not None:
                            act.wait_ge(kept[m % 2], 16 * (m // 2))
                    nc.scalar.activation(normed[:, m % 2], src[:, m], ACT.Copy,
                                         scale=rstd[:, m:m + 1]).then_inc(row_ready, 1)

            @block.vector
            def _(dve):
                dve.wait_ge(squared, 1)
                nc.vector.reciprocal(rstd[:], rstd[:]).then_inc(scale_ready, 1)
                for m in range(tiles):
                    dve.wait_ge(turned, m + 1)
                    b = 2 * (m % 2)
                    nc.vector.tensor_tensor(
                        dst[:, :, m * P:(m + 1) * P],
                        ps[:, b:b + 2, :].rearrange("p b (k t) -> p (b k) t", t=P),
                        gain[:].unsqueeze(2).to_broadcast([P, KD, P]), ALU.mult).then_inc(evacuated, 1)

            @block.tensor
            def _(pe):
                for m in range(tiles):
                    pe.wait_ge(row_ready, m + 1)
                    if m >= 2:
                        pe.wait_ge(evacuated, m - 1)
                    for k in range(KD):
                        ins = nc.tensor.transpose(ps[:, 2 * (m % 2) + k // 4, (k % 4) * P:(k % 4 + 1) * P],
                                                  normed[:, m % 2, k * P:(k + 1) * P], c.ident[:])
                    ins.then_inc(turned, 1)

            if keep is not None:
                @block.sync
                def _(sp):
                    for m in range(tiles):
                        sp.wait_ge(row_ready, m + 1)
                        sp.dma_start(keep[m * P:(m + 1) * P, :], normed[:, m % 2]).then_inc(kept[m % 2], 16)
                    for b in range(2):
                        sp.wait_ge(kept[b], 16 * tiles // 2)


def norm_split(c, name, src, dst, gain, tiles, room=None):
    nc = c.nc
    c.recycle()
    high, low = dst
    with ExitStack() as ctx:
        ssq = sbuf(ctx, nc, f"{name}_ssq", [P, tiles])
        if room is None:
            room = sbuf(ctx, nc, f"{name}_room", [P, 3 * D])[:]
        junk, normed = room[:, 2 * D:3 * D], room[:, 0:2 * D].rearrange("p (b d) -> p b d", b=2)
        ps = psum(ctx, nc, f"{name}_ps", 8)
        squared, row_ready, turned, high_ready, evacuated = [
            c.sem(f"{name}_{x}") for x in ("squared", "row_ready", "turned", "high_ready", "evacuated")]
        sums = lambda m: ps[:, 2 * (m % 4):2 * (m % 4) + 2, :].rearrange("p b (k t) -> p (b k) t", t=P)
        with nc.Block() as block:
            @block.scalar
            def _(act):
                do = c.chain("scalar", act)
                for m in range(tiles):
                    ins = nc.scalar.activation(junk, src[:, m], ACT.Square, accum_out=ssq[:, m:m + 1])
                    do(ins)
                nc.scalar.activation(ssq[:], ssq[:], ACT.Sqrt, bias=c.eps[:, 0:1], scale=1.0 / D).then_inc(squared, 1)
                for m in range(tiles):
                    act.wait_ge(turned, m + 1)
                    nc.scalar.activation(high[:, :, m * P:(m + 1) * P].bitcast(F32R), sums(m),
                                         ACT.Copy).then_inc(high_ready, 1)

            @block.vector
            def _(dve):
                def scale(m):
                    if m >= 2:
                        dve.wait_ge(turned, m - 1)
                    nc.vector.scalar_tensor_tensor(normed[:, m % 2], src[:, m], ssq[:, m:m + 1], gain,
                                                   ALU.mult, ALU.mult).then_inc(row_ready, 1)

                do = c.chain("vector", dve)
                dve.wait_ge(squared, 1)
                do(nc.vector.reciprocal(ssq[:], ssq[:]))
                scale(0)
                for m in range(tiles):
                    if m + 1 < tiles:
                        scale(m + 1)
                    dve.wait_ge(high_ready, m + 1)
                    at = (slice(None), slice(None), slice(m * P, (m + 1) * P))
                    nc.vector.tensor_tensor(low[at].bitcast(F32R), sums(m), high[at],
                                            ALU.subtract).then_inc(evacuated, 1)

            @block.tensor
            def _(pe):
                for m in range(tiles):
                    pe.wait_ge(row_ready, m + 1)
                    if m >= 4:
                        pe.wait_ge(evacuated, m - 3)
                    for k in range(KD):
                        ins = nc.tensor.transpose(ps[:, 2 * (m % 4) + k // 4, (k % 4) * P:(k % 4 + 1) * P],
                                                  normed[:, m % 2, k * P:(k + 1) * P], c.ident[:])
                    ins.then_inc(turned, 1)


class Job:

    def __init__(self, w, rows, src, evacuate, engine, tokens=None, then=None, finish=None, after=0):
        self.w, self.rows, self.evacuate, self.engine, self.then = w, rows, evacuate, engine, then
        self.src, self.nk, self.finish, self.after = src, w.shape[1], finish, after
        self.tokens = tokens or (lambda b: slice(b * P, (b + 1) * P))


class Stream:

    def __init__(self, c, ctx, name, kp=2, cuts=2):
        self.c, self.kp, self.cuts, self.started = c, kp, cuts, 0
        self.raw = sbuf(ctx, c.nc, f"{name}_raw", [P, 2, kp, CH])
        self.cut = sbuf(ctx, c.nc, f"{name}_cut", [P, cuts, 2, kp, CH])

    def load(self, sp, s, w):
        sp.dma_start(self.raw[:, s % 2, :, :w.shape[-1]], w).then_inc(self.c.arrived[s % 2], 16)

    def pieces(self, jobs):
        return [(i, k, j.w[:, k:k + self.kp]) for i, j in enumerate(jobs) for k in range(0, j.nk, self.kp)]

    def start(self, jobs):
        with self.c.nc.Block() as block:
            @block.sync
            def _(sp):
                for s, (_, _, w) in enumerate(self.pieces(jobs)[:2]):
                    self.load(sp, s, w)
        self.started = 2


def project(c, name, stream, jobs, banks=8, source=None):
    nc = c.nc
    c.recycle()
    pieces, kp, cuts = stream.pieces(jobs), stream.kp, stream.cuts
    n, started, before = len(pieces), stream.started, list(c.arrivals)
    stream.started = 0
    for s in range(n):
        c.arrivals[s % 2] += 1
    with ExitStack() as ctx:
        ps = psum(ctx, nc, f"{name}_ps", 8)
        high_ready, low_ready, products = [c.sem(f"{name}_{x}") for x in ("high_ready", "low_ready", "products")]
        emptied = {e: c.sem(f"{name}_{e}_emptied") for e in ("scalar", "vector")}
        source_high, source_low = c.sem(f"{name}_source_high"), c.sem(f"{name}_source_low")
        finished = c.sem(f"{name}_finished")
        order = [sum(j.engine == job.engine for j in jobs[:i]) for i, job in enumerate(jobs)]

        def part(s, which):
            return stream.cut[:, s % cuts, which, :, :pieces[s][2].shape[-1]]

        def raw(s):
            return stream.raw[:, s % 2, :, :pieces[s][2].shape[-1]]

        def make_high(act, s):
            act.wait_ge(c.arrived[s % 2], 16 * (before[s % 2] + s // 2 + 1))
            if s >= cuts:
                act.wait_ge(products, banks * (s - cuts + 1))
            nc.scalar.activation(part(s, 0).bitcast(F32R), raw(s), ACT.Copy).then_inc(high_ready, 1)

        def make_low(dve, s):
            dve.wait_ge(high_ready, s + 1)
            nc.vector.tensor_tensor(part(s, 1).bitcast(F32R), raw(s), part(s, 0),
                                    ALU.subtract).then_inc(low_ready, 1)

        def cut_source(eng, m):
            at = (slice(None), slice(None), slice(m * P, (m + 1) * P))
            high, low = [t[at] for t in jobs[0].src]
            if eng == "scalar":
                nc.scalar.activation(high.bitcast(F32R), source[at], ACT.Copy).then_inc(source_high, 1)
            else:
                nc.vector.wait_ge(source_high, m + 1)
                nc.vector.tensor_tensor(low.bitcast(F32R), source[at], high, ALU.subtract).then_inc(source_low, 1)

        def serve(eng, make, mine):
            make(eng, 0)
            if source is not None:
                for m in range(NT):
                    cut_source(mine, m)
            for s in range(1, min(cuts, n)):
                make(eng, s)
            for s, (i, k, _) in enumerate(pieces):
                job, last = jobs[i], k + kp == jobs[i].nk
                if last and job.engine == mine:
                    for b in range(banks):
                        eng.wait_ge(products, banks * s + b + 1)
                        job.evacuate(b, ps[:, b]).then_inc(emptied[mine], 1)
                    if job.then:
                        job.then()
                if s + cuts < n:
                    make(eng, s + cuts)
                if last and job.finish and mine == "vector":
                    for b in range(banks):
                        eng.wait_ge(emptied["scalar"], banks * order[i] + b + 1)
                        job.finish(b).then_inc(finished, 1)

        with nc.Block() as block:
            @block.sync
            def _(sp):
                for s in range(started, n):
                    if s >= 2:
                        sp.wait_ge(low_ready, s - 1)
                    stream.load(sp, s, pieces[s][2])

            @block.tensor
            def _(pe):
                for s, (i, first, _) in enumerate(pieces):
                    job = jobs[i]
                    high, low = [t.bitcast(F32R) for t in job.src]
                    if first == 0 and job.after:
                        pe.wait_ge(finished, job.after)
                    pe.wait_ge(low_ready, s + 1)
                    w = [part(s, h).bitcast(F32R) for h in range(2)]
                    for b in range(banks):
                        if i and first == 0:
                            pe.wait_ge(emptied[jobs[i - 1].engine], banks * order[i - 1] + b + 1)
                        if s == 0 and source is not None:
                            pe.wait_ge(source_low, b + 1 if job.rows else NT // 2 if b == 0 else NT)
                        for j in range(kp):
                            k = first + j
                            for sw, wh in ((high, 0), (high, 1), (low, 0)):
                                if job.rows:
                                    l, r = sw[:, k, job.tokens(b)], w[wh][:, j]
                                else:
                                    l = w[wh][:, j, (b // 2) * P:(b // 2 + 1) * P]
                                    r = sw[:, k, (b % 2) * CH:(b % 2 + 1) * CH]
                                ins = nc.tensor.matmul(
                                    ps[:, b, :r.shape[-1]], l, r, start=(k == 0 and sw is high and wh == 0),
                                    stop=(k == job.nk - 1 and sw is low))
                        ins.then_inc(products, 1)

            @block.scalar
            def _(act):
                serve(act, make_high, "scalar")

            @block.vector
            def _(dve):
                serve(dve, make_low, "vector")


def columns(w, i, width=CH):
    return w.rearrange("(k p) n -> p k n", p=P)[:, :, i * width:(i + 1) * width]


def turn_split(c, name, items, parts):
    nc = c.nc
    c.recycle()
    with ExitStack() as ctx:
        ps = psum(ctx, nc, f"{name}_ps", 8)
        turned, high_ready, emptied = [c.sem(f"{name}_{x}") for x in ("turned", "high_ready", "emptied")]
        sums = lambda n: ps[:, n % 8].rearrange("p (k t) -> p k t", t=P)
        with nc.Block() as block:
            @block.tensor
            def _(pe):
                for n, tiles in enumerate(items):
                    if n >= 8:
                        pe.wait_ge(emptied, n - 7)
                    for q, a in enumerate(tiles):
                        ins = nc.tensor.transpose(ps[:, n % 8, q * P:(q + 1) * P], a, c.ident[:])
                    ins.then_inc(turned, 1)

            @block.scalar
            def _(act):
                for n in range(len(items)):
                    act.wait_ge(turned, n + 1)
                    nc.scalar.activation(parts(n)[0].bitcast(F32R), sums(n), ACT.Copy).then_inc(high_ready, 1)

            @block.vector
            def _(dve):
                for n in range(len(items)):
                    dve.wait_ge(high_ready, n + 1)
                    high, low = parts(n)
                    nc.vector.tensor_tensor(low.bitcast(F32R), sums(n), high, ALU.subtract).then_inc(emptied, 1)


def turn(c, name, items, evacuate):
    nc = c.nc
    c.recycle()
    with ExitStack() as ctx:
        ps = psum(ctx, nc, f"{name}_ps", 8)
        turned = c.sem(f"{name}_turned")
        out = [c.sem(f"{name}_out{e}") for e in range(2)]

        def run(eng, copy, parity):
            for n in range(parity, len(items), 2):
                eng.wait_ge(turned, n + 1)
                evacuate(n, ps[:, n % 8], copy).then_inc(out[parity], 1)

        with nc.Block() as block:
            @block.tensor
            def _(pe):
                for n, parts in enumerate(items):
                    if n >= 8:
                        pe.wait_ge(out[n % 2], n // 2 - 3)
                    for q, a in enumerate(parts):
                        rows, cols = a.shape[0], a.shape[-1]
                        ins = nc.tensor.transpose(ps[:cols, n % 8, q * P:q * P + rows], a, c.ident[:rows, :rows])
                    ins.then_inc(turned, 1)

            @block.scalar
            def _(act):
                run(act, lambda o, i: nc.scalar.activation(o, i, ACT.Copy), 0)

            @block.vector
            def _(dve):
                run(dve, lambda o, i: nc.vector.tensor_copy(o, i), 1)


def attention(c, name, heads, keys, qT, kT, v, out, scale, width):
    nc = c.nc
    c.recycle()
    nk = keys // P
    n = heads * NT
    sb_ = min(keys, CH)
    nsb = keys // sb_
    with ExitStack() as ctx:
        ps_s = [psum(ctx, nc, f"{name}_scores{b}", nsb) for b in range(2)]
        ps_t = psum(ctx, nc, f"{name}_probsT", nsb)
        ps_o = psum(ctx, nc, f"{name}_out", 2)
        probs = sbuf(ctx, nc, f"{name}_probs", [P, 2, keys])
        probsT = sbuf(ctx, nc, f"{name}_probsT_sb", [P, 2, nk, P])
        top = sbuf(ctx, nc, f"{name}_top", [P, n])
        bias = sbuf(ctx, nc, f"{name}_bias", [P, n])
        total = sbuf(ctx, nc, f"{name}_total", [P, n])
        inv = sbuf(ctx, nc, f"{name}_inv", [P, n])
        scored, bias_ready, probs_ready, turned, mixed, stored = [
            c.sem(f"{name}_{x}") for x in
            ("scored", "bias_ready", "probs_ready", "turned", "mixed", "stored")]
        copied = [c.sem(f"{name}_copied{s}") for s in range(nsb)]
        per = min(nk, 4)

        def copy_bank(eng, copy, i, s):
            eng.wait_ge(turned, nsb * i + s + 1)
            if i >= 2:
                eng.wait_ge(mixed, i - 1)
            copy(probsT[:, i % 2, per * s:per * (s + 1)].rearrange("p j q -> p (j q)"),
                 ps_t[:, s, :per * P]).then_inc(copied[s], 1)

        with nc.Block() as block:
            @block.tensor
            def _(pe):
                def scores(i):
                    h, m = divmod(i, NT)
                    if i >= 2:
                        pe.wait_ge(probs_ready, i - 1)
                    pieces = list(zip(qT(h, m), kT(h)))
                    for s in range(nsb):
                        for k, (q, kk) in enumerate(pieces):
                            ins = nc.tensor.matmul(ps_s[i % 2][:, s, :sb_], q, kk[:, s * sb_:(s + 1) * sb_],
                                                   start=(k == 0), stop=(k == len(pieces) - 1))
                    ins.then_inc(scored, 1)

                def turn_probs(i):
                    pe.wait_ge(probs_ready, i + 1)
                    for s in range(nsb):
                        if i >= 1:
                            pe.wait_ge(copied[s], i)
                        for j in range(per):
                            ins = nc.tensor.transpose(ps_t[:, s, j * P:(j + 1) * P],
                                                      probs[:, i % 2, (per * s + j) * P:(per * s + j + 1) * P],
                                                      c.ident[:])
                        ins.then_inc(turned, 1)

                def mix(i):
                    h, m = divmod(i, NT)
                    for done in copied:
                        pe.wait_ge(done, i + 1)
                    if i >= 2:
                        pe.wait_ge(stored, i - 1)
                    for j in range(nk):
                        ins = nc.tensor.matmul(ps_o[:, i % 2, :width], probsT[:, i % 2, j, :], v(h, j),
                                               start=(j == 0), stop=(j == nk - 1))
                    ins.then_inc(mixed, 1)

                for i in range(n + 2):
                    if i < n:
                        scores(i)
                    if i >= 2:
                        mix(i - 2)
                    if 1 <= i <= n:
                        turn_probs(i - 1)

            @block.vector
            def _(dve):
                do = c.chain("vector", dve)

                def row_max(i):
                    dve.wait_ge(scored, i + 1)
                    do(nc.vector.tensor_reduce(top[:, i:i + 1], ps_s[i % 2][:, :, :sb_], mybir.AxisListType.XY, ALU.max))
                    nc.vector.tensor_scalar(bias[:, i:i + 1], top[:, i:i + 1], -scale, None,
                                            ALU.mult).then_inc(bias_ready, 1)

                def finish(i):
                    dve.wait_ge(probs_ready, i + 1)
                    do(nc.vector.reciprocal(inv[:, i:i + 1], total[:, i:i + 1]))
                    dve.wait_ge(mixed, i + 1)
                    h, m = divmod(i, NT)
                    nc.vector.tensor_scalar(out(h, m), ps_o[:, i % 2, :width], inv[:, i:i + 1], None,
                                            ALU.mult).then_inc(stored, 1)

                for i in range(n + 2):
                    if i < n:
                        row_max(i)
                    if nsb == 2 and 1 <= i <= n:
                        copy_bank(dve, nc.vector.tensor_copy, i - 1, 1)
                    if i >= 2:
                        finish(i - 2)

            @block.scalar
            def _(act):
                def exps(i):
                    act.wait_ge(bias_ready, i + 1)
                    if i >= 2:
                        act.wait_ge(turned, nsb * (i - 1))
                    nc.scalar.activation(probs[:, i % 2].rearrange("p (s k) -> p s k", k=sb_),
                                         ps_s[i % 2][:, :, :sb_], ACT.Exp, bias=bias[:, i:i + 1],
                                         scale=scale, accum_out=total[:, i:i + 1]).then_inc(probs_ready, 1)

                for i in range(n + 1):
                    if i < n:
                        exps(i)
                    if i >= 1:
                        copy_bank(act, lambda o, t: nc.scalar.activation(o, t, ACT.Copy), i - 1, 0)


def group_norm(c, name, x, sq, ssq, width, gain):
    nc = c.nc
    c.recycle()
    g = x.shape[1]
    meaned, rooted = c.sem(f"{name}_meaned"), c.sem(f"{name}_rooted")
    with nc.Block() as block:
        @block.vector
        def _(dve):
            do = c.chain("vector", dve)
            do(nc.vector.tensor_tensor(sq, x, x, ALU.mult))
            nc.vector.tensor_reduce(ssq, sq, AX, ALU.add).then_inc(meaned, 1)
            dve.wait_ge(rooted, 1)
            do(nc.vector.reciprocal(ssq, ssq))
            do(nc.vector.tensor_tensor(x, x, ssq.unsqueeze(2).to_broadcast([P, g, width]), ALU.mult))
            if gain is not None:
                do(nc.vector.tensor_tensor(x, x, gain.to_broadcast([P, g, width]), ALU.mult))

        @block.scalar
        def _(act):
            act.wait_ge(meaned, 1)
            nc.scalar.activation(ssq, ssq, ACT.Sqrt, bias=c.eps[:, 0:1], scale=1.0 / width).then_inc(rooted, 1)


def wide_norm(c, name, x, junk, ssq, width, gain):
    nc = c.nc
    c.recycle()
    tiles, groups = x.shape[1], x.shape[2]
    rooted = c.sem(f"{name}_rooted")
    with nc.Block() as block:
        @block.scalar
        def _(act):
            do = c.chain("scalar", act)
            for m in range(tiles):
                for g in range(groups):
                    n = m * groups + g
                    do(nc.scalar.activation(junk, x[:, m, g], ACT.Square, accum_out=ssq[:, n:n + 1]))
            nc.scalar.activation(ssq, ssq, ACT.Sqrt, bias=c.eps[:, 0:1], scale=1.0 / width).then_inc(rooted, 1)

        @block.vector
        def _(dve):
            do = c.chain("vector", dve)
            dve.wait_ge(rooted, 1)
            do(nc.vector.reciprocal(ssq, ssq))
            for m in range(tiles):
                for g in range(groups):
                    n = m * groups + g
                    nc.vector.scalar_tensor_tensor(x[:, m, g], x[:, m, g], ssq[:, n:n + 1], gain,
                                                   ALU.mult, ALU.mult)


def reduce_angle(nc, do, ang, tmp):
    do(nc.vector.tensor_scalar(tmp, ang, 1.0 / TWO_PI, ROUND, ALU.mult, ALU.add))
    do(nc.vector.tensor_scalar(tmp, tmp, -ROUND, None, ALU.add))
    for part in (PI_A, PI_B, PI_C):
        do(nc.vector.scalar_tensor_tensor(ang, tmp, -part, ang, ALU.mult, ALU.add))
    do(nc.vector.tensor_scalar(ang, ang, math.pi, -math.pi, ALU.min, ALU.max))



def level_masks(c, ctx):
    nc = c.nc
    mask = sbuf(ctx, nc, "mask", [P, LEVELS, P])
    with ExitStack() as tmp:
        half = sbuf(tmp, nc, "mask_half", [P, LEVELS, P])
        base = sbuf(tmp, nc, "mask_base", [P, LEVELS, P])
        halfT = sbuf(tmp, nc, "mask_halfT", [P, LEVELS, P])
        baseT = sbuf(tmp, nc, "mask_baseT", [P, LEVELS, P])
        with nc.Block() as block:
            @block.gpsimd
            def _(pool):
                for l in range(LEVELS):
                    w = 2 << l
                    nc.gpsimd.iota(base[:, l], [[w, P // w], [0, w]], base=0, channel_multiplier=0,
                                   allow_small_or_imprecise_dtypes=True)
                    nc.gpsimd.iota(half[:, l], [[w // 2, 2 * P // w], [0, w // 2]], base=0,
                                   channel_multiplier=0, allow_small_or_imprecise_dtypes=True)
        items = [[src[:, l]] for src in (base, half) for l in range(LEVELS)]

        def out(n, bank, copy):
            return copy((baseT if n < LEVELS else halfT)[:, n % LEVELS], bank[:, :P])

        turn(c, "masks", items, out)
        with nc.Block() as block:
            @block.vector
            def _(dve):
                do = c.chain("vector", dve)
                do(nc.vector.tensor_tensor(base[:], base[:], baseT[:], ALU.is_equal))
                do(nc.vector.tensor_tensor(half[:], half[:], halfT[:], ALU.not_equal))
                do(nc.vector.tensor_tensor(mask[:], base[:], half[:], ALU.mult))
    return mask


def hgrn_gates(c, logf, key, lb, lb1, reset, bcum):
    nc = c.nc
    c.recycle()
    decays = c.sem("hgrn_decays")
    logs = c.sem("hgrn_logs")
    with nc.Block() as block:
        @block.vector
        def _(dve):
            do = c.chain("vector", dve)
            for d in range(2):
                for h in range(HH):
                    do(nc.vector.tensor_scalar(logf[:, d, h], logf[:, d, h], lb1[:, d, h:h + 1], lb[:, d, h:h + 1],
                                               ALU.mult, ALU.add))
                    nc.vector.tensor_scalar(logf[:, d, h], logf[:, d, h], 2.0 ** -64, None,
                                            ALU.max).then_inc(decays, 1)
                    do(nc.vector.tensor_scalar(key[:, d, h], key[:, d, h], lb1[:, d, h:h + 1], None, ALU.mult))
            for d in range(2):
                dve.wait_ge(logs, HH * (d + 1))
                src = logf[:, d].rearrange("p h t -> p (h t)")
                dst = bcum[:, d].rearrange("p h t -> p (h t)")
                if d:
                    src, dst = src[:, ::-1], dst[:, ::-1]
                do(nc.vector.tensor_tensor_scan(dst, reset[:].rearrange("p h t -> p (h t)"), src, 0.0,
                                                ALU.mult, ALU.add))

        @block.scalar
        def _(act):
            for d in range(2):
                for h in range(HH):
                    act.wait_ge(decays, HH * d + h + 1)
                    nc.scalar.activation(logf[:, d, h], logf[:, d, h], ACT.Ln).then_inc(logs, 1)


def hgrn_pairs(c, h, q, key, bcum, mask, pairT):
    nc = c.nc
    c.recycle()
    with ExitStack() as ctx:
        side = sbuf(ctx, nc, f"hgrn{h}_side", [P, PAIR_BUFS, 2, T])
        both = sbuf(ctx, nc, f"hgrn{h}_both", [P, T])
        ps = psum(ctx, nc, f"hgrn{h}_ps", 6)
        both_ready, gap_ready, grown, side_ready, product, placed = [
            c.sem(f"hgrn{h}_{x}") for x in ("both_ready", "gap_ready", "grown", "side_ready", "product", "placed")]

        def halves(ap, l):
            w = 2 << l
            v = ap.rearrange("p (n w) -> p n w", w=w)
            return v[:, :, 0:w // 2], v[:, :, w // 2:w]

        with nc.Block() as block:
            @block.vector
            def _(dve):
                nc.vector.tensor_tensor(both[:], key[:, 0, h], key[:, 1, h], ALU.add).then_inc(both_ready, 1)

                def gaps(l):
                    if l >= PAIR_BUFS:
                        dve.wait_ge(product, l - PAIR_BUFS + 2)
                    wide = [P, T // (2 << l), 1 << l]
                    (l0, r0), (l1, r1) = [halves(bcum[:, d, h], l) for d in range(2)]
                    mid0 = l0[:, :, (1 << l) - 1:1 << l].to_broadcast(wide)
                    mid1 = r1[:, :, 0:1].to_broadcast(wide)
                    (kl, kr), (ql, qr) = [halves(side[:, l % PAIR_BUFS, i], l) for i in range(2)]
                    for o, first, second in ((kl, mid0, l0), (kr, mid1, r1), (ql, l1, mid1), (qr, r0, mid0)):
                        nc.vector.tensor_tensor(o, first, second, ALU.subtract).then_inc(gap_ready, 1)

                def place(l):
                    dve.wait_ge(product, l + 2)
                    dve.wait_ge(placed, l + 1)
                    b = 2 * (l % 2)
                    nc.vector.copy_predicated(
                        pairT[:], mask[:, l].bitcast(I32).unsqueeze(1).to_broadcast([P, NT, P]),
                        ps[:, b:b + 2, :].rearrange("p b (c t) -> p (b c) t", t=P)).then_inc(placed, 1)

                gaps(0)
                dve.wait_ge(product, 1)
                nc.vector.tensor_tensor(pairT[:], ps[:, 4:6, :].rearrange("p b (c t) -> p (b c) t", t=P),
                                        c.ident[:].unsqueeze(1).to_broadcast([P, NT, P]),
                                        ALU.mult).then_inc(placed, 1)
                for l in range(1, LEVELS):
                    gaps(l)
                    if l >= PAIR_BUFS - 1:
                        place(l - PAIR_BUFS + 1)
                for l in range(LEVELS - PAIR_BUFS + 1, LEVELS):
                    place(l)

            @block.scalar
            def _(act):
                for l in range(LEVELS):
                    act.wait_ge(gap_ready, 4 * (l + 1))
                    s = side[:, l % PAIR_BUFS]
                    nc.scalar.activation(s, s, ACT.Exp).then_inc(grown, 1)

            @block.gpsimd
            def _(pool):
                for l in range(LEVELS):
                    pool.wait_ge(grown, l + 1)
                    s = side[:, l % PAIR_BUFS]
                    for part, by in zip(halves(s[:, 0], l), (halves(key[:, 0, h], l)[0], halves(key[:, 1, h], l)[1])):
                        nc.gpsimd.tensor_tensor(part, part, by, ALU.mult).then_inc(side_ready, 1)
                    nc.gpsimd.tensor_tensor(s[:, 1], s[:, 1], q[:, h], ALU.mult).then_inc(side_ready, 1)

            @block.tensor
            def _(pe):
                pe.wait_ge(both_ready, 1)
                for t in range(NT):
                    ins = nc.tensor.matmul(ps[:, 4 + t // 4, (t % 4) * P:(t % 4 + 1) * P],
                                           both[:, t * P:(t + 1) * P], q[:, h, t * P:(t + 1) * P],
                                           start=True, stop=True)
                ins.then_inc(product, 1)
                for l in range(LEVELS):
                    pe.wait_ge(side_ready, 3 * (l + 1))
                    if l >= 2:
                        pe.wait_ge(placed, l)
                    for t in range(NT):
                        k, r = [side[:, l % PAIR_BUFS, i, t * P:(t + 1) * P] for i in range(2)]
                        ins = nc.tensor.matmul(ps[:, 2 * (l % 2) + t // 4, (t % 4) * P:(t % 4 + 1) * P], k, r,
                                               start=True, stop=True)
                    ins.then_inc(product, 1)


def hgrn_states(c, h, q, key, bcum, values, pairT, out):
    nc = c.nc
    c.recycle()
    hv = slice(h * HK, (h + 1) * HK)
    with ExitStack() as ctx:
        s = lambda n, shape: sbuf(ctx, nc, f"hst{h}_{n}", shape)
        qd, kd, kdT = s("qd", [P, 2, T]), s("kd", [P, 2, T]), s("kdT", [P, 2, NT, P])
        state, last = s("state", [P, 2, NT, P]), s("last", [P, 2, NT])
        ps = psum(ctx, nc, f"hst{h}_ps", 8)
        kgap, kgrown, kside, turned, copied, update, stated, summed = [
            c.sem(f"hst{h}_{x}") for x in
            ("kgap", "kgrown", "kside", "turned", "copied", "update", "stated", "summed")]
        wide = lambda b: ps[:, b:b + 2, :].rearrange("p b (c t) -> p (b c) t", t=P)
        with nc.Block() as block:
            @block.vector
            def _(dve):
                do = c.chain("vector", dve)
                for d in range(2):
                    b3 = bcum[:, d, h].rearrange("p (c t) -> p c t", t=P)
                    end = b3[:, :, 0:1] if d else b3[:, :, P - 1:P]
                    nc.vector.tensor_tensor(kd[:, d].rearrange("p (c t) -> p c t", t=P),
                                            end.to_broadcast([P, NT, P]), b3, ALU.subtract).then_inc(kgap, 1)
                for d in range(2):
                    dve.wait_ge(kgrown, 3 * (d + 1))
                    nc.vector.tensor_tensor(kd[:, d], kd[:, d], key[:, d, h], ALU.mult).then_inc(kside, 1)
                    do(nc.vector.tensor_tensor(qd[:, d], qd[:, d], q[:, h], ALU.mult))
                for d in range(2):
                    order = list(range(NT))[::-1] if d else list(range(NT))
                    do(nc.vector.memset(state[:, d, order[0]], 0.0))
                    dve.wait_ge(update, d + 1)
                    for prev, nxt in zip(order, order[1:]):
                        do(nc.vector.scalar_tensor_tensor(
                            state[:, d, nxt], state[:, d, prev], last[:, d, prev:prev + 1],
                            wide(4 + 2 * d)[:, prev], ALU.mult, ALU.add))
                nc.vector.tensor_copy(last[:, 0, 0:1], last[:, 0, 1:2]).then_inc(stated, 1)
                dve.wait_ge(summed, 1)
                do(nc.vector.tensor_copy(out[:, :, hv], wide(0)))

            @block.scalar
            def _(act):
                for d in range(2):
                    b3 = bcum[:, d, h].rearrange("p (c t) -> p c t", t=P)
                    end = b3[:, :, 0:1] if d else b3[:, :, P - 1:P]
                    nc.scalar.activation(qd[:, d], bcum[:, d, h], ACT.Exp).then_inc(kgrown, 1)
                    nc.scalar.activation(last[:, d].unsqueeze(2), end, ACT.Exp).then_inc(kgrown, 1)
                    act.wait_ge(kgap, d + 1)
                    nc.scalar.activation(kd[:, d], kd[:, d], ACT.Exp).then_inc(kgrown, 1)
                for d in range(2):
                    act.wait_ge(turned, d + 1)
                    nc.scalar.activation(kdT[:, d], wide(2 * d), ACT.Copy).then_inc(copied, 1)

            @block.tensor
            def _(pe):
                for d in range(2):
                    pe.wait_ge(kside, d + 1)
                    for t in range(NT):
                        ins = nc.tensor.transpose(wide(2 * d)[:, t], kd[:, d, t * P:(t + 1) * P], c.ident[:])
                    ins.then_inc(turned, 1)
                for d in range(2):
                    pe.wait_ge(copied, d + 1)
                    for t in range(NT):
                        ins = nc.tensor.matmul(wide(4 + 2 * d)[:, t], kdT[:, d, t], values[:, t, hv],
                                               start=True, stop=True)
                    ins.then_inc(update, 1)
                pe.wait_ge(stated, 1)
                for t in range(NT):
                    nc.tensor.matmul(wide(0)[:, t], pairT[:, t], values[:, t, hv], start=True, stop=False)
                    for d in range(2):
                        ins = nc.tensor.matmul(wide(0)[:, t], qd[:, d, t * P:(t + 1) * P], state[:, d, t],
                                               start=False, stop=(d == 1))
                ins.then_inc(summed, 1)


def mix_first(c, a, x):
    nc = c.nc
    with ExitStack() as ctx:
        s = lambda n, shape, dt=F32: sbuf(ctx, nc, n, shape, dt)
        hT, high = twins(ctx, nc, "mix_hT", "mix_high", [P, KD, T])
        mla_in = s("mla_in", [P, NT, QR + KVR + ROPE])
        w_in = a["w_in"][0].rearrange("(k p) n -> p k n", p=P)
        with ExitStack() as hg:
            s = lambda n, shape, dt=F32: sbuf(hg, nc, n, shape, dt)
            q = s("hg_q", [P, HH, T])
            logf = x[:].rearrange("p (d h) t -> p d h t", d=2)
            key = s("hg_key", [P, 2, HH, T])
            values = s("hg_values", [P, NT, HH * HK])
            gate = s("hg_gate", [P, NT, HH * HK])
            o = QR + KVR + ROPE
            do = c.chain("scalar", nc.scalar)

            def per_channel(i):
                def evacuate(b, ps):
                    ch, t = b // 2, slice((b % 2) * CH, (b % 2 + 1) * CH)
                    if i == 0:
                        return nc.scalar.activation(q[:, ch, t], ps, ACT.Silu)
                    nc.scalar.activation(logf[:, i - 1, ch, t], ps, ACT.Sigmoid)
                    return nc.scalar.activation(key[:, i - 1, ch, t], ps, ACT.Sigmoid, scale=-1.0)
                return evacuate

            part = lambda i: w_in[:, :, o + i * CH:o + (i + 1) * CH]
            low_ = ExitStack()
            low = sbuf(low_, nc, "mix_low", [P, KD, T])
            pair = (high, low)
            jobs = [Job(w_in[:, :, 0:o], True, pair,
                        lambda b, ps: nc.scalar.activation(mla_in[:, b], ps[:, :o], ACT.Copy), "scalar")]
            jobs += [Job(part(i), False, pair, per_channel(i), "scalar") for i in range(3)]
            jobs += [Job(part(3), True, pair, lambda b, ps: nc.vector.tensor_copy(values[:, b], ps), "vector"),
                     Job(part(4), True, pair, lambda b, ps: nc.scalar.activation(gate[:, b], ps, ACT.Silu), "scalar")]
            with low_:
                stream = Stream(c, low_, "mix_w", kp=1, cuts=3)
                stream.start(jobs)
                room = values[:].rearrange("p m v -> p (m v)")
                gain = room[:, 3 * D:4 * D]
                load(c, [(gain, a["norm_mix"].to_broadcast([P, D]))])
                norm_split(c, "mix", x, pair, gain, NT, room[:, :3 * D])
                project(c, "mix_in", stream, jobs)
            lbl, lb, lb1 = s("lb_logits", [P, 2, 2, HH]), s("lb", [P, 2, HH]), s("lb1", [P, 2, HH])
            onorm = s("hg_onorm", [P, 1, HK])
            load(c, [(lbl[:, r, d], a["hg_lb_logits"][r, d].rearrange("(h p) -> p h", p=P))
                     for r in range(2) for d in range(2)]
                 + [(onorm[:, 0], a["hg_o_norm"][0].unsqueeze(0).to_broadcast([P, HK]))])
            reset = hT[:, 0:HH]
            with nc.Block() as block:
                @block.vector
                def _(dve):
                    do = c.chain("vector", dve)
                    do(nc.vector.tensor_tensor(lb[:], lbl[:, 0], lbl[:, 1], ALU.subtract))
                    do(nc.vector.memset(reset, 1.0))
                    do(nc.vector.memset(reset.rearrange("p h (c t) -> p (h c) t", t=P)[:, :, 0:1], 0.0))
            with nc.Block() as block:
                @block.scalar
                def _(act):
                    do = c.chain("scalar", act)
                    do(nc.scalar.activation(lb1[:], lb[:], ACT.Sigmoid, scale=-1.0))
                    do(nc.scalar.activation(lb[:], lb[:], ACT.Sigmoid))
            hgrn_gates(c, logf, key, lb, lb1, reset, logf)
            mask = level_masks(c, hg)
            pairT = s("hg_pairT", [P, NT, P])
            mixed = hT[:, 4:8].rearrange("p k t -> p (k t)").rearrange("p (m v) -> p m v", v=HH * HK)
            for h in range(HH):
                hgrn_pairs(c, h, q, key, logf, mask, pairT)
                hgrn_states(c, h, q, key, logf, values, pairT, mixed)
            ssq = s("hg_ssq", [P, NT * HH])
            heads = lambda t: t.rearrange("p m (h v) -> p (m h) v", v=HK)
            group_norm(c, "hg_norm", heads(mixed), heads(values[:]), ssq[:], HK, onorm[:])
            with nc.Block() as block:
                @block.vector
                def _(dve):
                    do = c.chain("vector", dve)
                    do(nc.vector.tensor_tensor(values[:], mixed, gate[:], ALU.mult))
            items = [[values[:, m, h * P:(h + 1) * P] for h in range(HH)] for m in range(NT)]
            turn(c, "hg_turn", items, lambda n, ps, copy: copy(
                hT[:, HH:, n * P:(n + 1) * P], ps.rearrange("p (h t) -> p h t", t=P)))
        mla(c, a, mla_in, hT, x[:].rearrange("p m d -> p (m d)")[:, :NT * MH * QK].rearrange(
            "p (m h d) -> p m h d", m=NT, h=MH))
        with ExitStack() as w_:
            pair = [sbuf(w_, nc, f"mix_out_{n}", [P, KD, T]) for n in ("high", "low")]
            stream = Stream(c, w_, "mix_out_w")
            jobs = add_jobs(c, pair, a["w_out"][0], x)
            stream.start(jobs)
            load(c, [(x[:], a["x"][0].rearrange("(m p) d -> p m d", p=P))])
            project(c, "mix_out", stream, jobs, source=hT)


def add_jobs(c, src, w, x):
    nc = c.nc

    def add(i):
        at = slice(i * CH, (i + 1) * CH)
        return lambda b, ps: nc.vector.tensor_tensor(x[:, b, at], ps, x[:, b, at], ALU.add)

    return [Job(columns(w, i), True, src, add(i), "vector") for i in range(D // CH)]


def rope_tables(c, ctx, a):
    nc = c.nc
    s = lambda n, shape, dt=F32: sbuf(ctx, nc, n, shape, dt)
    cos, sin = s("rope_cos", [P, NT, HALF]), s("rope_sin", [P, NT, HALF])
    with ExitStack() as tmp:
        s = lambda n, shape, dt=F32: sbuf(tmp, nc, n, shape, dt)
        wide = a["positions"].dtype != I32
        posi = s("rope_posi", [P, NT, 2 if wide else 1], I32)
        pos, ang, t = s("rope_pos", [P, NT]), s("rope_ang", [P, NT, HALF]), s("rope_tmp", [P, NT, HALF])
        src = a["positions"][0]
        if wide:
            src = src.bitcast(I32)
        load(c, [(posi[:], src.rearrange("(m p two) -> p m two", p=P, two=2 if wide else 1))])
        with nc.Block() as block:
            @block.vector
            def _(dve):
                do = c.chain("vector", dve)
                do(nc.vector.tensor_copy(pos[:], posi[:, :, 0]))
                for j in range(HALF):
                    freq = float(np.float32(1.0) / np.float32(ROPE_BASE ** (j / HALF)))
                    do(nc.vector.tensor_scalar(ang[:, :, j], pos[:], freq, None, ALU.mult))
                reduce_angle(nc, do, ang[:], t[:])
                do(nc.vector.tensor_scalar(t[:], ang[:], -1.0, None, ALU.mult))
                do(nc.vector.tensor_tensor(t[:], t[:], ang[:], ALU.min))
                do(nc.vector.tensor_scalar(t[:], t[:], math.pi / 2, None, ALU.add))
        with nc.Block() as block:
            @block.scalar
            def _(act):
                nc.scalar.activation(sin[:], ang[:], ACT.Sin)
                nc.scalar.activation(cos[:], t[:], ACT.Sin)
    return cos, sin


def mla(c, a, mla_in, mixT, scratch):
    nc = c.nc
    with ExitStack() as ctx:
        s = lambda n, shape, dt=F32: sbuf(ctx, nc, n, shape, dt)
        qT, kT = s("mla_qT", [QK, MH, T]), s("mla_kT", [QK, MH, T])
        v = s("mla_v", [P, NT, MH, VD])
        with ExitStack() as ctx2:
            s = lambda n, shape, dt=F32: sbuf(ctx2, nc, n, shape, dt)
            q = scratch
            cos, sin = rope_tables(c, ctx2, a)
            qn, kn = s("mla_qn", [P, 1, QK]), s("mla_kn", [P, 1, QK])
            ssq = s("mla_ssq", [P, NT * MH])
            with ExitStack() as ctx3:
                s = lambda n, shape, dt=F32: sbuf(ctx3, nc, n, shape, dt)
                qga, qgb, kvg = s("mla_qga", [P, 1]), s("mla_qgb", [QR - P, 1]), s("mla_kvg", [P, 1])
                wqa, wqb = s("mla_wqa", [P, MH * QK]), s("mla_wqb", [QR - P, MH * QK])
                wkv = s("mla_wkv", [P, MH * (NOPE + VD)])
                cqT, cqT2, ckvT = s("mla_cqT", [P, T]), s("mla_cqT2", [QR - P, T]), s("mla_ckvT", [P, T])
                k = s("mla_k", [P, NT, MH, QK])
                load(c, [(qga[:], a["mla_q_a_norm"][0, 0:P].unsqueeze(1)),
                         (qgb[:], a["mla_q_a_norm"][0, P:QR].unsqueeze(1)),
                         (kvg[:], a["mla_kv_a_norm"][0].unsqueeze(1)),
                         (wqa[:], a["mla_w_q_up"][0, 0:P, :]), (wqb[:], a["mla_w_q_up"][0, P:QR, :]),
                         (wkv[:], a["mla_w_kv_up"][0]),
                         (qn[:, 0], a["mla_q_norm"][0].unsqueeze(0).to_broadcast([P, QK])),
                         (kn[:, 0], a["mla_k_norm"][0].unsqueeze(0).to_broadcast([P, QK]))])
                flat = lambda t: t.rearrange("p m h d -> p m (h d)")
                junk = flat(q[:])
                group_norm(c, "mla_cq", mla_in[:, :, 0:QR], junk[:, :, 0:QR], ssq[:, 0:NT], QR, None)
                group_norm(c, "mla_ckv", mla_in[:, :, QR:QR + KVR], junk[:, :, 0:KVR], ssq[:, 0:NT], KVR, None)
                items = [[mla_in[:, m, 0:P], mla_in[:, m, P:QR], mla_in[:, m, QR:QR + KVR]] for m in range(NT)]

                def out(n, ps, copy):
                    t = slice(n * P, (n + 1) * P)
                    if n % 2:
                        nc.vector.tensor_scalar(cqT[:, t], ps[:, 0:P], qga[:, 0:1], None, ALU.mult)
                        nc.vector.tensor_scalar(cqT2[:, t], ps[:QR - P, P:2 * P], qgb[:, 0:1], None, ALU.mult)
                        return nc.vector.tensor_scalar(ckvT[:, t], ps[:, 2 * P:3 * P], kvg[:, 0:1], None, ALU.mult)
                    nc.scalar.activation(cqT[:, t], ps[:, 0:P], ACT.Copy, scale=qga[:, 0:1])
                    nc.scalar.activation(cqT2[:, t], ps[:QR - P, P:2 * P], ACT.Copy, scale=qgb[:, 0:1])
                    return nc.scalar.activation(ckvT[:, t], ps[:, 2 * P:3 * P], ACT.Copy, scale=kvg[:, 0:1])

                turn(c, "mla_turn", items, out)
                up = ExitStack()
                ps = psum(up, nc, "mla_up_ps", 8)
                made = c.sem("mla_up_made")
                q_taken, kv_taken = c.sem("mla_q_taken"), c.sem("mla_kv_taken")
                hq = MH // 2 * QK
                with nc.Block() as block:
                    @block.tensor
                    def _(pe):
                        for m in range(NT):
                            t, b0 = slice(m * P, (m + 1) * P), 4 * (m % 2)
                            if m >= 2:
                                pe.wait_ge(q_taken, m - 1)
                                pe.wait_ge(kv_taken, m - 1)
                            for b in range(2):
                                nc.tensor.matmul(ps[:, b0 + b, :hq], cqT[:, t], wqa[:, b * hq:(b + 1) * hq],
                                                 start=True, stop=False)
                                nc.tensor.matmul(ps[:, b0 + b, :hq], cqT2[:, t], wqb[:, b * hq:(b + 1) * hq],
                                                 start=False, stop=True)
                            for b in range(2):
                                ins = nc.tensor.matmul(ps[:, b0 + 2 + b], ckvT[:, t], wkv[:, b * CH:(b + 1) * CH],
                                                       start=True, stop=True)
                            ins.then_inc(made, 1)

                    @block.scalar
                    def _(act):
                        for m in range(NT):
                            act.wait_ge(made, m + 1)
                            b0 = 4 * (m % 2)
                            nc.scalar.activation(
                                q[:, m].rearrange("p (b h) d -> p b (h d)", b=2), ps[:, b0:b0 + 2, :hq],
                                ACT.Copy).then_inc(q_taken, 1)

                    @block.vector
                    def _(dve):
                        for m in range(NT):
                            dve.wait_ge(made, m + 1)
                            b0 = 4 * (m % 2)
                            kv = ps[:, b0 + 2:b0 + 4, :].rearrange("p b (h d) -> p (b h) d", d=NOPE + VD)
                            nc.vector.tensor_copy(k[:, m, :, 0:NOPE], kv[:, :, 0:NOPE])
                            nc.vector.tensor_copy(
                                k[:, m, :, NOPE:],
                                mla_in[:, m, QR + KVR:].unsqueeze(1).to_broadcast([P, MH, ROPE]))
                            nc.vector.tensor_copy(v[:, m], kv[:, :, NOPE:]).then_inc(kv_taken, 1)
                up.close()
                for name, y, gain, dst in (("mla_qn", q, qn, qT), ("mla_kn", k, kn, kT)):
                    grp = y[:].rearrange("p m h d -> p (m h) d")
                    sqt = mixT[:, 0:4].rearrange("p k t -> p (k t)")[:, :NT * MH // 2 * QK].rearrange(
                        "p (g d) -> p g d", d=QK)
                    for hf in range(2):
                        gs = slice(hf * NT * MH // 2, (hf + 1) * NT * MH // 2)
                        group_norm(c, f"{name}{hf}", grp[:, gs], sqt, ssq[:, gs], QK, gain[:])
                    rope(c, name, y, cos, sin, sqt)
                    items = [[y[:, m, 4 * hh + i] for i in range(4)] for m in range(NT) for hh in range(2)]

                    def out(n, ps, copy, dst=dst):
                        m, hh = divmod(n, 2)
                        return copy(dst[:, 4 * hh:4 * hh + 4, m * P:(m + 1) * P],
                                    ps[:QK].rearrange("p (h t) -> p h t", t=P))

                    turn(c, f"{name}_turn", items, out)
        with ExitStack() as ctx2:
            o = sbuf(ctx2, nc, "mla_o", [P, NT, MH, VD])
            attention(c, "mla_attn", MH, T,
                      lambda h, m: [qT[:, h, m * P:(m + 1) * P]], lambda h: [kT[:, h]],
                      lambda h, j: v[:, j, h], lambda h, m: o[:, m, h], QK ** -0.5, VD)
            of = o[:].rearrange("p m h d -> p m (h d)")
            items = [[of[:, m, k * P:(k + 1) * P] for k in range(4)] for m in range(NT)]
            turn(c, "mla_oturn", items, lambda n, ps, copy: copy(
                mixT[:, 0:4, n * P:(n + 1) * P], ps.rearrange("p (h t) -> p h t", t=P)))


def rope(c, name, y, cos, sin, tmp):
    nc = c.nc
    with nc.Block() as block:
        @block.vector
        def _(dve):
            do = c.chain("vector", dve)
            for m in range(NT):
                y1, y2 = y[:, m, :, NOPE:NOPE + HALF], y[:, m, :, NOPE + HALF:]
                cs, sn = [t[:, m].unsqueeze(1).to_broadcast([P, MH, HALF]) for t in (cos, sin)]
                parts = [tmp[:, i * MH:(i + 1) * MH, 0:HALF] for i in range(4)]
                do_all = [(parts[0], y1, cs), (parts[1], y2, sn), (parts[2], y2, cs), (parts[3], y1, sn)]
                for o, l, r in do_all[:3]:
                    nc.vector.tensor_tensor(o, l, r, ALU.mult)
                do(nc.vector.tensor_tensor(*do_all[3], ALU.mult))
                nc.vector.tensor_tensor(y1, parts[0], parts[1], ALU.subtract)
                do(nc.vector.tensor_tensor(y2, parts[2], parts[3], ALU.add))



def cross_first(c, a, x):
    nc = c.nc
    kv_cols = 2 * XH * XD
    with ExitStack() as ctx:
        s = lambda n, shape, dt=F32: sbuf(ctx, nc, n, shape, dt)
        qn, kn = s("x_qn", [P, 1, XD]), s("x_kn", [P, 1, XD])
        kT = s("x_kT", [P, XH * 2, MEM])
        kv = s("x_kv", [P, MEM // P, kv_cols])
        ssq = s("x_ssq", [P, NT * XH])
        hT, high = twins(ctx, nc, "x_hT", "x_high", [P, KD, T])
        low = s("x_low", [P, KD, T])
        q = s("x_q", [P, NT, XH * XD])
        mem = q[:, 0:MEM // P]
        pair = (high, low)
        memT = [t[:, :, 0:MEM] for t in pair]
        stream = Stream(c, ctx, "x_w")
        with ExitStack() as g_:
            gain, mgain = sbuf(g_, nc, "x_gain", [P, D]), sbuf(g_, nc, "x_mgain", [P, D])

            def rows(src, dst, i, w):
                return Job(columns(w, i), True, src, lambda b, ps: nc.scalar.activation(
                    dst[:, b, i * CH:(i + 1) * CH], ps, ACT.Copy), "scalar")

            kv_jobs = [rows(memT, kv, i, a["x_w_kv"][0]) for i in range(kv_cols // CH)]
            q_jobs = [rows(pair, q, i, a["x_w_q"][0]) for i in range(D // CH)]
            stream.start(kv_jobs)
            load(c, [(mem, a["mem"][0].rearrange("(m p) d -> p m d", p=P)),
                     (gain[:], a["norm_cross"].to_broadcast([P, D])),
                     (mgain[:], a["norm_mem"].to_broadcast([P, D])),
                     (qn[:, 0], a["x_q_norm"][0].unsqueeze(0).to_broadcast([P, XD])),
                     (kn[:, 0], a["x_k_norm"][0].unsqueeze(0).to_broadcast([P, XD]))])
            norm_split(c, "x_mem", mem, memT, mgain[:], MEM // P)
            project(c, "x_kv_up", stream, kv_jobs, banks=MEM // P)
            stream.start(q_jobs)
            for m in range(MEM // P):
                grp = kv[:, m, 0:XH * XD].rearrange("p (h d) -> p h d", d=XD)
                group_norm(c, f"x_k{m}", grp, q[:, 0].rearrange("p (h d) -> p h d", d=XD), ssq[:, 0:XH], XD, kn[:])
            items = [[kv[:, m, (4 * g + j) * P:(4 * g + j + 1) * P] for j in range(4)]
                     for m in range(MEM // P) for g in range(2)]
            turn(c, "x_kturn", items, lambda n, ps, copy: copy(
                kT[:, 4 * (n % 2):4 * (n % 2) + 4, (n // 2) * P:(n // 2 + 1) * P],
                ps.rearrange("p (j t) -> p j t", t=P)))
            norm_split(c, "x_x", x, pair, gain[:], NT)
        project(c, "x_q_up", stream, q_jobs)
        out_jobs = add_jobs(c, pair, a["x_w_o"][0], x)
        stream.start(out_jobs)
        wide_norm(c, "x_qn", q[:].rearrange("p m (h d) -> p m h d", d=XD), hT[:, 0, 0:XD], ssq[:], XD, qn[:, 0])

        items = [[q[:, m, (4 * g + j) * P:(4 * g + j + 1) * P] for j in range(4)]
                 for m in range(NT) for g in range(2)]
        place = lambda t, n: t[:, 4 * (n % 2):4 * (n % 2) + 4, (n // 2) * P:(n // 2 + 1) * P]
        turn(c, "x_qturn", items, lambda n, ps, copy: copy(place(hT, n), ps.rearrange("p (j t) -> p j t", t=P)))
        attention(c, "x_attn", XH, MEM,
                  lambda h, m: [hT[:, 2 * h + j, m * P:(m + 1) * P] for j in range(2)],
                  lambda h: [kT[:, 2 * h + j] for j in range(2)],
                  lambda h, j: kv[:, j, XH * XD + h * XD:XH * XD + (h + 1) * XD],
                  lambda h, m: q[:, m, h * XD:(h + 1) * XD], XD ** -0.5, XD)
        turn_split(c, "x_oturn", items, lambda n: (place(high, n), place(low, n)))
        project(c, "x_out", stream, out_jobs)



def pick_first(nc, do, v, mx, ids, eq, oh):
    wide = mx.unsqueeze(2).to_broadcast([P, NT, 8])
    do(nc.vector.tensor_tensor(eq, v, wide, ALU.is_equal))
    do(nc.vector.scalar_tensor_tensor(eq, eq, -8.0, ids, ALU.mult, ALU.add))
    do(nc.vector.tensor_reduce(mx, eq, AX, ALU.min))
    do(nc.vector.tensor_tensor(oh, eq, wide, ALU.is_equal))


def route(c, a, hT, w1, w2, slot_tok, slot_row, ov_expert, ov_count, weights):
    nc = c.nc
    c.recycle()
    NE = G + E
    with ExitStack() as ctx:
        s = lambda n, shape, dt=F32: sbuf(ctx, nc, n, shape, dt)
        wr, bias = s("rt_w", [P, KD, NE]), s("rt_bias", [P, 1, NE])
        lg = s("rt_logits", [P, NT, NE])
        load(c, [(wr[:, :, 0:G], a["moe_w_group"][0].rearrange("(k p) n -> p k n", p=P)),
                 (wr[:, :, G:], a["moe_w_expert"][0].rearrange("(k p) n -> p k n", p=P)),
                 (bias[:, 0, 0:G], a["moe_b_group"][0].unsqueeze(0).to_broadcast([P, G])),
                 (bias[:, 0, G:], a["moe_b_expert"][0].unsqueeze(0).to_broadcast([P, E]))])
        ps = psum(ctx, nc, "rt_ps", 8)
        with nc.Block() as block:
            @block.sync
            def _(sp):
                for n in range(2):
                    load_expert_weights(sp, a, weights, n, 2, 2 * n)

            @block.tensor
            def _(pe):
                for m in range(NT):
                    for k in range(KD):
                        nc.tensor.matmul(ps[:, m, :NE], hT[:, k, m * P:(m + 1) * P], wr[:, k],
                                         start=(k == 0), stop=(k == KD - 1))
        ids8, tok = s("rt_ids8", [P, NT, 8]), s("rt_tok", [P, NT])
        e128, ids15 = s("rt_e128", [P, 1, E]), s("rt_ids15", [P, OVB])
        idsb = s("rt_idsb", [P, NBLK])
        gm, eq, gh = s("rt_gm", [P, NT]), s("rt_eq", [P, NT, 8]), s("rt_gh", [P, NT, 8])
        ex, gs = s("rt_ex", [P, NT, 8]), s("rt_gs", [P, NT])
        prod = s("rt_prod", [P, NT, G, PG])
        sel, m1, m2 = s("rt_sel", [P, NT, 8]), s("rt_m1", [P, NT]), s("rt_m2", [P, NT])
        oh = [s(f"rt_oh{k}", [P, NT, 8]) for k in range(2)]
        pick = [s(f"rt_pick{k}", [P, NT, G, PG]) for k in range(2)]
        both = s("rt_both", [P, NT, E])
        with nc.Block() as block:
            @block.gpsimd
            def _(pool):
                it = lambda t, pat, base, mul: nc.gpsimd.iota(t, pat, base=base, channel_multiplier=mul,
                                                              allow_small_or_imprecise_dtypes=True)
                it(ids8[:], [[0, NT], [1, 8]], 0, 0)
                it(tok[:], [[P, NT]], 0, 1)
                it(e128[:, 0], [[CAP, E]], 0, 0)
                it(ids15[:], [[1, OVB]], 0, 0)
                it(idsb[:], [[1, NBLK]], 0, 0)

            @block.vector
            def _(dve):
                do = c.chain("vector", dve)
                do(nc.vector.tensor_tensor(lg[:], ps[:, :, :NE], bias[:].to_broadcast([P, NT, NE]), ALU.add))
                do(nc.vector.tensor_reduce(gm[:], lg[:, :, 0:G], AX, ALU.max))
                do(nc.vector.tensor_tensor(ex[:], lg[:, :, 0:G], gm[:].unsqueeze(2).to_broadcast([P, NT, G]),
                                           ALU.subtract))
        with nc.Block() as block:
            @block.scalar
            def _(act):
                nc.scalar.activation(ex[:], ex[:], ACT.Exp)

            @block.vector
            def _(dve):
                do = c.chain("vector", dve)
                pick_first(nc, do, lg[:, :, 0:G], gm[:], ids8[:], eq[:], gh[:])
                do(nc.vector.tensor_tensor(prod[:], lg[:, :, G:].rearrange("p m (g l) -> p m g l", l=PG),
                                           gh[:].unsqueeze(3).to_broadcast([P, NT, G, PG]), ALU.mult))
                do(nc.vector.tensor_reduce(sel[:], prod[:].rearrange("p m g l -> p m l g"), AX, ALU.add))
                do(nc.vector.tensor_reduce(m1[:], sel[:], AX, ALU.max))
                do(nc.vector.tensor_copy(gm[:], m1[:]))
                pick_first(nc, do, sel[:], gm[:], ids8[:], eq[:], oh[0][:])
                do(nc.vector.scalar_tensor_tensor(sel[:], oh[0][:], -1e30, sel[:], ALU.mult, ALU.add))
                do(nc.vector.tensor_reduce(m2[:], sel[:], AX, ALU.max))
                do(nc.vector.tensor_copy(gm[:], m2[:]))
                pick_first(nc, do, sel[:], gm[:], ids8[:], eq[:], oh[1][:])
                do(nc.vector.tensor_tensor(m2[:], m2[:], m1[:], ALU.subtract))
                for k in range(2):
                    do(nc.vector.tensor_tensor(pick[k][:], gh[:].unsqueeze(3).to_broadcast([P, NT, G, PG]),
                                               oh[k][:].unsqueeze(2).to_broadcast([P, NT, G, PG]), ALU.mult))
                flat = [pick[k][:].rearrange("p m g l -> p m (g l)") for k in range(2)]
                do(nc.vector.tensor_tensor(both[:], flat[0], flat[1], ALU.add))
        with nc.Block() as block:
            @block.scalar
            def _(act):
                nc.scalar.activation(m2[:], m2[:], ACT.Exp)

            @block.tensor
            def _(pe):
                for m in range(NT):
                    for i in range(m + 1):
                        nc.tensor.matmul(ps[:, 0, m * E:(m + 1) * E], (c.before if i == m else c.ones)[:],
                                         both[:, i], start=(i == 0), stop=(i == m))
                for i in range(NT):
                    nc.tensor.matmul(ps[:, 1, :E], c.ones[:], both[:, i], start=(i == 0), stop=(i == NT - 1))
        nb, oend, high = s("rt_nb", [P, 1, E]), s("rt_oend", [P, 1, E]), s("rt_high", [P, 1, E])
        rank, low, dst = s("rt_rank", [P, NT, E]), s("rt_low", [P, NT, E]), s("rt_dst", [P, NT, E])
        dest, blk, pos, val = [s(f"rt_{n}", [P, 2, NT]) for n in ("dest", "blk", "pos", "val")]
        atpos = s("rt_atpos", [P, 2, NT, P])
        atblk = s("rt_atblk", [P, 2, NT, NBLK])
        over = s("rt_over", [P, OVB, E])
        oe = s("rt_oe", [P, OVB])
        with nc.Block() as block:
            @block.vector
            def _(dve):
                do = c.chain("vector", dve)
                v = nc.vector
                do(v.tensor_reduce(gs[:], ex[:], AX, ALU.add))
                do(v.tensor_scalar(m1[:], m2[:], 1.0, None, ALU.add))
                do(v.tensor_tensor(gs[:], gs[:], m1[:], ALU.mult))
                do(v.reciprocal(w1, gs[:]))
                do(v.tensor_tensor(w2, w1, m2[:], ALU.mult))
                do(v.tensor_scalar(nb[:, 0], ps[:, 1, :E], -float(CAP), 0.0, ALU.add, ALU.max))
                do(v.tensor_scalar(nb[:], nb[:], 1.0 / P, (P - 0.5) / P - 0.5, ALU.mult, ALU.add))
                do(v.tensor_scalar(nb[:], nb[:], ROUND, None, ALU.add))
                do(v.tensor_scalar(nb[:], nb[:], -ROUND, None, ALU.add))
                do(v.tensor_tensor_scan(oend[:, 0], c.ones[:, :E], nb[:, 0], 0.0, ALU.mult, ALU.add))
                do(v.tensor_tensor(high[:], oend[:], nb[:], ALU.subtract))
                do(v.tensor_scalar(high[:], high[:], float(P), float(E * CAP - CAP), ALU.mult, ALU.add))
                do(v.tensor_copy(rank[:].rearrange("p m e -> p (m e)"), ps[:, 0]))
                do(v.tensor_scalar(low[:], rank[:], float(CAP), None, ALU.is_lt))
                do(v.tensor_tensor(e128[:], e128[:], high[:], ALU.subtract))
                do(v.tensor_tensor(low[:], low[:], e128[:].to_broadcast([P, NT, E]), ALU.mult))
                do(v.tensor_tensor(dst[:], rank[:], high[:].to_broadcast([P, NT, E]), ALU.add))
                do(v.tensor_tensor(dst[:], dst[:], low[:], ALU.add))
                for k in range(2):
                    do(v.tensor_tensor(rank[:], dst[:], pick[k][:].rearrange("p m g l -> p m (g l)"), ALU.mult))
                    do(v.tensor_reduce(dest[:, k], rank[:], AX, ALU.add))
                    do(v.tensor_scalar(val[:, k], tok[:], 2.0, float(k + 1), ALU.mult, ALU.add))
                do(v.tensor_scalar(blk[:], dest[:], 1.0 / P, 0.5 / P - 0.5, ALU.mult, ALU.add))
                do(v.tensor_scalar(blk[:], blk[:], ROUND, None, ALU.add))
                do(v.tensor_scalar(blk[:], blk[:], -ROUND, None, ALU.add))
                do(v.scalar_tensor_tensor(pos[:], blk[:], -float(P), dest[:], ALU.mult, ALU.add))
                for k in range(2):
                    for m in range(NT):
                        v.tensor_scalar(atpos[:, k, m], c.row[:], pos[:, k, m:m + 1], None, ALU.is_equal)
                        v.tensor_scalar(atblk[:, k, m], idsb[:], blk[:, k, m:m + 1], val[:, k, m:m + 1],
                                        ALU.is_equal, ALU.mult)
                do(v.tensor_tensor(over[:], oend[:].to_broadcast([P, OVB, E]),
                                   ids15[:].unsqueeze(2).to_broadcast([P, OVB, E]), ALU.is_le))
                do(v.tensor_reduce(oe[:], over[:], AX, ALU.add))
                do(v.tensor_scalar(ov_expert, oe[0:1, :], float(E - 1), None, ALU.min))
                do(v.tensor_copy(ov_count, oend[0:1, 0, E - 1:E]))
        with nc.Block() as block:
            @block.tensor
            def _(pe):
                n = [(k, m) for k in range(2) for m in range(NT)]
                for i, (k, m) in enumerate(n):
                    nc.tensor.matmul(ps[:, 2, :NBLK], atpos[:, k, m], atblk[:, k, m], start=(i == 0),
                                     stop=(i == len(n) - 1))
        free, rowv, tokv = s("rt_free", [P, NBLK]), s("rt_rowv", [P, NBLK]), s("rt_tokv", [P, NBLK])
        with nc.Block() as block:
            @block.vector
            def _(dve):
                do = c.chain("vector", dve)
                v = nc.vector
                do(v.tensor_scalar(free[:], ps[:, 2, :NBLK], 0.0, 4.0 * T, ALU.is_equal, ALU.mult))
                do(v.tensor_scalar(rowv[:], ps[:, 2, :NBLK], -1.0, None, ALU.add))
                do(v.tensor_scalar(tokv[:], rowv[:], 0.5, -0.25, ALU.mult, ALU.add))
                do(v.tensor_scalar(tokv[:], tokv[:], ROUND, None, ALU.add))
                do(v.tensor_scalar(tokv[:], tokv[:], -ROUND, None, ALU.add))
                do(v.tensor_tensor(tokv[:], tokv[:], free[:], ALU.add))
                do(v.tensor_tensor(rowv[:], rowv[:], free[:], ALU.add))
                do(v.tensor_copy(slot_tok, tokv[:]))
                do(v.tensor_copy(slot_row, rowv[:]))


def wait_for(eng, sem, value):
    if not (isinstance(value, int) and value <= 0):
        eng.wait_ge(sem, value)


def expert_weights(c, ctx, name, small, parts, sem):
    return (sbuf(ctx, c.nc, f"{name}_wgu", [P, small * parts, KD, 2 * EH]),
            sbuf(ctx, c.nc, f"{name}_wd", [P, small * parts, EH // P, D]),
            [sem(f"{name}_gate_up_in{b}") for b in range(small)], [sem(f"{name}_down_in{b}") for b in range(small)])


def load_expert_weights(sp, a, weights, w, parts, expert, before=(lambda: None, lambda: None)):
    wgu, wd, gu_in, d_in = weights
    before[0]()
    for h in range(parts):
        for i, name in enumerate(("moe_w_gate", "moe_w_up")):
            src = a[name][0, bass.ds(expert + h, 1)].rearrange("o (k p) n -> p (o k) n", p=P)
            sp.dma_start(wgu[:, w * parts + h, :, i * EH:(i + 1) * EH], src).then_inc(gu_in[w], 16)
    before[1]()
    for h in range(parts):
        src = a["moe_w_down"][0, bass.ds(expert + h, 1)].rearrange("o (k p) n -> p (o k) n", p=P)
        sp.dma_start(wd[:, w * parts + h], src).then_inc(d_in[w], 16)


class ExpertSteps:

    def __init__(self, c, ctx, name, a, xn, y, gain, slot_tok, slot_row, depth, small, parts, weights=None):
        self.nc, self.c, self.a, self.xn, self.y, self.gain = c.nc, c, a, xn, y, gain
        self.depth, self.small, self.parts = depth, small, parts
        self.slot_tok, self.slot_row = slot_tok, slot_row
        s = lambda n, shape, dt=F32: sbuf(ctx, c.nc, f"{name}_{n}", shape, dt)
        d, e = depth, small
        self.wgu, self.wd, self.gu_in, self.d_in = weights or expert_weights(c, ctx, name, e, parts, c.sem)
        self.rows, self.rowsT = s("rows", [P, d, D]), s("rowsT", [P, e, KD, P])
        self.itok, self.irow = s("itok", [P, d], I32), s("irow", [P, d], I32)
        self.gated, self.hid, self.hidT = s("gated", [P, e, EH]), s("hid", [P, e, EH]), s("hidT", [P, e, 2, P])
        self.res = s("res", [P, d, D])
        self.ps_t, self.ps_h = psum(ctx, c.nc, f"{name}_pt", 2), psum(ctx, c.nc, f"{name}_ph", 2)
        self.ps_u, self.ps_y = psum(ctx, c.nc, f"{name}_pu", 1), psum(ctx, c.nc, f"{name}_py", 2)
        m = c.sem
        self.gathered = [m(f"{name}_gathered{b}") for b in range(d)]
        self.scattered = [m(f"{name}_scattered{b}") for b in range(d)]
        self.placed, self.gathers, self.scatters = [m(f"{name}_{x}") for x in ("placed", "gathers", "scatters")]
        self.indexed, self.rows_turned, self.rowsT_ready, self.up_done, self.gated_ready = [
            m(f"{name}_{x}") for x in ("indexed", "rows_turned", "rowsT_ready", "up_done", "gated_ready")]
        self.hid_ready, self.hid_turned, self.hidT_ready, self.down_done, self.res_ready = [
            m(f"{name}_{x}") for x in ("hid_ready", "hid_turned", "hidT_ready", "down_done", "res_ready")]

    def load_weights(self, sp, n, b, expert):
        load_expert_weights(
            sp, self.a, (self.wgu, self.wd, self.gu_in, self.d_in), b % self.small, self.parts, expert,
            (lambda: wait_for(sp, self.up_done, n - self.small + 1),
             lambda: wait_for(sp, self.down_done, n - self.small + 1)))

    def filled(self, b, use):
        return use * (self.depth // self.small) + b // self.small

    def gather(self, pool, n, b, column):
        nc, d = self.nc, self.depth
        source = self.slot_tok[:, bass.ds(column if isinstance(column, int) else pool.snap(column), 1)]
        wait_for(pool, self.rows_turned, n - d + 1)
        nc.gpsimd.tensor_copy(self.itok[:, b:b + 1], source).then_inc(self.indexed, 1)
        bound = pool.to_reg(T - 1)
        pool.wait_ge(self.indexed, n + 1)
        pool.sem_inc(self.gathers, 1)
        nc.gpsimd.indirect_dma_start(
            out=self.rows[:, b], out_offset=None, in_=self.xn[:],
            in_offset=bass.IndirectOffsetOnAxis(ap=self.itok[:, b:b + 1], axis=0),
            bounds_check=bound, oob_is_err=False).then_inc(self.gathered[b], 16)

    def scatter(self, pool, n, b, column, use):
        source = self.slot_row[:, bass.ds(column if isinstance(column, int) else pool.snap(column), 1)]
        wait_for(pool, self.scattered[b], 16 * use)
        self.nc.gpsimd.tensor_copy(self.irow[:, b:b + 1], source).then_inc(self.placed, 1)
        bound = pool.to_reg(2 * T - 1)
        pool.wait_ge(self.placed, n + 1)
        pool.wait_ge(self.res_ready, n + 1)
        pool.sem_inc(self.scatters, 1)
        self.nc.gpsimd.indirect_dma_start(
            out=self.y[:], out_offset=bass.IndirectOffsetOnAxis(ap=self.irow[:, b:b + 1], axis=0),
            in_=self.res[:, b], in_offset=None,
            bounds_check=bound, oob_is_err=False).then_inc(self.scattered[b], 16)

    def turn_rows(self, pe, n, b, use):
        pe.wait_ge(self.gathered[b], 16 * use + 16)
        wait_for(pe, self.rowsT_ready, n)
        for k in range(KD):
            ins = self.nc.tensor.transpose(self.ps_t[:, k // 4, (k % 4) * P:(k % 4 + 1) * P],
                                           self.rows[:, b, k * P:(k + 1) * P], self.c.ident[:])
        ins.then_inc(self.rows_turned, 1)

    def up(self, pe, n, b, use):
        pe.wait_ge(self.rowsT_ready, n + 1)
        w, each = b % self.small, 32 * self.parts
        pe.wait_ge(self.gu_in[w], each * self.filled(b, use) + each)
        wait_for(pe, self.hid_ready, n - self.small + 1)
        for k in range(KD):
            for h in range(self.parts):
                r = slice(h * P // self.parts, (h + 1) * P // self.parts)
                ins = self.nc.tensor.matmul(self.ps_h[r, w], self.rowsT[:, w, k, r],
                                            self.wgu[:, w * self.parts + h, k], start=(k == 0), stop=(k == KD - 1))
        ins.then_inc(self.up_done, 1)

    def turn_hidden(self, pe, n, b):
        pe.wait_ge(self.hid_ready, n + 1)
        wait_for(pe, self.hidT_ready, n)
        for k in range(EH // P):
            ins = self.nc.tensor.transpose(self.ps_u[:, 0, k * P:(k + 1) * P],
                                           self.hid[:, b % self.small, k * P:(k + 1) * P], self.c.ident[:])
        ins.then_inc(self.hid_turned, 1)

    def down(self, pe, n, b, use):
        pe.wait_ge(self.hidT_ready, n + 1)
        w, each = b % self.small, 16 * self.parts
        pe.wait_ge(self.d_in[w], each * self.filled(b, use) + each)
        wait_for(pe, self.res_ready, n)
        for half in range(D // CH):
            for k in range(EH // P):
                for h in range(self.parts):
                    r = slice(h * P // self.parts, (h + 1) * P // self.parts)
                    ins = self.nc.tensor.matmul(self.ps_y[r, half], self.hidT[:, w, k, r],
                                                self.wd[:, w * self.parts + h, k, half * CH:(half + 1) * CH],
                                                start=(k == 0), stop=(k == EH // P - 1))
        ins.then_inc(self.down_done, 1)

    def take_rowsT(self, dve, n, b):
        dve.wait_ge(self.rows_turned, n + 1)
        wait_for(dve, self.up_done, n - self.small + 1)
        self.nc.vector.tensor_tensor(
            self.rowsT[:, b % self.small], self.ps_t[:].rearrange("p b (k t) -> p (b k) t", t=P),
            self.gain[:].unsqueeze(2).to_broadcast([P, KD, P]), ALU.mult).then_inc(self.rowsT_ready, 1)

    def take_hidden(self, dve, n, b):
        dve.wait_ge(self.gated_ready, n + 1)
        wait_for(dve, self.hid_turned, n - self.small + 1)
        self.nc.vector.tensor_tensor(self.hid[:, b % self.small], self.ps_h[:, b % self.small, EH:],
                                     self.gated[:, b % self.small], ALU.mult).then_inc(self.hid_ready, 1)

    def take_hiddenT(self, dve, n, b):
        dve.wait_ge(self.hid_turned, n + 1)
        wait_for(dve, self.down_done, n - self.small + 1)
        self.nc.vector.tensor_copy(self.hidT[:, b % self.small].rearrange("p k t -> p (k t)"),
                                   self.ps_u[:, 0, :EH]).then_inc(self.hidT_ready, 1)

    def gate(self, act, n, b):
        act.wait_ge(self.up_done, n + 1)
        wait_for(act, self.hid_ready, n - self.small + 1)
        self.nc.scalar.activation(self.gated[:, b % self.small], self.ps_h[:, b % self.small, :EH],
                                  ACT.Silu).then_inc(self.gated_ready, 1)

    def take_result(self, act, n, b, use):
        act.wait_ge(self.down_done, n + 1)
        wait_for(act, self.scattered[b], 16 * use)
        self.nc.scalar.activation(self.res[:, b].rearrange("p (h n) -> p h n", n=CH), self.ps_y[:],
                                  ACT.Copy).then_inc(self.res_ready, 1)


BUFS = 4


def over_blocks(eng, body):
    for n in range(BUFS):
        body(n, n, 0)
    with eng.Fori(1, PAIRED // BUFS - 1) as i:
        for b in range(BUFS):
            body(i * BUFS + b, b, i)
    for n in range(PAIRED - BUFS, PAIRED):
        body(n, n % BUFS, n // BUFS)


def ahead(n, b, use, by):
    if isinstance(n, int) and n + by >= PAIRED:
        return None
    return n + by, (b + by) % BUFS, use + (b + by) // BUFS


def moe_first(c, a, x):
    nc = c.nc
    xn = nc.dram_tensor("ffn_rows", [T, D], F32).ap()
    y = nc.dram_tensor("expert_results", [2 * T, D], F32).ap()
    with ExitStack() as ctx:
        s = lambda n, shape, dt=F32: sbuf(ctx, nc, n, shape, dt)
        gain = s("ffn_gain", [P, KD])
        w1, w2 = s("moe_w1", [P, NT]), s("moe_w2", [P, NT])
        slot_tok, slot_row = s("slot_tok", [P, NBLK], I32), s("slot_row", [P, NBLK], I32)
        ov_expert, ov_count = s("ov_expert", [1, OVB], I32), s("ov_count", [1, 1], I32)
        weights = expert_weights(c, ctx, "moe", 2, 2, c.hold_sem)
        with ExitStack() as tmp:
            hT = sbuf(tmp, nc, "ffn_hT", [P, KD, T])
            load(c, [(gain[:], a["norm_ffn"][0].rearrange("(k p) -> p k", p=P))])
            norm_transpose(c, "ffn", x, hT, gain, NT, keep=xn)
            route(c, a, hT, w1[:], w2[:], slot_tok[:], slot_row[:], ov_expert[:], ov_count[:], weights)
        c.recycle(0)
        with ExitStack() as run:
            st = ExpertSteps(c, run, "moe", a, xn, y, gain, slot_tok, slot_row, BUFS, 2, 2, weights)
            clear_rows(c, st.rows)
            with nc.Block() as block:
                @block.sync
                def _(sp):
                    def body(n, b, use):
                        if not isinstance(n, int) or n >= 2:
                            st.load_weights(sp, n, b, n * 2)

                    over_blocks(sp, body)

                @block.gpsimd
                def _(pool):
                    for n in range(3):
                        st.gather(pool, n, n, n)

                    def body(n, b, use):
                        if nxt := ahead(n, b, use, 3):
                            st.gather(pool, nxt[0], nxt[1], nxt[0])
                        st.scatter(pool, n, b, n, use)

                    over_blocks(pool, body)
                    for b in range(BUFS):
                        pool.wait_ge(st.scattered[b], 16 * PAIRED // BUFS)

                @block.tensor
                def _(pe):
                    st.turn_rows(pe, 0, 0, 0)
                    st.up(pe, 0, 0, 0)
                    st.turn_rows(pe, 1, 1, 0)

                    def body(n, b, use):
                        if nxt := ahead(n, b, use, 2):
                            st.turn_rows(pe, *nxt)
                        if nxt := ahead(n, b, use, 1):
                            st.up(pe, *nxt)
                        st.turn_hidden(pe, n, b)
                        st.down(pe, n, b, use)

                    over_blocks(pe, body)

                @block.vector
                def _(dve):
                    st.take_rowsT(dve, 0, 0)
                    st.take_rowsT(dve, 1, 1)
                    st.take_hidden(dve, 0, 0)

                    def body(n, b, use):
                        if nxt := ahead(n, b, use, 2):
                            st.take_rowsT(dve, *nxt[:2])
                        if nxt := ahead(n, b, use, 1):
                            st.take_hidden(dve, *nxt[:2])
                        st.take_hiddenT(dve, n, b)

                    over_blocks(dve, body)

                @block.scalar
                def _(act):
                    st.gate(act, 0, 0)

                    def body(n, b, use):
                        if nxt := ahead(n, b, use, 1):
                            st.gate(act, *nxt[:2])
                        st.take_result(act, n, b, use)

                    over_blocks(act, body)
        c.recycle(0)
        with ExitStack() as run:
            st = ExpertSteps(c, run, "over", a, xn, y, gain, slot_tok, slot_row, 1, 1, 1)
            clear_rows(c, st.rows)
            blocks_out = c.sem("over_blocks_out")

            def each(eng, body):
                count = eng.value_load(ov_count[0:1, 0:1], min_val=0, max_val=OVB)
                with eng.Fori(0, OVB) as j:
                    with eng.If(j < count):
                        body(j)

            with nc.Block() as block:
                @block.sync
                def _(sp):
                    def body(j):
                        e = sp.value_load(ov_expert[0:1, bass.ds(j, 1)], min_val=0, max_val=E - 1)
                        st.load_weights(sp, j, 0, e)
                    each(sp, body)

                @block.gpsimd
                def _(pool):
                    def body(j):
                        st.gather(pool, j, 0, j + PAIRED)
                        st.scatter(pool, j, 0, j + PAIRED, j)
                        pool.wait_ge(st.scattered[0], 16 * j + 16)
                        pool.sem_inc(blocks_out, 1)
                    each(pool, body)

                @block.tensor
                def _(pe):
                    def body(j):
                        st.turn_rows(pe, j, 0, j)
                        st.up(pe, j, 0, j)
                        st.turn_hidden(pe, j, 0)
                        st.down(pe, j, 0, j)
                    each(pe, body)

                @block.vector
                def _(dve):
                    def body(j):
                        st.take_rowsT(dve, j, 0)
                        st.take_hidden(dve, j, 0)
                        st.take_hiddenT(dve, j, 0)
                    each(dve, body)

                @block.scalar
                def _(act):
                    def body(j):
                        st.gate(act, j, 0)
                        st.take_result(act, j, 0, j)
                    each(act, body)
        c.recycle(0)
        with ExitStack() as run:
            got = sbuf(run, nc, "moe_got", [P, 2, 2, D])
            arrived = [c.sem(f"moe_got{b}") for b in range(2)]
            added = c.sem("moe_added")
            src = y.rearrange("(m p k) d -> p m k d", p=P, k=2)
            with nc.Block() as block:
                @block.sync
                def _(sp):
                    for m in range(NT):
                        if m >= 2:
                            sp.wait_ge(added, 2 * (m - 1))
                        sp.dma_start(got[:, m % 2], src[:, m]).then_inc(arrived[m % 2], 16)

                @block.vector
                def _(dve):
                    for m in range(NT):
                        dve.wait_ge(arrived[m % 2], 16 * (m // 2 + 1))
                        for k, w in enumerate((w1, w2)):
                            nc.vector.scalar_tensor_tensor(x[:, m], got[:, m % 2, k], w[:, m:m + 1], x[:, m],
                                                           ALU.mult, ALU.add).then_inc(added, 1)
                            dve.wait_ge(added, 2 * m + k + 1)


def clear_rows(c, rows):
    nc = c.nc
    with nc.Block() as block:
        @block.vector
        def _(dve):
            nc.vector.memset(rows[:], 0.0)



S5_RAW = 3 * PAIRS + 2 * PAIRS * SC


def s5_raw(t):
    small = [t[:, i * PAIRS:(i + 1) * PAIRS] for i in range(3)]
    n = PAIRS * SC
    return small + [t[:, 3 * PAIRS + i * n:3 * PAIRS + (i + 1) * n].rearrange("p (q c) -> p q c", c=SC)
                    for i in range(2)]


def s5_relay(sp, a, relaid, done):
    lr, li, dt, br, bi = s5_raw(relaid)
    cs = relaid[:, S5_RAW:].rearrange("p (i t n) -> p i t n", i=2, t=4)
    n = 0
    for two in range(2):
        h = slice(two * SN, (two + 1) * SN)
        for dst, src in ((lr, a["lam_re_2"][0, two::2].rearrange("q n -> n q")),
                         (li, a["lam_im_2"][0, two::2].rearrange("q n -> n q")),
                         (dt, a["log_dt_2"][0, two::2].unsqueeze(0).to_broadcast([SN, PAIRS])),
                         (br, a["ssm_b_re_2"][0, two::2].rearrange("q n c -> n q c")),
                         (bi, a["ssm_b_im_2"][0, two::2].rearrange("q n c -> n q c"))):
            sp.dma_start(dst[h], src).then_inc(done, 16)
            n += 1
        for i, name in enumerate(("ssm_c_re_2", "ssm_c_im_2")):
            sp.dma_start(cs[:, i, :, h], a[name][0].rearrange("g c n -> (g c) n").rearrange(
                "(t p) n -> p t n", p=P)).then_inc(done, 16)
            n += 1
    return n


def real_part(eng, do, out, l, r, t):
    do(eng.tensor_tensor(out, l[0], r[0], ALU.mult))
    do(eng.tensor_tensor(t, l[1], r[1], ALU.mult))
    do(eng.tensor_tensor(out, out, t, ALU.subtract))


def imaginary_part(eng, do, out, l, r, t):
    do(eng.tensor_tensor(out, l[0], r[1], ALU.mult))
    do(eng.tensor_tensor(t, l[1], r[0], ALU.mult))
    do(eng.tensor_tensor(out, out, t, ALU.add))


def s5_parameters(c, a, relaid, tmp, kept, scratch, scratch2):
    nc = c.nc
    c.recycle()
    t = lambda n, shape, dt=F32: sbuf(tmp, nc, f"s5_{n}", shape, dt)
    Q = PAIRS
    cre, cim, rho, cos8, sin8, bnr, bni = kept
    raw = t("raw", [P, S5_RAW])
    lr, li, dt, br, bi = s5_raw(raw)
    craw = scratch[:, 4096 - 2 * 4 * P:4096].rearrange("p (i t n) -> p i t n", i=2, t=4)
    load(c, [(raw[:], relaid[:, 0:S5_RAW]), (craw.rearrange("p i t n -> p (i t n)"), relaid[:, S5_RAW:])])
    cn = t("cn", [P, 2, Q, SC])
    items = [[craw[:, i, j] for j in range(4)] for i in range(2)]

    def split(n, ps, copy):
        v = ps.rearrange("p (q two c) -> p q two c", two=2, c=SC)
        copy(cn[0:SN, n], v[0:SN, :, 0])
        return copy(cn[SN:P, n], v[SN:P, :, 1])

    turn(c, "s5_cturn", items, split)
    ang, size, root, tq = t("ang", [P, Q]), t("size", [P, Q]), t("root", [P, Q]), t("tq", [P, Q])
    sn, cs = t("sin", [P, Q]), t("cos", [P, Q])
    with nc.Block() as block:
        @block.scalar
        def _(act):
            nc.scalar.activation(dt, dt, ACT.Exp)
    with nc.Block() as block:
        @block.vector
        def _(dve):
            do = c.chain("vector", dve)
            do(nc.vector.tensor_tensor(size[:], lr, dt, ALU.mult))
            do(nc.vector.tensor_tensor(ang[:], li, dt, ALU.mult))
            reduce_angle(nc, do, ang[:], tq[:])
            do(nc.vector.tensor_scalar(tq[:], ang[:], -1.0, None, ALU.mult))
            do(nc.vector.tensor_tensor(tq[:], tq[:], ang[:], ALU.min))
            do(nc.vector.tensor_scalar(tq[:], tq[:], math.pi / 2, None, ALU.add))
    with nc.Block() as block:
        @block.scalar
        def _(act):
            nc.scalar.activation(rho[:], size[:], ACT.Exp, scale=float(SJ))
            nc.scalar.activation(root[:], size[:], ACT.Exp)
            nc.scalar.activation(sn[:], ang[:], ACT.Sin)
            nc.scalar.activation(cs[:], tq[:], ACT.Sin)
    pr, pi = t("pr", [P, SJ + 1, Q]), t("pi", [P, SJ + 1, Q])
    er, den, qr, qi = [t(n, [P, Q]) for n in ("er", "den", "qr", "qi")]
    bbr, bbi = t("bbr", [P, Q, SC]), t("bbi", [P, Q, SC])
    tmp4 = scratch[:, 0:Q * (SJ + 1) * SC]
    powers_ready = c.sem("s5_powers_ready")
    c_wide = tuple(cn[:, i].unsqueeze(2).to_broadcast([P, Q, SJ + 1, SC]) for i in range(2))

    def power(js, n):
        return tuple(p[:, js].rearrange("p j q -> p q j").unsqueeze(3).to_broadcast([P, Q, n, SC]) for p in (pr, pi))

    with nc.Block() as block:
        @block.vector
        def _(dve):
            do = c.chain("vector", dve)
            tt = lambda o, l, r, op: do(nc.vector.tensor_tensor(o, l, r, op))

            def product(o_re, o_im, l, r, t):
                real_part(nc.vector, do, o_re, l, r, t)
                imaginary_part(nc.vector, do, o_im, l, r, t)

            do(nc.vector.memset(pr[:, 0], 1.0))
            do(nc.vector.memset(pi[:, 0], 0.0))
            tt(pr[:, 1], root[:], cs[:], ALU.mult)
            tt(pi[:, 1], root[:], sn[:], ALU.mult)
            done = 1
            while done < SJ:
                lhs = (pr[:, 1:done + 1], pi[:, 1:done + 1])
                rhs = tuple(p[:, done:done + 1].to_broadcast([P, done, Q]) for p in (pr, pi))
                t3 = tmp4[:, :done * Q].rearrange("p (j q) -> p j q", q=Q)
                product(pr[:, done + 1:2 * done + 1], pi[:, done + 1:2 * done + 1], lhs, rhs, t3)
                done *= 2
            nc.vector.tensor_copy(tq[:], tq[:]).then_inc(powers_ready, 1)
            cur = (cs[:], sn[:])
            for n, o in enumerate(((qr[:], qi[:]), (er[:], den[:]), (cos8[:], sin8[:]))):
                product(o[0], o[1], cur, cur, tq[:])
                cur = o
            tt(den[:], lr, lr, ALU.mult)
            tt(tq[:], li, li, ALU.mult)
            tt(den[:], den[:], tq[:], ALU.add)
            do(nc.vector.reciprocal(den[:], den[:]))
            do(nc.vector.tensor_scalar(er[:], pr[:, 1], -1.0, None, ALU.add))
            tt(qr[:], er[:], lr, ALU.mult)
            tt(tq[:], pi[:, 1], li, ALU.mult)
            tt(qr[:], qr[:], tq[:], ALU.add)
            tt(qr[:], qr[:], den[:], ALU.mult)
            tt(qi[:], pi[:, 1], lr, ALU.mult)
            tt(tq[:], er[:], li, ALU.mult)
            tt(qi[:], qi[:], tq[:], ALU.subtract)
            tt(qi[:], qi[:], den[:], ALU.mult)
            wide = lambda v: v.unsqueeze(2).to_broadcast([P, Q, SC])
            product(bbr[:], bbi[:], (wide(qr[:]), wide(qi[:])), (br, bi),
                    tmp4[:, :Q * SC].rearrange("p (q c) -> p q c", c=SC))
            product(bnr[:], bni[:], power(slice(SJ - 1, None, -1), SJ),
                    tuple(b[:].unsqueeze(2).to_broadcast([P, Q, SJ, SC]) for b in (bbr, bbi)),
                    tmp4[:, :Q * SJ * SC].rearrange("p (q j c) -> p q j c", q=Q, c=SC))
            imaginary_part(nc.vector, do, cim[:], power(slice(0, SJ + 1), SJ + 1), c_wide,
                           tmp4.rearrange("p (q j c) -> p q j c", q=Q, c=SC))
            do(nc.vector.tensor_scalar(cim[:], cim[:], -1.0, None, ALU.mult))

        @block.gpsimd
        def _(pool):
            do = c.chain("gpsimd", pool)
            pool.wait_ge(powers_ready, 1)
            t = scratch2[:, 0:Q * (SJ + 1) * SC].rearrange("p (q j c) -> p q j c", q=Q, c=SC)
            real_part(nc.gpsimd, do, cre[:], power(slice(0, SJ + 1), SJ + 1), c_wide, t)
    return bbr, bbi


def s5(c, a, relaid, u, y):
    nc = c.nc
    Q = PAIRS
    with ExitStack() as keep:
        k = lambda n, shape, dt=F32: sbuf(keep, nc, f"s5_{n}", shape, dt)
        cre, cim = k("cre", [P, Q, SJ + 1, SC]), k("cim", [P, Q, SJ + 1, SC])
        rho, cos8, sin8 = k("rho", [P, Q]), k("cos8", [P, Q]), k("sin8", [P, Q])
        bnr, bni = k("bnr", [P, Q, SJ, SC]), k("bni", [P, Q, SJ, SC])
        wre, wim = [b[:].rearrange("p q j c -> p q (j c)") for b in (bnr, bni)]
        with ExitStack() as mid:
            bTr, bTi = [sbuf(mid, nc, f"s5_bT{n}", [P, Q, P]) for n in "ri"]
            toe = sbuf(mid, nc, "s5_toe", [P, SG, SJ * SC])
            dskip = sbuf(mid, nc, "s5_dskip", [P, SG, SC])
            tmp = ExitStack()
            bbr, bbi = s5_parameters(c, a, relaid, tmp, (cre, cim, rho, cos8, sin8, bnr, bni),
                                     toe[:].rearrange("p g n -> p (g n)"), y.rearrange("p j g c -> p (j g c)"))
            items = [[src[:, 4 * i + j].rearrange("p j c -> p (j c)") for j in range(4)]
                     for src in (bnr, bni) for i in range(4)]
            turn(c, "s5_bturn", items, lambda n, ps, copy: copy(
                (bTr, bTi)[n // 4][:, 4 * (n % 4):4 * (n % 4) + 4], ps.rearrange("p (q s) -> p q s", s=P)))
            resp = y[0:SC].rearrange("p j g c -> p (j g c)").rearrange("p (g n) -> p g n", g=SG)
            with ExitStack() as pctx:
                ps = psum(pctx, nc, "s5_resp_ps", 8)
                with nc.Block() as block:
                    @block.tensor
                    def _(pe):
                        for g in range(SG):
                            q, h = g // 2, slice((g % 2) * SN, (g % 2 + 1) * SN)
                            o = ps[0:SC, 4 * (g % 2) + q // 4, (q % 4) * P:(q % 4 + 1) * P]
                            rows = lambda t: t[h, q, 0:SJ].rearrange("p j c -> p (j c)")
                            nc.tensor.matmul(o, bbr[h, q], rows(cre), start=True, stop=False)
                            nc.tensor.matmul(o, bbi[h, q], rows(cim), start=False, stop=True)

                    @block.vector
                    def _(dve):
                        nc.vector.memset(toe[:], 0.0)
                with nc.Block() as block:
                    @block.vector
                    def _(dve):
                        for b in range(8):
                            first = 8 * (b % 4) + b // 4
                            nc.vector.tensor_copy(resp[:, first:first + 7:2],
                                                  ps[0:SC, b].rearrange("p (g n) -> p g n", g=4))
            load(c, [(toe[j * SC:(j + 1) * SC, :, j * SC:], resp[:, :, 0:(SJ - j) * SC]) for j in range(SJ)]
                 + [(dskip[:], a["ssm_d_2"][0].rearrange("(g c) -> g c", c=SC).unsqueeze(0).to_broadcast(
                     [P, SG, SC]))])
            tmp.close()
            uT = y.rearrange("p j g c -> p (j g c)").rearrange("p (g m) -> p g m", g=SG)
            items = [[u[:, 4 * i + j].rearrange("p j c -> p (j c)") for j in range(4)] for i in range(SG // 4)]
            turn(c, "s5_uturn", items, lambda n, ps, copy: copy(
                uT[:, 4 * n:4 * n + 4], ps.rearrange("p (g m) -> p g m", m=SM)))
            with ExitStack() as pctx:
                ps = psum(pctx, nc, "s5_w_ps", 8)
                with nc.Block() as block:
                    @block.tensor
                    def _(pe):
                        for g in range(SG):
                            q, h = g // 2, slice((g % 2) * SN, (g % 2 + 1) * SN)
                            for i, bT in enumerate((bTr, bTi)):
                                nc.tensor.matmul(ps[h, 4 * i + q // 4, (q % 4) * SM:(q % 4 + 1) * SM],
                                                 bT[:, q, h], uT[:, g], start=True, stop=True)
                with nc.Block() as block:
                    @block.vector
                    def _(dve):
                        nc.vector.tensor_copy(wre.rearrange("p (b q) m -> p b (q m)", b=4), ps[:, 0:4])
                        nc.vector.tensor_tensor(
                            u, u, dskip[:].unsqueeze(2).to_broadcast([P, SG, SJ, SC]), ALU.mult)

                    @block.scalar
                    def _(act):
                        nc.scalar.activation(wim.rearrange("p (b q) m -> p b (q m)", b=4), ps[:, 4:8], ACT.Copy)
                with nc.Block() as block:
                    @block.tensor
                    def _(pe):
                        for g in range(SG):
                            nc.tensor.matmul(ps[:, g // 4, (g % 4) * P:(g % 4 + 1) * P], uT[:, g], toe[:, g],
                                             start=True, stop=True)
                with nc.Block() as block:
                    @block.vector
                    def _(dve):
                        flat = u.rearrange("p (b g) j c -> p b (g j c)", b=8)
                        nc.vector.tensor_tensor(flat, ps[:], flat, ALU.add)
        s = lambda n, shape: sbuf(keep, nc, f"s5_{n}", shape)
        ct, st = s("ct", [P, Q, SM]), s("st", [P, Q, SM])
        both = y.rearrange("p j g c -> p (j g c)").rearrange("p (i q m) -> p i q m", i=2, q=Q)
        tr, ti = both[:, 0], both[:, 1]
        sre, sim = s("sre", [P, Q, SM + 1]), s("sim", [P, Q, SM + 1])
        with nc.Block() as block:
            @block.vector
            def _(dve):
                do = c.chain("vector", dve)
                tt = lambda o, l, r, op: do(nc.vector.tensor_tensor(o, l, r, op))
                do(nc.vector.memset(ct[:, :, 0:1], 1.0))
                do(nc.vector.memset(st[:, :, 0:1], 0.0))
                n = 1
                while n < SM:
                    cw, sw = [v[:].unsqueeze(2).to_broadcast([P, Q, n]) for v in (cos8, sin8)]
                    tt(tr[:, :, :n], ct[:, :, :n], cw, ALU.mult)
                    tt(ti[:, :, :n], st[:, :, :n], sw, ALU.mult)
                    tt(ct[:, :, n:2 * n], tr[:, :, :n], ti[:, :, :n], ALU.subtract)
                    tt(tr[:, :, :n], ct[:, :, :n], sw, ALU.mult)
                    tt(ti[:, :, :n], st[:, :, :n], cw, ALU.mult)
                    tt(st[:, :, n:2 * n], tr[:, :, :n], ti[:, :, :n], ALU.add)
                    tt(tr[:, :, 0], cos8[:], cos8[:], ALU.mult)
                    tt(ti[:, :, 0], sin8[:], sin8[:], ALU.mult)
                    tt(sin8[:], cos8[:], sin8[:], ALU.mult)
                    do(nc.vector.tensor_scalar(sin8[:], sin8[:], 2.0, None, ALU.mult))
                    tt(cos8[:], tr[:, :, 0], ti[:, :, 0], ALU.subtract)
                    n *= 2
                tt(tr, wre, ct[:], ALU.mult)
                tt(ti, wim, st[:], ALU.mult)
                tt(tr, tr, ti, ALU.add)
                tt(ti, wim, ct[:], ALU.mult)
                tt(wre, wre, st[:], ALU.mult)
                tt(ti, ti, wre, ALU.subtract)
                do(nc.vector.memset(sre[:, :, 0:SM], 1.0))
                tt(wim, sre[:, :, 0:SM], rho[:].unsqueeze(2).to_broadcast([P, Q, SM]), ALU.mult)
                do(nc.vector.memset(wim[:, :, 0:1], 0.0))
                flat = lambda t: t.rearrange("p q m -> p (q m)")
                do(nc.vector.tensor_tensor_scan(flat(wre), flat(wim), flat(tr), 0.0, ALU.mult, ALU.add))
                do(nc.vector.tensor_tensor_scan(flat(tr), flat(wim), flat(ti), 0.0, ALU.mult, ALU.add))
                do(nc.vector.memset(sre[:, :, 0:1], 0.0))
                do(nc.vector.memset(sim[:, :, 0:1], 0.0))
                tt(ti, wre, ct[:], ALU.mult)
                tt(wim, tr, st[:], ALU.mult)
                tt(sre[:, :, 1:], ti, wim, ALU.subtract)
                tt(ti, wre, st[:], ALU.mult)
                tt(wim, tr, ct[:], ALU.mult)
                tt(sim[:, :, 1:], ti, wim, ALU.add)
        with ExitStack() as pctx:
            ps = psum(pctx, nc, "s5_y_ps", 8)
            with nc.Block() as block:
                @block.tensor
                def _(pe):
                    for g in range(SG):
                        q, h = g // 2, slice((g % 2) * SN, (g % 2 + 1) * SN)
                        o = ps[:, 4 * (g % 2) + q // 4, (q % 4) * P:(q % 4 + 1) * P]
                        rows = lambda t: t[h, q, 1:SJ + 1].rearrange("p j c -> p (j c)")
                        nc.tensor.matmul(o, sre[h, q, 0:SM], rows(cre), start=True, stop=False)
                        nc.tensor.matmul(o, sim[h, q, 0:SM], rows(cim), start=False, stop=True)
            with nc.Block() as block:
                @block.vector
                def _(dve):
                    for b in range(8):
                        first = 8 * (b % 4) + b // 4
                        gs = slice(first, first + 7, 2)
                        nc.vector.tensor_tensor(
                            y[:, :, gs].rearrange("p j g c -> p g j c"),
                            ps[:, b].rearrange("p (g j c) -> p g j c", g=4, j=SJ), u[:, gs], ALU.add)


def mix_second(c, a, x):
    nc = c.nc
    SW = SG * SC
    w_in = a["w_in_2"][0]
    part = lambda i: w_in[:, SW + i * D:SW + (i + 1) * D]
    with ExitStack() as ctx:
        s = lambda n, shape, dt=F32: sbuf(ctx, nc, n, shape, dt)
        t1, t2 = s("m2_t1", [P, KD, T]), s("m2_t2", [P, KD, T])
        u = s("m2_u", [P, SG, SJ, SC])
        residual = nc.dram_tensor("residual", [P, NT * D], F32).ap()
        gate = x[:].rearrange("p m d -> p (m d)").rearrange("p (k t) -> p k t", k=KD)
        c.recycle(0)
        moved, relay = c.hold_sem("residual_moved"), c.hold_sem("s5_parameters_laid_out")
        relaid = nc.dram_tensor("s5_laid_out", [P, S5_RAW + 8 * P], F32).ap()
        with ExitStack() as early:
            s = lambda n, shape, dt=F32: sbuf(early, nc, n, shape, dt)
            bias = s("m2_bias", [P, 5, KD])
            cw, cb = s("m2_cw", [P, 3, KD]), s("m2_cb", [P, KD])
            ubias = s("m2_ubias", [P, SG, SC])
            pair = (s("m2_high", [P, KD, T]), s("m2_low", [P, KD, T]))
            v = nc.vector

            def channels(i, j, apply, engine, then=None):
                return Job(columns(part(i), j), False, pair, lambda b, ps: apply(
                    4 * j + b // 2, slice((b % 2) * CH, (b % 2 + 1) * CH), ps), engine, then=then)

            add_in = lambda i, dst: lambda ch, t, ps: v.tensor_scalar(
                dst[:, ch, t], ps, bias[:, i, ch:ch + 1], None, ALU.add)
            times_in = lambda i, dst: lambda ch, t, ps: v.scalar_tensor_tensor(
                dst[:, ch, t], ps, bias[:, i, ch:ch + 1], dst[:, ch, t], ALU.add, ALU.mult)
            gate_in = lambda i, dst: lambda ch, t, ps: nc.scalar.activation(
                dst[:, ch, t], ps, ACT.Sigmoid, bias=bias[:, i, ch:ch + 1])

            def convolve():
                do = c.chain("vector", nc.vector)
                for k in range(KD):
                    do(v.tensor_scalar(t2[:, k], t1[:, k], cw[:, 2, k:k + 1], cb[:, k:k + 1], ALU.mult, ALU.add))
                    for lag in (1, 2):
                        do(v.scalar_tensor_tensor(t2[:, k, lag:], t1[:, k, :T - lag], cw[:, 2 - lag, k:k + 1],
                                                  t2[:, k, lag:], ALU.mult, ALU.add))

            jobs = [channels(1, 0, add_in(1, t1), "vector"), channels(1, 1, add_in(1, t1), "vector"),
                    channels(2, 0, times_in(2, t1), "vector"),
                    channels(2, 1, times_in(2, t1), "vector", convolve),
                    Job(columns(w_in[:, 0:SW], 0), True, pair, lambda b, ps: v.tensor_tensor(
                        u[:, :, b], ps.rearrange("p (g c) -> p g c", c=SC), ubias[:], ALU.add),
                        "vector", tokens=lambda b: slice(b, T, SJ)),
                    channels(0, 0, times_in(0, t2), "vector"), channels(0, 1, times_in(0, t2), "vector"),
                    channels(4, 0, gate_in(4, t1), "scalar"), channels(4, 1, gate_in(4, t1), "scalar"),
                    channels(3, 0, gate_in(3, gate), "scalar"), channels(3, 1, gate_in(3, gate), "scalar")]
            relays = []
            with nc.Block() as block:
                @block.sync
                def _(sp):
                    sp.dma_start(residual, x[:].rearrange("p m d -> p (m d)")).then_inc(moved, 16)
            stream = Stream(c, early, "m2_w")
            stream.start(jobs)
            room = t1[:].rearrange("p k t -> p (k t)")
            gain = room[:, 3 * D:4 * D]
            load(c, [(gain, a["norm_mix_g_2"].to_broadcast([P, D])),
                     (cb[:], a["conv_b_2"][0].rearrange("(k p) -> p k", p=P)),
                     (ubias[:].rearrange("p g c -> p (g c)"),
                      a["b_in_2"][0, 0:SW].unsqueeze(0).to_broadcast([P, SW]))]
                 + [(bias[:, i], a["b_in_2"][0, SW + i * D:SW + (i + 1) * D].rearrange("(k p) -> p k", p=P))
                    for i in range(5)]
                 + [(cw[:, i], a["conv_w_2"][0, i].rearrange("(k p) -> p k", p=P)) for i in range(3)])
            with nc.Block() as block:
                @block.sync
                def _(sp):
                    with nc.allow_non_contiguous_dma("small parameters"):
                        relays.append(s5_relay(sp, a, relaid, relay))
            norm_split(c, "m2_norm", x, pair, gain, NT, room[:, :3 * D])
            with nc.Block() as block:
                @block.sync
                def _(sp):
                    sp.wait_ge(moved, 16)
                    sp.wait_ge(relay, 16 * relays[0])
            project(c, "m2_in", stream, jobs)

            def times_gate(j):
                def evacuate(b, ps):
                    at = (slice(None), 4 * j + b // 2, slice((b % 2) * CH, (b % 2 + 1) * CH))
                    return v.tensor_tensor(t1[at], ps, t1[at], ALU.mult)
                return evacuate

            jobs = [Job(columns(a["w_conv_out_2"][0], j), False, pair, times_gate(j), "vector") for j in range(2)]
            project(c, "m2_co", stream, jobs, source=t2)
            with nc.Block() as block:
                @block.scalar
                def _(act):
                    nc.scalar.activation(t2[:], gate, ACT.Copy)
        with ExitStack() as late:
            y = sbuf(late, nc, "m2_y", [P, SJ, SG, SC])
            s5(c, a, relaid, u[:], y[:])
            z = u[:].rearrange("p g j c -> p (g j c)")
            with nc.Block() as block:
                @block.sync
                def _(sp):
                    sp.dma_start(x[:].rearrange("p m d -> p (m d)"), residual).then_inc(moved, 16)

                @block.scalar
                def _(act):
                    nc.scalar.activation(z, y[:].rearrange("p j g c -> p (j g c)"), ACT.Gelu_apprx_tanh)
        with ExitStack() as late:
            nk = SW // P
            z = z.rearrange("p (j n) -> p j n", j=SJ)
            stream = Stream(c, late, "m2_glu_w")
            pair = high, low = [sbuf(late, nc, f"m2_z{n}", [P, nk, T]) for n in ("high", "low")]
            glu = sbuf(late, nc, "m2_glu", [P, KD, T])
            half = lambda b: slice((b % 2) * CH, (b % 2 + 1) * CH)
            do = c.chain("vector", nc.vector)

            def gate_glu(j):
                return lambda b, ps: nc.scalar.activation(glu[:, 4 * j + b // 2, half(b)], ps, ACT.Sigmoid)

            def mix_in(j):
                def evacuate(b, ps):
                    at = (slice(None), 4 * j + b // 2, half(b))
                    do(nc.vector.tensor_tensor(glu[at], ps, glu[at], ALU.mult))
                    do(nc.vector.tensor_tensor(glu[at], glu[at], t2[at], ALU.mult))
                    return nc.vector.tensor_tensor(t1[at], t1[at], glu[at], ALU.add)
                return evacuate

            jobs = [Job(columns(a["w_glu_b_2"][0], j), False, pair, gate_glu(j), "scalar") for j in range(2)]
            jobs += [Job(columns(a["w_glu_a_2"][0], j), False, pair, mix_in(j), "vector") for j in range(2)]
            stream.start(jobs)
            items = [[z[:, j, k * P:(k + 1) * P] for k in range(nk)] for j in range(SJ)]
            turn_split(c, "m2_zturn", items, lambda n: (high[:, :, n::SJ], low[:, :, n::SJ]))
            project(c, "m2_glu", stream, jobs)
        with ExitStack() as w_:
            with nc.Block() as block:
                @block.sync
                def _(sp):
                    sp.wait_ge(moved, 32)
            pair = [sbuf(w_, nc, f"m2_out_{n}", [P, KD, T]) for n in ("high", "low")]
            project(c, "m2_out", Stream(c, w_, "m2_out_w"), add_jobs(c, pair, a["w_out_2"][0], x), source=t1)


def mlp_second(c, a, x):
    nc = c.nc
    with ExitStack() as ctx:
        s = lambda n, shape, dt=F32: sbuf(ctx, nc, n, shape, dt)
        normed = (s("mlp_high", [P, KD, T]), s("mlp_low", [P, KD, T]))
        per = CH // P
        hidden = [[s(f"mlp_hidden_{n}{b}", [P, per, T]) for n in ("high", "low")] for b in range(2)]
        squares = s("mlp_squares", [P, 8, CH])
        stream = Stream(c, ctx, "mlp_w")
        do = c.chain("scalar", nc.scalar)
        do_v = c.chain("vector", nc.vector)

        def up(j):
            def evacuate(b, ps):
                do(nc.scalar.activation(squares[:, b], ps, ACT.Relu))
                return nc.scalar.activation(squares[:, b], squares[:, b], ACT.Square)

            def finish(b):
                high, low = [t[:, b // 2, (b % 2) * CH:(b % 2 + 1) * CH] for t in hidden[j % 2]]
                do_v(nc.vector.tensor_copy(high.bitcast(F32R), squares[:, b]))
                return nc.vector.tensor_tensor(low.bitcast(F32R), squares[:, b], high, ALU.subtract)

            return Job(columns(a["w_ff1_2"][0], j), False, normed, evacuate, "scalar", finish=finish)

        def down(j):
            jobs = add_jobs(c, hidden[j % 2], a["w_ff2_2"][0, j * CH:(j + 1) * CH], x)
            jobs[0].after = 8 * (j + 1)
            return jobs

        n = DFF // CH
        jobs = [up(0)]
        for j in range(n):
            jobs += ([up(j + 1)] if j + 1 < n else []) + down(j)
        stream.start(jobs)
        with ExitStack() as g_:
            gain = sbuf(g_, nc, "mlp_gain", [P, D])
            load(c, [(gain[:], a["norm_mlp_g_2"].to_broadcast([P, D]))])
            norm_split(c, "mlp_norm", x, normed, gain[:], NT, squares[:].rearrange("p b n -> p (b n)"))
        project(c, "mlp", stream, jobs)


def final_norm(c, a, x):
    nc = c.nc
    with ExitStack() as ctx:
        s = lambda n, shape, dt=F32: sbuf(ctx, nc, n, shape, dt)
        gain, junk, ssq = s("fin_gain", [P, 1, D]), s("fin_junk", [P, D]), s("fin_ssq", [P, NT])
        load(c, [(gain[:, 0], a["norm_final_g_2"].unsqueeze(0).to_broadcast([P, D]))])
        wide_norm(c, "fin", x[:].unsqueeze(2), junk[:], ssq[:], D, gain[:, 0])


INS = ['x', 'mem', 'positions', 'norm_mix', 'w_in', 'mla_q_a_norm', 'mla_w_q_up', 'mla_kv_a_norm', 'mla_w_kv_up',
       'mla_q_norm', 'mla_k_norm', 'hg_lb_logits', 'hg_o_norm', 'w_out', 'norm_cross', 'norm_mem', 'x_w_q',
       'x_w_kv', 'x_q_norm', 'x_k_norm', 'x_w_o', 'norm_ffn', 'moe_w_group', 'moe_b_group', 'moe_w_expert',
       'moe_b_expert', 'moe_w_gate', 'moe_w_up', 'moe_w_down', 'norm_mix_g_2', 'w_in_2', 'b_in_2', 'lam_re_2',
       'lam_im_2', 'log_dt_2', 'ssm_b_re_2', 'ssm_b_im_2', 'ssm_c_re_2', 'ssm_c_im_2', 'ssm_d_2', 'w_glu_a_2',
       'w_glu_b_2', 'conv_w_2', 'conv_b_2', 'w_conv_out_2', 'w_out_2', 'norm_mlp_g_2', 'w_ff1_2', 'w_ff2_2',
       'norm_final_g_2']


def program(nc, a, out, stages=("mix", "cross", "moe", "mix2", "mlp", "final")):
    with ExitStack() as ctx:
        c = Core(nc, ctx)
        done = ctx.enter_context(nc.semaphore("result_stored"))
        x = sbuf(ctx, nc, "x", [P, NT, D])
        make_constants(c)
        load(c, [(x[:], a["x"][0].rearrange("(m p) d -> p m d", p=P))])
        for st in stages:
            STAGES[st](c, a, x)
        with nc.Block() as block:
            @block.sync
            def _(sp):
                sp.dma_start(out[0].rearrange("(m p) d -> p m d", p=P), x[:]).then_inc(done, 16)
                sp.wait_ge(done, 16)


STAGES = {"mix": mix_first, "cross": cross_first, "moe": moe_first, "mix2": mix_second,
          "mlp": mlp_second, "final": final_norm}


def kernel(**inputs):
    import numpy as _np
    import concourse.bacc as _bacc
    from concourse import mybir as _mybir
    from concourse.bass_utils import run_bass_kernel_spmd as _run

    nc = _bacc.Bacc("TRN2", target_bir_lowering=False, num_devices=1)
    arrays, a = {}, {}
    for name in INS:
        v = _np.ascontiguousarray(inputs[name])
        arrays[f"in_{name}_dram"] = v
        a[name] = nc.dram_tensor(f"in_{name}_dram", v.shape, _mybir.dt.from_np(v.dtype), kind="ExternalInput").ap()
    out = nc.dram_tensor("out_0_dram", (1, T, D), F32, kind="ExternalOutput").ap()
    program(nc, a, out)
    r = _run(nc, [arrays], core_ids=[0])
    return r.results[0]["out_0_dram"]
```
